# Optimizing a Trainium2 kernel written in Bass

```python
import math
import jax, jax.numpy as jnp
from jax import lax
import numpy as np

D_MODEL = 1024
BATCH = 1
SEQ = 1024
DEPTH = 1

N_META = 16
D_MIX = D_MODEL
HEAD_DIM = 64
RWKV_WIDTH = D_MIX // 2
SB_WIDTH = D_MIX - RWKV_WIDTH
RWKV_HEADS = RWKV_WIDTH // HEAD_DIM
SB_HEADS = SB_WIDTH // HEAD_DIM
DECAY_RANK = 64
A_RANK = 64
GATE_RANK = 128
D_FF = 4 * D_MODEL
SB_BLOCK = 128
RMS_EPS = 1e-6
GN_EPS = 1e-5 * HEAD_DIM
RWKV_SPLITS = [RWKV_WIDTH, 2 * RWKV_WIDTH, 3 * RWKV_WIDTH,
               3 * RWKV_WIDTH + DECAY_RANK, 3 * RWKV_WIDTH + DECAY_RANK + A_RANK]
RWKV_COLS = 3 * RWKV_WIDTH + DECAY_RANK + A_RANK + GATE_RANK
SB_COLS = 3 * SB_WIDTH
IN_COLS = RWKV_COLS + SB_COLS

kernel_name = "hymba_rwkv7_stickbreak_hybrid"

def rmsnorm(x, gain):
    x32 = x.astype(jnp.float32)
    y = x32 * lax.rsqrt(jnp.mean(jnp.square(x32), axis=-1, keepdims=True) + RMS_EPS) * gain.astype(jnp.float32)
    return y.astype(x.dtype)

def rwkv7_group(p, mu, w_decay_up, decay_bias, w_a_up, a_bias, w_g_up, k_k, k_a, r_k, lnx_gain, lnx_bias):
    B, T, _ = p.shape
    H, N = RWKV_HEADS, HEAD_DIM
    p = p.astype(jnp.float32)
    prev = jnp.pad(p[:, :-1], ((0, 0), (1, 0), (0, 0)))
    p = p + (prev - p) * mu.astype(jnp.float32)
    r, k, v, dw, da, dg = jnp.split(p, RWKV_SPLITS, axis=-1)
    w_log = -jax.nn.softplus(-(decay_bias + jnp.tanh(dw) @ w_decay_up)) - 0.5
    decay = jnp.exp(-jnp.exp(w_log))
    a = jax.nn.sigmoid(a_bias + da @ w_a_up)
    g = jax.nn.sigmoid(dg) @ w_g_up
    heads = lambda t: t.reshape(B, T, H, N)
    kk = heads(k * k_k)
    kk = kk * lax.rsqrt(jnp.sum(jnp.square(kk), axis=-1, keepdims=True) + 1e-12)
    k = k * (1.0 + (a - 1.0) * k_a)
    rh, kh, vh, wh, ah = heads(r), heads(k), heads(v), heads(decay), heads(a)

    def step(S, inp):
        r_t, w_t, k_t, v_t, kk_t, a_t = inp
        sa = jnp.einsum('bhvk,bhk->bhv', S, -kk_t)
        S = (S * w_t[:, :, None, :] + sa[..., None] * (kk_t * a_t)[:, :, None, :]
             + v_t[..., None] * k_t[:, :, None, :])
        return S, jnp.einsum('bhvk,bhk->bhv', S, r_t)

    xs = tuple(jnp.moveaxis(t, 1, 0) for t in (rh, wh, kh, vh, kk, ah))
    S0 = jnp.zeros((B, H, N, N), jnp.float32)
    _, y = lax.scan(step, S0, xs)
    y = jnp.moveaxis(y, 0, 1)
    mean = jnp.mean(y, axis=-1, keepdims=True)
    var = jnp.mean(jnp.square(y - mean), axis=-1, keepdims=True)
    y = (y - mean) * lax.rsqrt(var + GN_EPS) * lnx_gain.reshape(H, N) + lnx_bias.reshape(H, N)
    y = y + jnp.sum(rh * kh * r_k, axis=-1, keepdims=True) * vh
    return y.reshape(B, T, H * N) * g

def stick_breaking_group(q, k, v, out_gain):
    B, T, _ = q.shape
    H, N = SB_HEADS, HEAD_DIM
    to_heads = lambda t: t.astype(jnp.float32).reshape(B, T, H, N).transpose(0, 2, 1, 3)
    qh, kh, vh = to_heads(q), to_heads(k), to_heads(v)
    scale = 1.0 / math.sqrt(N)
    bounds = [(0, N_META)] + [(s, min(s + SB_BLOCK, T)) for s in range(N_META, T, SB_BLOCK)]
    outs = []
    for q0, q1 in bounds:
        qb, kb, vb = qh[:, :, q0:q1], kh[:, :, :q1], vh[:, :, :q1]
        z = jnp.einsum('bhqd,bhkd->bhqk', qb, kb) * scale
        t_idx = q0 + jnp.arange(q1 - q0)
        s_idx = jnp.arange(q1)
        mask = s_idx[None, :] < t_idx[:, None]
        log_beta = jax.nn.log_sigmoid(z)
        log_1m = jnp.where(mask, log_beta - z, 0.0)
        log_a = log_beta + lax.cumsum(log_1m, axis=3, reverse=True) - log_1m
        A = jnp.where(mask, jnp.exp(log_a), 0.0)
        outs.append(jnp.einsum('bhqk,bhkd->bhqd', A, vb))
    o = jnp.concatenate(outs, axis=2)
    o = o * lax.rsqrt(jnp.mean(jnp.square(o), axis=-1, keepdims=True) + RMS_EPS)
    o = o * out_gain.astype(jnp.float32).reshape(H, N)[None, :, None, :]
    return o.transpose(0, 2, 1, 3).reshape(B, T, H * N)

def setup_inputs(seed: int = 0) -> dict:
    key = jax.random.key(seed)
    ks = jax.random.split(key, 24)
    f = jnp.float32
    nrm = lambda k, shape, fan_in: jax.random.normal(k, shape, f) * (fan_in ** -0.5)
    gain = lambda k, shape: 1.0 + 0.05 * jax.random.normal(k, shape, f)
    return {
        "x": jax.random.normal(ks[0], (BATCH, SEQ, D_MODEL), f),
        "meta_tokens": jax.random.normal(ks[1], (N_META, D_MODEL), f),
        "g_pre_mix": gain(ks[2], (DEPTH, D_MODEL)),
        "g_post_mix": gain(ks[3], (DEPTH, D_MODEL)),
        "g_pre_ffn": gain(ks[4], (DEPTH, D_MODEL)),
        "g_post_ffn": gain(ks[5], (DEPTH, D_MODEL)),
        "w_in": nrm(ks[6], (DEPTH, D_MODEL, IN_COLS), D_MODEL),
        "tshift_mu": jax.random.uniform(ks[7], (DEPTH, RWKV_COLS), f),
        "w_decay_up": 0.1 * nrm(ks[8], (DEPTH, DECAY_RANK, RWKV_WIDTH), DECAY_RANK),
        "decay_bias": jax.random.uniform(ks[9], (DEPTH, RWKV_WIDTH), f, -5.0, 1.0),
        "w_a_up": nrm(ks[10], (DEPTH, A_RANK, RWKV_WIDTH), A_RANK),
        "a_bias": 0.1 * jax.random.normal(ks[11], (DEPTH, RWKV_WIDTH), f),
        "w_g_up": nrm(ks[12], (DEPTH, GATE_RANK, RWKV_WIDTH), GATE_RANK),
        "k_k": 0.85 + 0.05 * jax.random.normal(ks[13], (DEPTH, RWKV_WIDTH), f),
        "k_a": gain(ks[14], (DEPTH, RWKV_WIDTH)),
        "r_k": 0.1 * jax.random.normal(ks[15], (DEPTH, RWKV_HEADS, HEAD_DIM), f),
        "lnx_gain": gain(ks[16], (DEPTH, RWKV_WIDTH)),
        "lnx_bias": 0.02 * jax.random.normal(ks[17], (DEPTH, RWKV_WIDTH), f),
        "sb_out_gain": gain(ks[18], (DEPTH, SB_WIDTH)),
        "w_out": nrm(ks[19], (DEPTH, D_MIX, D_MODEL), D_MIX),
        "w_ffn_up": nrm(ks[20], (DEPTH, D_MODEL, D_FF), D_MODEL),
        "w_ffn_down": nrm(ks[21], (DEPTH, D_FF, D_MODEL), D_FF),
    }

def reference(x, meta_tokens, g_pre_mix, g_post_mix, g_pre_ffn, g_post_ffn, w_in, tshift_mu,
              w_decay_up, decay_bias, w_a_up, a_bias, w_g_up, k_k, k_a, r_k, lnx_gain, lnx_bias,
              sb_out_gain, w_out, w_ffn_up, w_ffn_down):
    B = x.shape[0]
    meta = jnp.broadcast_to(meta_tokens[None].astype(x.dtype), (B, N_META, D_MODEL))
    h = jnp.concatenate([meta, x], axis=1)
    for l in range(DEPTH):
        xn = rmsnorm(h, g_pre_mix[l])
        p = xn @ w_in[l]
        p_rwkv, p_sb = p[..., :RWKV_COLS], p[..., RWKV_COLS:]
        y_a = rwkv7_group(p_rwkv, tshift_mu[l], w_decay_up[l], decay_bias[l], w_a_up[l], a_bias[l],
                          w_g_up[l], k_k[l], k_a[l], r_k[l], lnx_gain[l], lnx_bias[l])
        q, k, v = jnp.split(p_sb, 3, axis=-1)
        y_b = stick_breaking_group(q, k, v, sb_out_gain[l])
        y = jnp.concatenate([y_a, y_b], axis=-1).astype(h.dtype) @ w_out[l]
        h = h + rmsnorm(y, g_post_mix[l])
        m = rmsnorm(h, g_pre_ffn[l])
        m = jnp.square(jax.nn.relu(m @ w_ffn_up[l])) @ w_ffn_down[l]
        h = h + rmsnorm(m, g_post_ffn[l])
    return h[:, N_META:]


_drawn_inputs = setup_inputs


def setup_inputs(seed=0):
    import zlib

    import numpy as np

    out = dict(_drawn_inputs(seed))
    spreads = {}
    factors = {'w_decay_up': 8.0,
     'a_bias': 4.044,
     'k_k': 4.342,
     'k_a': 3.201,
     'lnx_gain': 3.262,
     'lnx_bias': 8.0}
    for name, (base, spread) in spreads.items():
        noise = np.random.default_rng([zlib.crc32(name.encode()), seed]).standard_normal(out[name].shape)
        drawn = base * np.exp(spread * noise) if base else spread * noise
        out[name] = __import__('jax').numpy.asarray(drawn.astype(out[name].dtype))
    for name, factor in factors.items():
        out[name] = (out[name] * factor).astype(out[name].dtype)
    return out
```

```python
import concourse.bass as bass
from concourse import mybir
from contextlib import ExitStack

F32 = mybir.dt.float32
F32R = mybir.dt.float32r
ALU = mybir.AluOpType
ACT = mybir.ActivationFunctionType
ds = bass.ds

P = 128
D = 1024
KD = D // P
META = 16
SEQ = 1024
T = META + SEQ
HD = 64
RW = 512
PAIRS = RW // P
CH = 64
TPAD = 1088
PAD = TPAD - T
CHUNKS = TPAD // CH
IN_TILES = 26
T_R, T_K, T_V, T_DA, T_G, T_SQ, T_SK, T_SV = 0, 4, 8, 12, 13, 14, 18, 22
FF = 4 * D
FF_TILES = FF // P
TOK_TILES = SEQ // P
RMS_EPS = 1e-6
GN_EPS = 1e-5 * HD
TOK_GROUPS = [(0, 348), (348, 346), (694, 346)]


class Mem:

    def __init__(self, nc, ctx, stage):
        self.nc, self.ctx, self.stage = nc, ctx, stage

    def sb(self, name, shape, dt=F32):
        return self.ctx.enter_context(self.nc.sbuf_tensor(f"{self.stage}_{name}", shape, dt))

    def ps(self, name, shape=(P, 512)):
        return self.ctx.enter_context(self.nc.psum_tensor(f"{self.stage}_{name}", list(shape), F32))

    def sem(self, name):
        return self.ctx.enter_context(self.nc.semaphore(f"{self.stage}_{name}"))


def stage_constants(nc, ident, ones_bd):
    with ExitStack() as ctx:
        m = Mem(nc, ctx, "const")
        filled, zeroed, done = m.sem("filled"), m.sem("zeroed"), m.sem("done")
        block = ctx.enter_context(nc.Block())

        @block.gpsimd
        def _(pool):
            pool.memset(ident[:, :], 0.0).then_inc(filled, 1)
            pool.wait_ge(filled, 1)
            pool.affine_select(out=ident[:, :], in_=ident[:, :], compare_op=ALU.not_equal, fill=1.0,
                               base=0, pattern=[[-1, P]], channel_multiplier=1).then_inc(done, 1)

        @block.vector
        def _(dve):
            dve.memset(ones_bd[:, :], 0.0).then_inc(zeroed, 1)
            dve.wait_ge(zeroed, 1)
            for h in range(2):
                half = ones_bd[h * HD:(h + 1) * HD, h * HD:(h + 1) * HD]
                dve.memset(half, 1.0).then_inc(done, 1)
            dve.wait_ge(done, 3)


def stage_norm_transpose(nc, name, rows_of, rows0, gain_cols, ident, xh, xl):
    first = rows0.shape[0] if rows0 is not None else 0
    lead = 1 if first else 0
    with ExitStack() as ctx:
        m = Mem(nc, ctx, name)
        x = [m.sb(f"x{s}", [P, D]) for s in range(2)]
        xs = [m.sb(f"xs{s}", [P, D]) for s in range(2)]
        xf = [m.sb(f"xf{s}", [P, KD, P]) for s in range(2)]
        square = m.sb("square", [P, D])
        sumsq = [m.sb(f"sumsq{s}", [P, 1]) for s in range(2)]
        root = [m.sb(f"root{s}", [P, 1]) for s in range(2)]
        rinv = [m.sb(f"rinv{s}", [P, 1]) for s in range(2)]
        gain = m.sb("gain", [P, KD])
        eps = m.sb("eps", [P, 1])
        tp = [[m.ps(f"tp{s}{b}") for b in range(2)] for s in range(2)]
        loaded = [m.sem(f"loaded{s}") for s in range(2)]
        gain_loaded, eps_set = m.sem("gain_loaded"), m.sem("eps_set")
        x_free = m.sem("x_free")
        squared, rooted, inverted, scaled = m.sem("squared"), m.sem("rooted"), m.sem("inverted"), m.sem("scaled")
        turned, gained, high, low = m.sem("turned"), m.sem("gained"), m.sem("high"), m.sem("low")
        block = ctx.enter_context(nc.Block())

        def each(eng, step):
            if lead:
                step(0, 0, 0, first, 0)
            with eng.Fori(0, TOK_TILES // 2) as i:
                for s in range(2):
                    slot = (s + lead) % 2
                    step(slot, i + (1 if lead and slot == 0 else 0), i * 2 + (s + lead), P,
                         i * 2 * P + (first + s * P))

        @block.sync
        def _(sp):
            sp.dma_start(gain[:, :], gain_cols).then_inc(gain_loaded, 16)

            def load(s, i, n, rows, c0):
                sp.wait_ge(x_free, n)
                src = rows0 if rows != P else rows_of(c0 - first if lead else c0)
                sp.dma_start(x[s][0:rows, :], src).then_inc(loaded[s], 16)
            each(sp, load)

        @block.scalar
        def _(act):
            act.wait_ge(eps_set, 1)

            def norm(s, i, n, rows, c0):
                act.wait_ge(loaded[s], i * 16 + 16)
                act.wait_ge(inverted, n)
                act.activation(square[0:rows, :], x[s][0:rows, :], ACT.Square,
                               accum_out=sumsq[s][0:rows, :]).then_inc(squared, 1)
                act.wait_ge(squared, n + 1)
                act.activation(root[s][0:rows, :], sumsq[s][0:rows, :], ACT.Sqrt,
                               scale=1.0 / D, bias=eps[0:rows, :]).then_inc(rooted, 1)
                act.wait_ge(gained, n * 2 + 2)
                act.activation(xh[:, :, ds(c0, rows)], xf[s][:, :, 0:rows], ACT.Copy).then_inc(high, 1)
            each(act, norm)

        @block.vector
        def _(dve):
            dve.memset(eps[:, :], RMS_EPS).then_inc(eps_set, 1)
            dve.wait_ge(gain_loaded, 16)

            def scale(s, i, n, rows, c0):
                dve.wait_ge(rooted, n + 1)
                dve.reciprocal(rinv[s][0:rows, :], root[s][0:rows, :]).then_inc(inverted, 1)
                dve.wait_ge(inverted, n + 1)
                dve.wait_ge(turned, n)
                dve.tensor_scalar(xs[s][0:rows, :], x[s][0:rows, :], rinv[s][0:rows, :], None,
                                  ALU.mult).then_inc(scaled, 1)
                dve.wait_ge(scaled, n + 1)
                dve.sem_inc(x_free, 1)
                dve.wait_ge(turned, n + 1)
                dve.wait_ge(low, n)
                for b in range(2):
                    half = tp[s][b][:, :].rearrange("p (k c) -> p k c", k=4)[:, :, 0:rows]
                    g = gain[:, 4 * b:4 * b + 4].unsqueeze(2).broadcast_to((P, 4, rows))
                    dve.tensor_tensor(xf[s][:, 4 * b:4 * b + 4, 0:rows], half, g, ALU.mult).then_inc(gained, 1)
            each(dve, scale)

        @block.tensor
        def _(pe):
            def turn(s, i, n, rows, c0):
                pe.wait_ge(scaled, n + 1)
                pe.wait_ge(gained, n * 2)
                for k in range(KD):
                    last = pe.transpose(tp[s][k // 4][:, (k % 4) * P:(k % 4) * P + rows],
                                        xs[s][0:rows, k * P:(k + 1) * P], ident[0:rows, 0:rows])
                last.then_inc(turned, 1)
            each(pe, turn)

        @block.gpsimd
        def _(pool):
            def remainder(s, i, n, rows, c0):
                pool.wait_ge(high, n + 1)
                pool.tensor_tensor(xl[:, :, ds(c0, rows)], xf[s][:, :, 0:rows],
                                   xh[:, :, ds(c0, rows)].bitcast(F32), ALU.subtract).then_inc(low, 1)
            each(pool, remainder)


def stage_in_proj(nc, w_in, p_dram, xh, xl):
    with ExitStack() as ctx:
        m = Mem(nc, ctx, "inproj")
        raw = [m.sb(f"raw{s}", [P, KD, P]) for s in range(2)]
        wh = [m.sb(f"wh{s}", [P, KD, P], F32R) for s in range(2)]
        wl = [m.sb(f"wl{s}", [P, KD, P], F32R) for s in range(2)]
        out = [m.sb(f"out{s}", [P, T]) for s in range(2)]
        acc = [[m.ps(f"acc{s}{g}") for g in range(3)] for s in range(2)]
        loaded = [m.sem(f"loaded{s}") for s in range(2)]
        stored = [m.sem(f"stored{s}") for s in range(2)]
        raw_free = m.sem("raw_free")
        w_high, w_low = m.sem("w_high"), m.sem("w_low")
        w_free = m.sem("w_free")
        group_done = m.sem("group_done")
        group_read = m.sem("group_read")
        AHEAD = 5
        block = ctx.enter_context(nc.Block())

        @block.sync
        def _(sp):
            for s in range(2):
                sp.dma_start(raw[s][:, :, :], w_in[s]).then_inc(loaded[s], 16)
            with sp.Fori(0, IN_TILES // 2 - 1) as i:
                for s in range(2):
                    sp.wait_ge(raw_free, i * 2 + (s + 1))
                    sp.dma_start(raw[s][:, :, :], w_in[ds(i * 2 + (s + 2), 1)].squeeze(0)).then_inc(loaded[s], 16)

        @block.gpsimd
        def _(pool):
            with pool.Fori(0, IN_TILES // 2) as i:
                for s in range(2):
                    pool.wait_ge(group_read, i * 6 + (3 * (s + 1) + AHEAD))
                    pool.dma_start(p_dram[ds(i * 2 + s, 1)].squeeze(0)[:, PAD:TPAD],
                                   out[s][:, :]).then_inc(stored[s], 16)
            for s in range(2):
                pool.wait_ge(stored[s], 16 * (IN_TILES // 2))

        @block.scalar
        def _(act):
            def high(s, i):
                act.wait_ge(loaded[s], i * 16 + 16)
                act.wait_ge(w_free, i * 2 + (s + 1))
                act.activation(wh[s][:, :, :], raw[s][:, :, :], ACT.Copy).then_inc(w_high, 1)

            act.sem_inc(group_read, AHEAD)
            high(0, 0)
            def drain(s, i):
                act.wait_ge(stored[s], i * 16)
                for g, (c, n) in enumerate(TOK_GROUPS):
                    act.wait_ge(group_done, i * 6 + (3 * s + g + 1))
                    act.activation(out[s][:, c:c + n], acc[s][g][:, 0:n], ACT.Copy).then_inc(group_read, 1)

            with act.Fori(0, IN_TILES // 2 - 1) as i:
                high(1, i)
                drain(0, i)
                high(0, i + 1)
                drain(1, i)
            high(1, IN_TILES // 2 - 1)
            drain(0, IN_TILES // 2 - 1)
            drain(1, IN_TILES // 2 - 1)

        @block.vector
        def _(dve):
            with dve.Fori(0, IN_TILES // 2) as i:
                for s in range(2):
                    dve.wait_ge(w_high, i * 2 + (s + 1))
                    dve.tensor_tensor(wl[s][:, :, :], raw[s][:, :, :], wh[s][:, :, :].bitcast(F32),
                                      ALU.subtract).then_inc(w_low, 1)
                    dve.wait_ge(w_low, i * 2 + (s + 1))
                    dve.sem_inc(raw_free, 1)

        @block.tensor
        def _(pe):
            pe.sem_inc(w_free, 2)
            with pe.Fori(0, IN_TILES // 2) as i:
                for s in range(2):
                    pe.wait_ge(w_high, i * 2 + (s + 1))
                    pe.wait_ge(w_low, i * 2 + (s + 1))
                    for g, (c, n) in enumerate(TOK_GROUPS):
                        pe.wait_ge(group_read, i * 6 + (3 * s + g))
                        for k in range(KD):
                            for j, (w, xx) in enumerate([(wh, xh), (wh, xl), (wl, xh)]):
                                last = pe.matmul(acc[s][g][:, 0:n], w[s][:, k, :], xx[:, k, c:c + n],
                                                 start=(k == 0 and j == 0), stop=(k == KD - 1 and j == 2))
                        last.then_inc(group_done, 1)
                    pe.sem_inc(w_free, 1)
import math

DECAY_C = math.exp(-0.5)
PGROUPS = [(0, 364), (364, 362), (726, 362)]
XGROUPS = [(CH, 512), (CH + 512, 512)]
V_MU, V_DB, V_AB, V_KK, V_KA, V_RK = 0, 3, 4, 5, 6, 7
NV = 8
F_A, F_R, F_B, F_K, F_V = range(5)


def stand_alone(eng):
    eng.nop(nofuse=True)


class Steps:

    def __init__(self, sem, names):
        self.sem, self.names, self.seen = sem, names.split(), 0

    def at(self, i, name):
        return i * len(self.names) + (self.names.index(name) + 1)

    def done(self, ins, name):
        assert self.names[self.seen % len(self.names)] == name, (name, self.names[self.seen % len(self.names)])
        self.seen += 1
        ins.then_inc(self.sem, 1)

    def wait(self, eng, i, name):
        eng.wait_ge(self.sem, self.at(i, name))


def stage_rwkv_prep(nc, p_dram, vecs, mu_low, w_decay_up, w_a_up, w_g_up, chunk_dram, gate_dram, bonus_dram,
                    pc, ones_bd):
    with ExitStack() as ctx:
        m = Mem(nc, ctx, "prep")
        low = m.sb("low", [P, 2, TPAD + 1])
        rkv = m.sb("rkv", [P, 3, TPAD + 1])
        mul = m.sb("mul", [P, 2])
        omul = m.sb("omul", [P, 2])
        tl = m.sb("tl", [P, TPAD])
        sg = m.sb("sg", [P, TPAD])
        wlow = m.sb("wlow", [P, 3, P])
        vec = m.sb("vec", [P, NV])
        omv = m.sb("omv", [P, 4])
        prev = [m.sb(f"prev{j}", [P, TPAD]) for j in range(3)]
        r = m.sb("r", [P, TPAD])
        k = m.sb("k", [P, TPAD])
        sw = m.sb("sw", [P, TPAD])
        aa = m.sb("aa", [P, TPAD])
        gate = m.sb("gate", [P, SEQ])
        bv = m.sb("bv", [P, SEQ])
        cum = m.sb("cum", [P, TPAD])
        grow = m.sb("grow", [P, CHUNKS, CH])
        fade = m.sb("fade", [P, CHUNKS, CH + 1])
        keep = m.sb("keep", [P, CHUNKS, CH])
        kk = m.sb("kk", [P, TPAD])
        sq = m.sb("sq", [P, TPAD])
        root = m.sb("root", [P, TPAD])
        fields = m.sb("fields", [P, CHUNKS, 5, CH])
        tiny = m.sb("tiny", [P, 1])
        bank = [m.ps(f"bank{b}") for b in range(5)]
        loaded, low_loaded, stored = m.sem("loaded"), m.sem("low_loaded"), m.sem("stored")
        init, lowp, lowa = m.sem("init"), m.sem("lowp"), m.sem("lowa")
        V = Steps(m.sem("vec_done"), "om omka r k v t1 kmod scan rinv A B rk bv0 bv1")
        A = Steps(m.sem("act_done"), "w0 w1 w2 a0 a1 a2 g0 g1 sq fade grow pc root0 root1 root2")
        G = Steps(m.sem("pool_done"), "p0 p1 p2 kk kkn R ka K")
        M = Steps(m.sem("mm_done"), "w0 w1 w2 a0 a1 a2 g0 g1 n0 n1 n2 b0 b1")
        block = ctx.enter_context(nc.Block())
        c3 = lambda t: t[:, :].rearrange("p (c n) -> p c n", n=CH)

        @block.sync
        def _(sp):
            sp.wait_ge(init, 7)
            for j, t in enumerate((T_DA, T_G)):
                sp.dma_start(low[:, j, 1 + PAD:], p_dram[t, :, PAD:TPAD]).then_inc(low_loaded, 16)
            sp.dma_start(mul[:, :], mu_low).then_inc(low_loaded, 16)
            with sp.Fori(0, PAIRS) as i:
                for steps in (V, G, M):
                    sp.wait_ge(steps.sem, i * len(steps.names))
                    stand_alone(sp)
                for j, t in enumerate((T_R, T_K, T_V)):
                    sp.dma_start(rkv[:, j, 1 + PAD:], p_dram[ds(i + t, 1)].squeeze(0)[:, PAD:TPAD]).then_inc(loaded, 16)
                sp.dma_start(vec[:, :], vecs[ds(i, 1)].squeeze(0)).then_inc(loaded, 16)
                sp.dma_start(wlow[0:HD, 0, :], w_decay_up[:, ds(i * P, P)]).then_inc(loaded, 16)
                sp.dma_start(wlow[HD:P, 1, :], w_a_up[:, ds(i * P, P)]).then_inc(loaded, 16)
                sp.dma_start(wlow[:, 2, :], w_g_up[:, ds(i * P, P)]).then_inc(loaded, 16)
                for steps, name in ((V, "bv1"), (G, "K"), (A, "root2")):
                    steps.wait(sp, i, name)
                    stand_alone(sp)
                sp.dma_start(chunk_dram[ds(i, 1)].squeeze(0).rearrange("c p f -> p c f"),
                             fields[:, :, :, :].rearrange("p c f n -> p c (f n)")).then_inc(stored, 16)
                sp.dma_start(gate_dram[ds(i, 1)].squeeze(0), gate[:, :]).then_inc(stored, 16)
                sp.dma_start(bonus_dram[ds(i, 1)].squeeze(0), bv[:, :]).then_inc(stored, 16)
                sp.wait_ge(stored, i * 48 + 48)
                stand_alone(sp)

        @block.gpsimd
        def _(pool):
            pool.wait_ge(low_loaded, 48)
            for j in range(2):
                pool.tensor_scalar(prev[j][:, :], low[:, j, 0:TPAD], mul[:, j:j + 1], None, ALU.mult).then_inc(lowp, 1)
            pool.wait_ge(lowa, 2)
            with pool.Fori(0, PAIRS) as i:
                pool.wait_ge(loaded, i * 112 + 112)
                V.wait(pool, i, "om")
                stand_alone(pool)
                for j in range(3):
                    G.done(pool.tensor_scalar(prev[j][:, :], rkv[:, j, 0:TPAD], vec[:, V_MU + j:V_MU + j + 1],
                                              None, ALU.mult), f"p{j}")
                V.wait(pool, i, "k")
                stand_alone(pool)
                G.done(pool.tensor_scalar(kk[:, :], k[:, :], vec[:, V_KK:V_KK + 1], None, ALU.mult), "kk")
                V.wait(pool, i, "rinv")
                G.wait(pool, i, "kk")
                G.done(pool.tensor_tensor(kk[:, :], kk[:, :], root[:, :], ALU.mult), "kkn")
                A.wait(pool, i, "pc")
                G.done(pool.tensor_tensor(fields[:, :, F_R, :], c3(r), fade[:, :, 1:], ALU.mult), "R")
                G.wait(pool, i, "kkn")
                G.done(pool.tensor_tensor(sq[:, :], kk[:, :], aa[:, :], ALU.mult), "ka")
                G.done(pool.tensor_tensor(fields[:, :, F_K, :], c3(k), grow[:, :, :], ALU.mult), "K")

        @block.scalar
        def _(act):
            act.wait_ge(lowp, 5)
            act.activation(tl[0:HD, :], tl[0:HD, :], ACT.Tanh).then_inc(lowa, 1)
            act.activation(sg[:, :], sg[:, :], ACT.Sigmoid).then_inc(lowa, 1)
            with act.Fori(0, PAIRS) as i:
                act.wait_ge(V.sem, i * len(V.names))
                act.wait_ge(G.sem, i * len(G.names))
                act.wait_ge(loaded, i * 112 + 112)
                for g, (c, n) in enumerate(PGROUPS):
                    M.wait(act, i, f"w{g}")
                    A.done(act.activation(sw[:, c:c + n], bank[g][:, 0:n], ACT.Sigmoid, bias=vec[:, V_DB:V_DB + 1]), f"w{g}")
                for g, (c, n) in enumerate(PGROUPS):
                    M.wait(act, i, f"a{g}")
                    A.done(act.activation(aa[:, c:c + n], bank[g][:, 0:n], ACT.Sigmoid, bias=vec[:, V_AB:V_AB + 1]), f"a{g}")
                act.wait_ge(stored, i * 48)
                for g, (c, n) in enumerate(XGROUPS):
                    M.wait(act, i, f"g{g}")
                    A.done(act.activation(gate[:, c - CH:c - CH + n], bank[3 + g][:, 0:n], ACT.Copy), f"g{g}")
                G.wait(act, i, "kk")
                A.done(act.activation(sq[:, :], kk[:, :], ACT.Square), "sq")
                V.wait(act, i, "scan")
                A.done(act.activation(fade[:, :, 1:], c3(cum), ACT.Exp, scale=-DECAY_C), "fade")
                A.done(act.activation(grow[:, :, :], c3(cum), ACT.Exp, scale=DECAY_C), "grow")
                A.wait(act, i, "fade")
                A.done(act.activation(pc[:, ds(i, 1), :].squeeze(1), fade[:, :, CH], ACT.Copy), "pc")
                for g, (c, n) in enumerate(PGROUPS):
                    M.wait(act, i, f"n{g}")
                    A.done(act.activation(root[:, c:c + n], bank[g][:, 0:n], ACT.Sqrt, bias=tiny[:, :]), f"root{g}")

        @block.vector
        def _(dve):
            dve.memset(low[:, :, 0:1 + PAD], 0.0).then_inc(init, 1)
            dve.memset(rkv[:, :, 0:1 + PAD], 0.0).then_inc(init, 1)
            dve.memset(wlow[:, 0:2, :], 0.0).then_inc(init, 1)
            dve.memset(fade[:, :, 0:1], 1.0).then_inc(init, 1)
            dve.memset(tiny[:, :], 1e-12).then_inc(init, 1)
            dve.memset(keep[:, :, :], 1.0).then_inc(init, 1)
            dve.wait_ge(init, 6)
            dve.memset(keep[:, :, 0:1], 0.0).then_inc(init, 1)
            dve.wait_ge(low_loaded, 48)
            dve.tensor_scalar(omul[:, :], mul[:, :], -1.0, 1.0, ALU.mult, ALU.add).then_inc(lowp, 1)
            dve.wait_ge(lowp, 3)
            for j, t in enumerate((tl, sg)):
                dve.scalar_tensor_tensor(t[:, :], low[:, j, 1:], omul[:, j:j + 1], prev[j][:, :],
                                         ALU.mult, ALU.add).then_inc(lowp, 1)
            with dve.Fori(0, PAIRS) as i:
                dve.wait_ge(loaded, i * 112 + 112)
                V.done(dve.tensor_scalar(omv[:, 0:3], vec[:, V_MU:V_MU + 3], -1.0, 1.0, ALU.mult, ALU.add), "om")
                V.done(dve.tensor_scalar(omv[:, 3:4], vec[:, V_KA:V_KA + 1], -1.0, 1.0, ALU.mult, ALU.add), "omka")
                V.wait(dve, i, "omka")
                dve.wait_ge(stored, i * 48)
                for j, (t, name) in enumerate(((r[:, :], "r"), (k[:, :], "k"), (fields[:, :, F_V, :], "v"))):
                    G.wait(dve, i, f"p{j}")
                    cur, before = rkv[:, j, 1:], prev[j][:, :]
                    if name == "v":
                        cur, before = (a.rearrange("p (c n) -> p c n", n=CH) for a in (cur, before))
                    V.done(dve.scalar_tensor_tensor(t, cur, omv[:, j:j + 1], before, ALU.mult, ALU.add), name)
                V.wait(dve, i, "v")
                A.wait(dve, i, "a2")
                V.done(dve.tensor_scalar(prev[0][:, :], aa[:, :], vec[:, V_KA:V_KA + 1], omv[:, 3:4], ALU.mult, ALU.add), "t1")
                V.wait(dve, i, "t1")
                G.wait(dve, i, "kk")
                V.done(dve.tensor_tensor(k[:, :], k[:, :], prev[0][:, :], ALU.mult), "kmod")
                V.done(dve.tensor_tensor_scan(cum[:, :], keep[:, :, :].rearrange("p c n -> p (c n)"), sw[:, :], 0.0,
                                              ALU.mult, ALU.add), "scan")
                A.wait(dve, i, "root2")
                V.done(dve.reciprocal(root[:, :], root[:, :]), "rinv")
                G.wait(dve, i, "kkn")
                V.done(dve.scalar_tensor_tensor(fields[:, :, F_A, :], c3(kk), -1.0, fade[:, :, 0:CH], ALU.mult, ALU.mult), "A")
                G.wait(dve, i, "ka")
                V.done(dve.tensor_tensor(fields[:, :, F_B, :], c3(sq), grow[:, :, :], ALU.mult), "B")
                V.done(dve.scalar_tensor_tensor(prev[1][:, :], r[:, :], vec[:, V_RK:V_RK + 1], k[:, :], ALU.mult, ALU.mult), "rk")
                for g, (c, n) in enumerate(XGROUPS):
                    M.wait(dve, i, f"b{g}")
                    vv = fields[:, c // CH:(c + n) // CH, F_V, :]
                    V.done(dve.tensor_tensor(bv[:, c - CH:c - CH + n].rearrange("p (c n) -> p c n", n=CH),
                                             bank[3 + g][:, 0:n].rearrange("p (c n) -> p c n", n=CH), vv, ALU.mult), f"bv{g}")

        @block.tensor
        def _(pe):
            pe.wait_ge(lowa, 2)
            pe.wait_ge(lowp, 5)
            with pe.Fori(0, PAIRS) as i:
                pe.wait_ge(loaded, i * 112 + 112)
                pe.wait_ge(V.sem, i * len(V.names))
                pe.wait_ge(A.sem, i * len(A.names))
                for g, (c, n) in enumerate(PGROUPS):
                    M.done(pe.matmul(bank[g][:, 0:n], wlow[:, 0, :], tl[:, c:c + n], start=True, stop=True), f"w{g}")
                for g, (c, n) in enumerate(PGROUPS):
                    A.wait(pe, i, f"w{g}")
                    M.done(pe.matmul(bank[g][:, 0:n], wlow[:, 1, :], tl[:, c:c + n], start=True, stop=True), f"a{g}")
                for g, (c, n) in enumerate(XGROUPS):
                    M.done(pe.matmul(bank[3 + g][:, 0:n], wlow[:, 2, :], sg[:, c:c + n], start=True, stop=True), f"g{g}")
                A.wait(pe, i, "sq")
                for g, (c, n) in enumerate(PGROUPS):
                    M.done(pe.matmul(bank[g][:, 0:n], ones_bd[:, :], sq[:, c:c + n], start=True, stop=True), f"n{g}")
                V.wait(pe, i, "rk")
                for g, (c, n) in enumerate(XGROUPS):
                    M.done(pe.matmul(bank[3 + g][:, 0:n], ones_bd[:, :], prev[1][:, c:c + n], start=True, stop=True), f"b{g}")

LEVELS = [2, 4, 8, 16, 32]


M_N, M_K, M_R, M_L1T, M_LEVEL = 0, 1, 2, 3, 4
N_MASKS = M_LEVEL + len(LEVELS)


def stage_rwkv_masks(nc, masks):
    with ExitStack() as ctx:
        m = Mem(nc, ctx, "masks")
        step = m.sem("step")
        ones = m.sem("ones")
        block = ctx.enter_context(nc.Block())
        count = [0]

        @block.vector
        def _(dve):
            dve.memset(masks[:, :, :], 1.0).then_inc(ones, 1)

        @block.gpsimd
        def _(pool):
            pool.wait_ge(ones, 1)

            def select(view, pattern, base, mult, op=ALU.is_ge):
                pool.affine_select(out=view, in_=view, compare_op=op, fill=0.0, base=base, pattern=pattern,
                                   channel_multiplier=mult).then_inc(step, 1)
                count[0] += 1
                pool.wait_ge(step, count[0])

            def heads(k):
                return masks[:, k, :].rearrange("p (h n) -> p h n", h=2)

            for k in (M_N, M_K, M_R):
                op = ALU.is_ge if k == M_R else ALU.is_gt
                for h in range(2):
                    rows = slice(h * HD, (h + 1) * HD)
                    v = masks[rows, k, :].rearrange("p (h n) -> p h n", h=2)
                    select(v, [[0, 2], [1, CH]], 0, -1, op)
            select(heads(M_N), [[-CH, 2], [0, CH]], 0, 1)
            select(heads(M_N), [[CH, 2], [0, CH]], CH - 1, -1)
            select(masks[0:HD, M_K, 0:CH], [[0, CH]], -1, 0)
            select(masks[HD:P, M_K, CH:P], [[0, CH]], -1, 0)
            pairs2 = lambda k, b: masks[:, k, :].rearrange("p (j c) -> p j c", c=b)
            def block_diag(view, n, b):
                select(view, [[-b, n], [0, b]], 0, 1)
                select(view, [[b, n], [0, b]], b - 1, -1)
            block_diag(pairs2(M_L1T, 2), P // 2, 2)
            select(masks[:, M_L1T, :], [[1, P]], 0, -1, ALU.is_gt)
            for j, l in enumerate(LEVELS):
                k = M_LEVEL + j
                b = 2 * l
                v = pairs2(k, b)
                select(v, [[-b, P // b], [0, b]], -l, 1)
                select(v, [[b, P // b], [0, b]], b - 1, -1)
                select(v, [[0, P // b], [-1, b]], l - 1, 0)


def stage_rwkv_scan(nc, chunk_dram, masks, ident, pc, y_sb):
    with ExitStack() as ctx:
        m = Mem(nc, ctx, "scan")
        ar = [m.sb(f"ar{s}", [P, PAIRS, 3, 2, CH]) for s in range(2)]
        bkb = [m.sb(f"bkb{s}", [P, PAIRS, 3, CH]) for s in range(2)]
        v2 = [m.sb(f"v2{s}", [P, PAIRS, 2, CH]) for s in range(2)]
        nl = m.sb("nl", [P, PAIRS, 2, P])
        rb = m.sb("rb", [P, PAIRS, 2, 2, CH])
        x = m.sb("x", [P, PAIRS, P])
        xt = m.sb("xt", [P, PAIRS, P])
        z = m.sb("z", [P, PAIRS, P])
        ak = m.sb("ak", [P, PAIRS, 2, CH])
        wuv = m.sb("wuv", [P, PAIRS, 2, 2, CH])
        qm = m.sb("qm", [P, PAIRS, 2, 2, CH])
        state = m.sb("state", [P, PAIRS, CH])
        bank = [[m.ps(f"bank{q}{b}") for b in range(2)] for q in range(PAIRS)]
        loaded = [m.sem(f"loaded{s}") for s in range(2)]
        zeroed = m.sem("zeroed")
        qs = range(PAIRS)
        every = lambda names: " ".join(f"{n}{q}" for n in names.split() for q in qs)
        inv = " ".join(f"z{l} x{l}" for l in LEVELS)
        V = Steps(m.sem("vec_done"), every(f"nl rl x1a x1b {inv} qm0 qm1 s"))
        A = Steps(m.sem("act_done"), every(f"ta0 ta1 tv0 tv1 tbk lv x0 {' '.join(f't{l}' for l in LEVELS)} w0 w1 y"))
        M = Steps(m.sem("mm_done"), every(f"g tp x0 lv {' '.join(f'n{l} x{l} t{l}' for l in LEVELS)} wu qm sy"))
        block = ctx.enter_context(nc.Block())

        def laps(eng, lap):
            with eng.Fori(0, CHUNKS // 2) as i:
                for s in range(2):
                    lap(i * 2 + s, s, i)
            lap(CHUNKS - 1, 0, CHUNKS // 2)

        LOADS = 8 * 16
        ZEROED = 7

        @block.sync
        def _(sp):
            def load(n, s):
                src = chunk_dram[:, ds(n, 1)].squeeze(1).rearrange("q p f -> p q f")
                for h in range(2):
                    rows = slice(h * HD, (h + 1) * HD)
                    for f in (F_A, F_R):
                        sp.dma_start(ar[s][rows, :, f, h, :], src[rows, :, f * CH:(f + 1) * CH]).then_inc(loaded[s], 16)
                sp.dma_start(bkb[s][:, :, 0:2, :].rearrange("p q f n -> p q (f n)"),
                             src[:, :, 2 * CH:4 * CH]).then_inc(loaded[s], 16)
                sp.dma_start(bkb[s][:, :, 2, :], src[:, :, 2 * CH:3 * CH]).then_inc(loaded[s], 16)
                for h in range(2):
                    sp.dma_start(v2[s][:, :, h, :], src[:, :, 4 * CH:]).then_inc(loaded[s], 16)

            def reload(n, s, before):
                for steps in (V, M):
                    sp.wait_ge(steps.sem, before * len(steps.names))
                    stand_alone(sp)
                load(n, s)

            sp.wait_ge(zeroed, ZEROED)
            load(0, 0)
            load(1, 1)
            with sp.Fori(1, CHUNKS // 2) as i:
                for s in range(2):
                    reload(i * 2 + s, s, i * 2 + (s - 1))
            reload(CHUNKS - 1, 0, CHUNKS - 2)


        @block.vector
        def _(dve):
            for s in range(2):
                dve.memset(ar[s][:, :, 0:2, :, :].rearrange("p q f h n -> p q (f h n)"), 0.0).then_inc(zeroed, 1)
                for h in range(2):
                    same = ident[:, :].rearrange("p (h n) -> p h n", h=2)
                    rows = slice(h * HD, (h + 1) * HD)
                    for q in qs:
                        last = dve.tensor_copy(ar[s][rows, q, 2, h, :], same[rows, h, :])
                last.then_inc(zeroed, 1)
            dve.memset(wuv[:, :, :, :, :], 0.0).then_inc(zeroed, 1)
            dve.memset(qm[:, :, :, :, :], 0.0).then_inc(zeroed, 1)
            dve.memset(state[:, :, :], 0.0).then_inc(zeroed, 1)
            dve.wait_ge(zeroed, ZEROED)

            def lap(n, s, i):
                for q in qs:
                    M.wait(dve, n, f"g{q}")
                    both = bank[q][1][:, 0:P].unsqueeze(1).broadcast_to((P, 2, P))
                    V.done(dve.tensor_tensor(nl[:, q, :, :], both, masks[:, M_N:M_N + 2, :], ALU.mult), f"nl{q}")
                for q in qs:
                    V.done(dve.tensor_tensor(rb[:, q, 0, :, :].rearrange("p h n -> p (h n)"), bank[q][1][:, P:2 * P],
                                             masks[:, M_R, :], ALU.mult), f"rl{q}")
                for q in qs:
                    V.wait(dve, n, f"nl{q}")
                    V.done(dve.tensor_tensor(xt[:, q, :], nl[:, q, 0, :], masks[:, M_L1T, :], ALU.mult), f"x1a{q}")
                for q in qs:
                    V.wait(dve, n, f"x1a{q}")
                    V.done(dve.tensor_tensor(xt[:, q, :], xt[:, q, :], ident[:, :], ALU.add), f"x1b{q}")
                for j, l in enumerate(LEVELS):
                    for q in qs:
                        M.wait(dve, n, f"n{l}{q}")
                        V.done(dve.tensor_tensor(z[:, q, :], bank[q][0][:, 0:P], masks[:, M_LEVEL + j, :], ALU.mult), f"z{l}{q}")
                    for q in qs:
                        M.wait(dve, n, f"x{l}{q}")
                        V.done(dve.tensor_tensor(x[:, q, :], x[:, q, :], bank[q][1][:, 0:P], ALU.add), f"x{l}{q}")
                for h in range(2):
                    rows = slice(h * HD, (h + 1) * HD)
                    for q in qs:
                        M.wait(dve, n, f"qm{q}")
                        V.done(dve.tensor_tensor(
                            qm[rows, q, :, h, :], bank[q][0][rows, 0:2 * P].rearrange("p (f h n) -> p f h n", f=2, h=2)[:, :, h, :],
                            ar[s][rows, q, 1:3, h, :], ALU.add), f"qm{h}{q}")
                for q in qs:
                    A.wait(dve, n, f"y{q}")
                    V.done(dve.tensor_scalar(state[:, q, :], bank[q][1][:, 0:CH], pc[:, q, ds(n, 1)], None, ALU.mult), f"s{q}")
            laps(dve, lap)

        @block.scalar
        def _(act):
            act.wait_ge(zeroed, ZEROED)

            def lap(n, s, i):
                def copy(out, in_, name):
                    A.done(act.activation(out, in_, ACT.Copy), name)
                lo, hi = slice(0, HD), slice(HD, P)
                for q in qs:
                    M.wait(act, n, f"tp{q}")
                    copy(ak[lo, q, 0, :], bank[q][0][lo, 0:CH], f"ta0{q}")
                for q in qs:
                    copy(ak[hi, q, 0, :], bank[q][0][hi, CH:2 * CH], f"ta1{q}")
                for q in qs:
                    copy(wuv[hi, q, 1, 0, :], bank[q][0][hi, P:P + CH], f"tv0{q}")
                for q in qs:
                    copy(wuv[lo, q, 1, 1, :], bank[q][0][lo, P + CH:2 * P], f"tv1{q}")
                for q in qs:
                    t = bank[q][0][:, 2 * P:4 * P].rearrange("p (t n) -> p t n", n=CH)[:, 0:4:3, :]
                    copy(rb[:, q, 1, :, :], t, f"tbk{q}")
                for q in qs:
                    M.wait(act, n, f"lv{q}")
                    copy(ak[:, q, 1, :], bank[q][0][:, 0:CH], f"lv{q}")
                for q in qs:
                    M.wait(act, n, f"x0{q}")
                    copy(x[:, q, :], bank[q][1][:, 0:P], f"x0{q}")
                for l in LEVELS:
                    for q in qs:
                        M.wait(act, n, f"t{l}{q}")
                        copy(xt[:, q, :], bank[q][1][:, 0:P], f"t{l}{q}")
                for h in range(2):
                    rows = slice(h * HD, (h + 1) * HD)
                    for q in qs:
                        M.wait(act, n, f"wu{q}")
                        copy(wuv[rows, q, :, h, :], bank[q][1][rows, 0:P].rearrange("p (f n) -> p f n", f=2), f"w{h}{q}")
                for q in qs:
                    M.wait(act, n, f"sy{q}")
                    copy(y_sb[:, q, ds(n * CH, CH)], bank[q][1][:, CH:P], f"y{q}")
            laps(act, lap)

        @block.tensor
        def _(pe):
            pe.wait_ge(zeroed, ZEROED)

            def lap(n, s, i):
                pe.wait_ge(loaded[s], i * LOADS + LOADS)
                pe.wait_ge(V.sem, n * len(V.names))
                pe.wait_ge(A.sem, n * len(A.names))
                for q in qs:
                    for h in range(2):
                        out = bank[q][1][:, 0:2 * P].rearrange("p (f h n) -> p f h n", f=2, h=2)[:, :, h, :]
                        last = pe.matmul(out, bkb[s][:, q, h:h + 2, :].rearrange("p f n -> p (f n)"),
                                         ar[s][:, q, 0:2, h, :], start=True, stop=True)
                    M.done(last, f"g{q}")
                for q in qs:
                    tp = bank[q][0]
                    pe.transpose(tp[:, 0:P], ar[s][:, q, 0, :, :].rearrange("p h n -> p (h n)"), ident[:, :])
                    pe.transpose(tp[:, P:2 * P], v2[s][:, q, :, :].rearrange("p f n -> p (f n)"), ident[:, :])
                    pe.transpose(tp[:, 2 * P:3 * P], bkb[s][:, q, 0:2, :].rearrange("p f n -> p (f n)"), ident[:, :])
                    M.done(pe.transpose(tp[:, 3 * P:4 * P], bkb[s][:, q, 1:3, :].rearrange("p f n -> p (f n)"), ident[:, :]), f"tp{q}")
                for q in qs:
                    V.wait(pe, n, f"x1b{q}")
                    V.wait(pe, n, f"rl{q}")
                    M.done(pe.transpose(bank[q][1][:, 0:P], xt[:, q, :], ident[:, :]), f"x0{q}")
                for q in qs:
                    A.wait(pe, n, f"tbk{q}")
                    for h in range(2):
                        last = pe.matmul(bank[q][0][h * HD:(h + 1) * HD, 0:CH], nl[:, q, 1, h * CH:(h + 1) * CH],
                                         wuv[:, q, 1, h, :], start=True, stop=True)
                    M.done(last, f"lv{q}")
                for l in LEVELS:
                    for q in qs:
                        if l == LEVELS[0]:
                            A.wait(pe, n, f"x0{q}")
                            A.wait(pe, n, f"lv{q}")
                        M.done(pe.matmul(bank[q][0][:, 0:P], nl[:, q, 0, :], x[:, q, :], start=True, stop=True), f"n{l}{q}")
                    for q in qs:
                        V.wait(pe, n, f"z{l}{q}")
                        if l != LEVELS[0]:
                            A.wait(pe, n, f"t{l // 2}{q}")
                        M.done(pe.matmul(bank[q][1][:, 0:P], xt[:, q, :], z[:, q, :], start=True, stop=True), f"x{l}{q}")
                    for q in qs:
                        V.wait(pe, n, f"x{l}{q}")
                        M.done(pe.transpose(bank[q][1][:, 0:P], x[:, q, :], ident[:, :]), f"t{l}{q}")
                for q in qs:
                    A.wait(pe, n, f"t{LEVELS[-1]}{q}")
                    M.done(pe.matmul(bank[q][1][:, 0:P], xt[:, q, :], ak[:, q, :, :].rearrange("p f n -> p (f n)"),
                                     start=True, stop=True), f"wu{q}")
                for q in qs:
                    A.wait(pe, n, f"w1{q}")
                    M.done(pe.matmul(bank[q][0][:, 0:2 * P], wuv[:, q, 0, :, :].rearrange("p h n -> p (h n)"),
                                     rb[:, q, :, :, :].rearrange("p f h n -> p (f h n)"), start=True, stop=True), f"qm{q}")
                for q in qs:
                    V.wait(pe, n, f"qm1{q}")
                    for h in range(2):
                        s_out = bank[q][1][h * HD:(h + 1) * HD, 0:CH]
                        pe.matmul(s_out, rb[:, q, 1, h, :], wuv[:, q, 1, h, :], start=True, stop=False)
                        pe.matmul(s_out, qm[:, q, 1, h, :], state[:, q, :], start=False, stop=True)
                    for h in range(2):
                        y_out = bank[q][1][h * HD:(h + 1) * HD, CH:P]
                        pe.matmul(y_out, state[:, q, :], qm[:, q, 0, h, :], start=True, stop=False)
                        last = pe.matmul(y_out, wuv[:, q, 1, h, :], rb[:, q, 0, h, :], start=False, stop=True)
                    M.done(last, f"sy{q}")
            laps(pe, lap)

SB_CLAMP = 40.0
SBW = 512
GROUPS = SEQ // SBW


def sb_tasks():
    tasks = []
    for g in reversed(range(GROUPS)):
        top = (g + 1) * SBW // P
        for b in range(top, -1, -1):
            off = max(0, (b - 1) * P - g * SBW)
            for h in range(2):
                tasks.append((h, g, b, off, b > g * SBW // P))
    return tasks


def stage_stick_breaking(nc, p_dram, o_sb, ident):
    tasks = sb_tasks()
    N = len(tasks)
    diag_at = [n for n in range(N) if tasks[n][4]]
    ND = len(diag_at)
    last_of = {(h, g): n for n, (h, g, b, _, _) in enumerate(tasks) if b == 0}
    ends = sorted(last_of.values())
    with ExitStack() as ctx:
        m = Mem(nc, ctx, "sb")
        qz = m.sb("qz", [P, 2, SEQ])
        kt = m.sb("kt", [P, TPAD])
        vt = m.sb("vt", [P, TPAD])
        v = m.sb("v", [P, 9, P])
        tri = m.sb("tri", [P, P])
        rest = m.sb("rest", [P, P])
        z = [m.sb(f"z{i}", [P, SBW]) for i in range(4)]
        w = [m.sb(f"w{i}", [P, SBW]) for i in range(4)]
        a = [m.sb(f"a{i}", [P, SBW]) for i in range(3)]
        zb = [m.ps(f"zb{i}") for i in range(4)]
        cb = [m.ps(f"cb{h}") for h in range(2)]
        ob = [m.ps(f"ob{h}") for h in range(2)]
        loaded, init, tri_set = m.sem("loaded"), m.sem("init"), m.sem("tri_set")
        v_turned, v_copied = m.sem("v_turned"), m.sem("v_copied")
        z_done, z_copied, clamped = m.sem("z_done"), m.sem("z_copied"), m.sem("clamped")
        exp_done, ln_done, soft, soft_masked = m.sem("exp_done"), m.sem("ln_done"), m.sem("soft"), m.sem("soft_masked")
        tri_done, exponent, rest_done = m.sem("tri_done"), m.sem("exponent"), m.sem("rest_done")
        weights, weights_masked, pv_done, o_copied = m.sem("weights"), m.sem("weights_masked"), m.sem("pv_done"), m.sem("o_copied")
        block = ctx.enter_context(nc.Block())
        LOADS = 4 * 16

        def rows(n):
            return CH if tasks[n][2] == 0 else P

        def keys(b):
            return (0, CH) if b == 0 else (CH + (b - 1) * P, P)

        def ok(n):
            return 0 <= n < N

        @block.sync
        def _(sp):
            sp.wait_ge(init, 2)
            with sp.Fori(0, PAIRS) as i:
                sp.wait_ge(pv_done, i * N)
                for h in range(2):
                    half = slice(h * HD, (h + 1) * HD)
                    sp.dma_start(qz[half, h, :], p_dram[ds(i + T_SQ, 1)].squeeze(0)[half, CH:TPAD]).then_inc(loaded, 16)
                sp.dma_start(kt[:, PAD:], p_dram[ds(i + T_SK, 1)].squeeze(0)[:, PAD:TPAD]).then_inc(loaded, 16)
                sp.dma_start(vt[:, PAD:], p_dram[ds(i + T_SV, 1)].squeeze(0)[:, PAD:TPAD]).then_inc(loaded, 16)

        @block.gpsimd
        def _(pool):
            pool.wait_ge(init, 2)
            pool.affine_select(out=tri[:, :], in_=tri[:, :], compare_op=ALU.is_ge, fill=0.0, base=0,
                               pattern=[[-1, P]], channel_multiplier=1).then_inc(tri_set, 1)
            pool.affine_select(out=rest[:, :], in_=rest[:, :], compare_op=ALU.is_gt, fill=0.0, base=0,
                               pattern=[[1, P]], channel_multiplier=-1).then_inc(tri_set, 1)
            with pool.Fori(0, PAIRS) as i:
                def mask(tile, off, sem):
                    stand_alone(pool)
                    part = tile[:, off:off + P]
                    pool.affine_select(out=part, in_=part, compare_op=ALU.is_gt, fill=0.0, base=0,
                                       pattern=[[1, P]], channel_multiplier=-1).then_inc(sem, 1)
                for t in range(N + 6):
                    n = t - 4
                    if ok(n) and tasks[n][4]:
                        pool.wait_ge(weights, i * N + (n + 1))
                        mask(a[n % 3], tasks[n][3], weights_masked)
                    n = t - 2
                    if ok(n) and tasks[n][4]:
                        pool.wait_ge(soft, i * N + (n + 1))
                        mask(w[n % 4], tasks[n][3], soft_masked)

        @block.scalar
        def _(act):
            with act.Fori(0, PAIRS) as i:
                for j in range(3):
                    act.wait_ge(v_turned, i * 3 + (j + 1))
                    out, src = (v[:, 4 * j + 1:4 * j + 5, :], zb[j][:, :].rearrange("p (b n) -> p b n", n=P)) if j < 2 \
                        else (v[0:CH, 0, :], zb[j][0:CH, 0:P])
                    act.activation(out, src, ACT.Copy).then_inc(v_copied, 1)
                for t in range(N + 6):
                    n = t - 1
                    if ok(n):
                        r, off = rows(n), tasks[n][3]
                        act.wait_ge(z_done, i * N + (n + 1))
                        act.wait_ge(exponent, i * N + (n - 3) if n >= 4 else i * N)
                        act.activation(z[n % 4][0:r, off:], zb[n % 4][0:r, off:], ACT.Copy, scale=HD ** -0.5).then_inc(z_copied, 1)
                    n = t - 2
                    if ok(n):
                        r, off = rows(n), tasks[n][3]
                        s = w[n % 4][0:r, off:]
                        act.wait_ge(clamped, i * N + (n + 1))
                        act.activation(s, s, ACT.Exp).then_inc(exp_done, 1)
                        act.wait_ge(exp_done, i * N + (n + 1))
                        act.activation(s, s, ACT.Ln, bias=1.0).then_inc(ln_done, 1)
                    n = t - 4
                    if ok(n):
                        r, off = rows(n), tasks[n][3]
                        s = a[n % 3][0:r, off:]
                        act.wait_ge(exponent, i * N + (n + 1))
                        act.activation(s, s, ACT.Exp).then_inc(weights, 1)
                    n = t - 6
                    if n in ends:
                        h, g = tasks[n][0:2]
                        half = slice(h * HD, (h + 1) * HD)
                        act.wait_ge(pv_done, i * N + (n + 1))
                        act.activation(o_sb[half, ds(i, 1), g * SBW:(g + 1) * SBW].squeeze(1), ob[h][half, :],
                                       ACT.Copy).then_inc(o_copied, 1)

        @block.vector
        def _(dve):
            for tile in (qz[:, :, :], kt[:, 0:PAD], vt[:, 0:PAD]):
                dve.memset(tile, 0.0)
            dve.memset(tri[:, :], 1.0).then_inc(init, 1)
            dve.memset(rest[:, :], 1.0).then_inc(init, 1)
            with dve.Fori(0, PAIRS) as i:
                for t in range(N + 6):
                    n = t - 1
                    if ok(n):
                        r, off = rows(n), tasks[n][3]
                        dve.wait_ge(z_copied, i * N + (n + 1))
                        dve.wait_ge(rest_done, i * N + (n - 3) if n >= 4 else i * N)
                        dve.tensor_scalar(w[n % 4][0:r, off:], z[n % 4][0:r, off:], SB_CLAMP, None, ALU.min).then_inc(clamped, 1)
                    n = t - 2
                    if ok(n):
                        r, off = rows(n), tasks[n][3]
                        s = w[n % 4][0:r, off:]
                        dve.wait_ge(ln_done, i * N + (n + 1))
                        dve.tensor_tensor(s, z[n % 4][0:r, off:], s, ALU.max).then_inc(soft, 1)
                    n = t - 3
                    if ok(n):
                        h, g, b, off, _ = tasks[n]
                        r = rows(n)
                        dve.wait_ge(tri_done, i * N + (n + 1))
                        dve.wait_ge(pv_done, i * N + (n - 2) if n >= 3 else i * N)
                        dve.tensor_tensor(a[n % 3][0:r, off:], z[n % 4][0:r, off:], cb[h][0:r, off:], ALU.subtract).then_inc(exponent, 1)

        @block.tensor
        def _(pe):
            pe.wait_ge(tri_set, 2)
            with pe.Fori(0, PAIRS) as i:
                pe.wait_ge(loaded, i * LOADS + LOADS)
                pe.wait_ge(z_copied, i * N)
                for j in range(9):
                    c, r = keys((j + 1) % 9)
                    last = pe.transpose(zb[j // 4][0:r, (j % 4) * P:(j % 4 + 1) * P], vt[:, c:c + r], ident[:, :])
                    if j % 4 == 3 or j == 8:
                        last.then_inc(v_turned, 1)
                for t in range(N + 6):
                    n = t
                    if ok(n):
                        h, g, b, off, _ = tasks[n]
                        c, r = keys(b)
                        if n < 4:
                            pe.wait_ge(v_copied, i * 3 + 3)
                        else:
                            pe.wait_ge(z_copied, i * N + (n - 3))
                        pe.matmul(zb[n % 4][0:r, off:], kt[:, c:c + r], qz[:, h, g * SBW + off:(g + 1) * SBW],
                                  start=True, stop=True).then_inc(z_done, 1)
                    n = t - 4
                    if ok(n):
                        h, g, b, off, diag = tasks[n]
                        r = rows(n)
                        pe.wait_ge(exponent, i * N + (n + 1))
                        if b:
                            pe.matmul(cb[h][:, off:], rest[0:r, :], w[n % 4][0:r, off:], start=False, stop=True,
                                      skip_group_check=True).then_inc(rest_done, 1)
                        else:
                            pe.sem_inc(rest_done, 1)
                    n = t - 3
                    if ok(n):
                        h, g, b, off, diag = tasks[n]
                        r = rows(n)
                        top = (g + 1) * SBW // P
                        if diag:
                            pe.wait_ge(soft_masked, i * ND + (diag_at.index(n) + 1))
                        else:
                            pe.wait_ge(soft, i * N + (n + 1))
                        if r == CH:
                            stand_alone(pe)
                        pe.matmul(cb[h][0:r, off:], tri[0:r, 0:r], w[n % 4][0:r, off:], start=(b == top), stop=True,
                                  skip_group_check=True).then_inc(tri_done, 1)
                    n = t - 5
                    if ok(n):
                        h, g, b, off, diag = tasks[n]
                        r = rows(n)
                        top = (g + 1) * SBW // P
                        if diag:
                            pe.wait_ge(weights_masked, i * ND + (diag_at.index(n) + 1))
                        else:
                            pe.wait_ge(weights, i * N + (n + 1))
                        if b == top:
                            before = [e for e in ends if tasks[e][0] == h and e < n]
                            pe.wait_ge(o_copied, i * len(ends) + (ends.index(before[-1]) + 1 if before else 0))
                        if r == CH:
                            stand_alone(pe)
                        half = slice(h * HD, (h + 1) * HD)
                        pe.matmul(ob[h][half, off:], v[0:r, b, h * HD:(h + 1) * HD], a[n % 3][0:r, off:],
                                  start=(b == top), stop=(b == 0), skip_group_check=True).then_inc(pv_done, 1)

V_LG, V_LB, V_SG = 0, 1, 2


def stage_post_heads(nc, y_sb, o_sb, vecs, gate_dram, bonus_dram, ones_bd):
    with ExitStack() as ctx:
        m = Mem(nc, ctx, "post")
        vec = m.sb("vec", [P, PAIRS, 3])
        gate = [m.sb(f"gate{s}", [P, SEQ]) for s in range(2)]
        bonus = [m.sb(f"bonus{s}", [P, SEQ]) for s in range(2)]
        dev = m.sb("dev", [P, SEQ])
        sq = m.sb("sq", [P, SEQ])
        root = m.sb("root", [P, SEQ])
        osq = m.sb("osq", [P, SEQ])
        oroot = m.sb("oroot", [P, SEQ])
        eps = m.sb("eps", [P, 2])
        bank = [m.ps(f"bank{b}") for b in range(6)]
        loaded = [m.sem(f"loaded{s}") for s in range(2)]
        vec_loaded, init = m.sem("vec_loaded"), m.sem("init")
        V = Steps(m.sem("vec_done"), "d0 d1 rinv n gb b g orinv o")
        A = Steps(m.sem("act_done"), "sq osq r0 r1 or0 or1")
        M = Steps(m.sem("mm_done"), "m0 m1 o0 o1 v0 v1")
        block = ctx.enter_context(nc.Block())
        halves = [(0, 512), (512, 512)]

        @block.sync
        def _(sp):
            sp.dma_start(vec[:, :, :], vecs).then_inc(vec_loaded, 16)
            for q in range(PAIRS):
                if q >= 2:
                    V.wait(sp, q - 2, "o")
                sp.dma_start(gate[q % 2][:, :], gate_dram[q]).then_inc(loaded[q % 2], 16)
                sp.dma_start(bonus[q % 2][:, :], bonus_dram[q]).then_inc(loaded[q % 2], 16)

        @block.scalar
        def _(act):
            act.wait_ge(init, 2)
            for q in range(PAIRS):
                V.wait(act, q, "d1")
                A.done(act.activation(sq[:, :], dev[:, :], ACT.Square), "sq")
                A.done(act.activation(osq[:, :], o_sb[:, q, :], ACT.Square), "osq")
                for g, (c, n) in enumerate(halves):
                    M.wait(act, q, f"v{g}")
                    A.done(act.activation(root[:, c:c + n], bank[2 + g][:, :], ACT.Sqrt, scale=1.0 / HD, bias=eps[:, 0:1]), f"r{g}")
                for g, (c, n) in enumerate(halves):
                    M.wait(act, q, f"o{g}")
                    A.done(act.activation(oroot[:, c:c + n], bank[4 + g][:, :], ACT.Sqrt, scale=1.0 / HD, bias=eps[:, 1:2]), f"or{g}")

        @block.vector
        def _(dve):
            dve.memset(eps[:, 0:1], GN_EPS).then_inc(init, 1)
            dve.memset(eps[:, 1:2], RMS_EPS).then_inc(init, 1)
            dve.wait_ge(vec_loaded, 16)
            for q in range(PAIRS):
                y = y_sb[:, q, CH:TPAD]
                for g, (c, n) in enumerate(halves):
                    M.wait(dve, q, f"m{g}")
                    V.done(dve.scalar_tensor_tensor(dev[:, c:c + n], bank[g][:, :], -1.0 / HD, y[:, c:c + n], ALU.mult, ALU.add), f"d{g}")
                A.wait(dve, q, "r1")
                V.done(dve.reciprocal(root[:, :], root[:, :]), "rinv")
                V.wait(dve, q, "rinv")
                V.done(dve.tensor_tensor(dev[:, :], dev[:, :], root[:, :], ALU.mult), "n")
                V.wait(dve, q, "n")
                V.done(dve.tensor_scalar(dev[:, :], dev[:, :], vec[:, q, V_LG:V_LG + 1], vec[:, q, V_LB:V_LB + 1], ALU.mult, ALU.add), "gb")
                V.wait(dve, q, "gb")
                dve.wait_ge(loaded[q % 2], 32 * (q // 2 + 1))
                V.done(dve.tensor_tensor(dev[:, :], dev[:, :], bonus[q % 2][:, :], ALU.add), "b")
                V.wait(dve, q, "b")
                V.done(dve.tensor_tensor(y, dev[:, :], gate[q % 2][:, :], ALU.mult), "g")
                A.wait(dve, q, "or1")
                V.done(dve.reciprocal(oroot[:, :], oroot[:, :]), "orinv")
                V.wait(dve, q, "orinv")
                V.done(dve.scalar_tensor_tensor(o_sb[:, q, :], o_sb[:, q, :], vec[:, q, V_SG:V_SG + 1], oroot[:, :], ALU.mult, ALU.mult), "o")

        @block.tensor
        def _(pe):
            for q in range(PAIRS):
                if q:
                    pe.wait_ge(V.sem, q * len(V.names))
                    pe.wait_ge(A.sem, q * len(A.names))
                for g, (c, n) in enumerate(halves):
                    M.done(pe.matmul(bank[g][:, :], ones_bd[:, :], y_sb[:, q, CH + c:CH + c + n], start=True, stop=True), f"m{g}")
                A.wait(pe, q, "osq")
                for g, (c, n) in enumerate(halves):
                    M.done(pe.matmul(bank[4 + g][:, :], ones_bd[:, :], osq[:, c:c + n], start=True, stop=True), f"o{g}")
                for g, (c, n) in enumerate(halves):
                    M.done(pe.matmul(bank[2 + g][:, :], ones_bd[:, :], sq[:, c:c + n], start=True, stop=True), f"v{g}")


def stage_out_proj(nc, y_sb, o_sb, w_out, x_dram, gain_row, h_dram):
    with ExitStack() as ctx:
        m = Mem(nc, ctx, "oproj")
        raw = [m.sb(f"raw{s}", [P, D]) for s in range(2)]
        wh = m.sb("wh", [P, KD, D], F32R)
        wl = m.sb("wl", [P, KD, D], F32R)
        yh = [m.sb(f"yh{s}", [P, KD, P], F32R) for s in range(2)]
        yl = [m.sb(f"yl{s}", [P, KD, P], F32R) for s in range(2)]
        x = [m.sb(f"x{s}", [P, D]) for s in range(2)]
        h = [m.sb(f"h{s}", [P, D]) for s in range(2)]
        square = m.sb("square", [P, D])
        gain = m.sb("gain", [P, D])
        ss = [m.sb(f"ss{s}", [P, 2]) for s in range(2)]
        root = [m.sb(f"root{s}", [P, 1]) for s in range(2)]
        eps = m.sb("eps", [P, 1])
        acc = [[m.ps(f"acc{s}{g}") for g in range(2)] for s in range(2)]
        w_loaded = [m.sem(f"w_loaded{s}") for s in range(2)]
        x_loaded = [m.sem(f"x_loaded{s}") for s in range(2)]
        gain_loaded, init, stored = m.sem("gain_loaded"), m.sem("init"), m.sem("stored")
        w_high, w_low, y_low = m.sem("w_high"), m.sem("w_low"), m.sem("y_low")
        V = Steps(m.sem("vec_done"), "add rinv n0 n1 h")
        A = Steps(m.sem("act_done"), "yh0 yh1 s0 s1 root")
        mm_done = m.sem("mm_done")
        block = ctx.enter_context(nc.Block())

        @block.sync
        def _(sp):
            sp.dma_start(gain[:, :], gain_row.broadcast_to((P, D))).then_inc(gain_loaded, 16)
            for k in range(KD):
                if k >= 2:
                    sp.wait_ge(w_low, k - 1)
                sp.dma_start(raw[k % 2][:, :], w_out[k]).then_inc(w_loaded[k % 2], 16)
            with sp.Fori(0, TOK_TILES // 2) as i:
                for s in range(2):
                    sp.wait_ge(V.sem, i * (2 * len(V.names)))
                    sp.dma_start(x[s][:, :], x_dram[ds(i * 2 * P + s * P, P), :]).then_inc(x_loaded[s], 16)
                for s in range(2):
                    V.wait(sp, i * 2 + s, "h")
                    sp.dma_start(h_dram[ds(i * 2 * P + s * P, P), :], h[s][:, :]).then_inc(stored, 16)
            sp.wait_ge(stored, 16 * TOK_TILES)

        @block.scalar
        def _(act):
            for k in range(KD):
                act.wait_ge(w_loaded[k % 2], 16 * (k // 2 + 1))
                act.activation(wh[:, k, :], raw[k % 2][:, :], ACT.Copy).then_inc(w_high, 1)
            act.wait_ge(init, 1)
            with act.Fori(0, TOK_TILES // 2) as i:
                for s in range(2):
                    n = i * 2 + s
                    act.wait_ge(mm_done, i * 2)
                    cols = ds(i * 2 * P + s * P, P)
                    A.done(act.activation(yh[s][:, 0:4, :], y_sb[:, :, ds(i * 2 * P + (s * P + CH), P)], ACT.Copy), "yh0")
                    A.done(act.activation(yh[s][:, 4:8, :], o_sb[:, :, cols], ACT.Copy), "yh1")
                    act.wait_ge(mm_done, n + 1)
                    for g in range(2):
                        A.done(act.activation(square[:, g * 512:g * 512 + 512], acc[s][g][:, :], ACT.Square,
                                              accum_out=ss[s][:, g:g + 1]), f"s{g}")
                    V.wait(act, n, "add")
                    A.done(act.activation(root[s][:, :], ss[s][:, 0:1], ACT.Sqrt, scale=1.0 / D, bias=eps[:, :]), "root")

        @block.vector
        def _(dve):
            dve.memset(eps[:, :], RMS_EPS).then_inc(init, 1)
            for k in range(KD):
                dve.wait_ge(w_high, k + 1)
                dve.tensor_tensor(wl[:, k, :], raw[k % 2][:, :], wh[:, k, :].bitcast(F32), ALU.subtract).then_inc(w_low, 1)
            dve.wait_ge(gain_loaded, 16)
            with dve.Fori(0, TOK_TILES // 2) as i:
                for s in range(2):
                    n = i * 2 + s
                    A.wait(dve, n, "s1")
                    V.done(dve.tensor_tensor(ss[s][:, 0:1], ss[s][:, 0:1], ss[s][:, 1:2], ALU.add), "add")
                    A.wait(dve, n, "root")
                    V.done(dve.reciprocal(root[s][:, :], root[s][:, :]), "rinv")
                    V.wait(dve, n, "rinv")
                    dve.wait_ge(stored, i * 32)
                    for g in range(2):
                        c = slice(g * 512, g * 512 + 512)
                        V.done(dve.scalar_tensor_tensor(h[s][:, c], acc[s][g][:, :], root[s][:, :], gain[:, c], ALU.mult, ALU.mult), f"n{g}")
                    V.wait(dve, n, "n1")
                    dve.wait_ge(x_loaded[s], i * 16 + 16)
                    V.done(dve.tensor_tensor(h[s][:, :], h[s][:, :], x[s][:, :], ALU.add), "h")

        @block.gpsimd
        def _(pool):
            with pool.Fori(0, TOK_TILES // 2) as i:
                for s in range(2):
                    A.wait(pool, i * 2 + s, "yh1")
                    pool.tensor_tensor(yl[s][:, 0:4, :], y_sb[:, :, ds(i * 2 * P + (s * P + CH), P)],
                                       yh[s][:, 0:4, :].bitcast(F32), ALU.subtract).then_inc(y_low, 1)
                    pool.tensor_tensor(yl[s][:, 4:8, :], o_sb[:, :, ds(i * 2 * P + s * P, P)],
                                       yh[s][:, 4:8, :].bitcast(F32), ALU.subtract).then_inc(y_low, 1)

        @block.tensor
        def _(pe):
            pe.wait_ge(w_low, KD)
            with pe.Fori(0, TOK_TILES // 2) as i:
                for s in range(2):
                    pe.wait_ge(y_low, i * 4 + 2 * (s + 1))
                    pe.wait_ge(V.sem, i * (2 * len(V.names)))
                    for g in range(2):
                        c = slice(g * 512, g * 512 + 512)
                        for k in range(KD):
                            for j, (yy, w) in enumerate([(yh, wh), (yh, wl), (yl, wh)]):
                                last = pe.matmul(acc[s][g][:, :], yy[s][:, k, :], w[:, k, c],
                                                 start=(k == 0 and j == 0), stop=(k == KD - 1 and j == 2))
                    last.then_inc(mm_done, 1)


FC = 2
FF_CHUNKS = FF_TILES // FC


def stage_ffn(nc, mh, ml, w_up, w_down, acc):
    with ExitStack() as ctx:
        m = Mem(nc, ctx, "ffn")
        raw_u = [m.sb(f"raw_u{s}", [P, KD, P]) for s in range(2)]
        raw_d = [m.sb(f"raw_d{s}", [P, D]) for s in range(2)]
        wuh = [m.sb(f"wuh{s}", [P, KD, P], F32R) for s in range(2)]
        wul = [m.sb(f"wul{s}", [P, KD, P], F32R) for s in range(2)]
        wdh = [m.sb(f"wdh{s}", [P, FC, D], F32R) for s in range(2)]
        wdl = [m.sb(f"wdl{s}", [P, FC, D], F32R) for s in range(2)]
        uh = [m.sb(f"uh{s}", [P, FC, SEQ], F32R) for s in range(2)]
        ul = [m.sb(f"ul{s}", [P, FC, SEQ], F32R) for s in range(2)]
        relu = [m.sb(f"relu{s}", [P, 512]) for s in range(2)]
        ups = [m.ps(f"up{b}") for b in range(4)]
        downs = [m.ps(f"down{b}") for b in range(4)]
        u_loaded = [m.sem(f"u_loaded{s}") for s in range(2)]
        d_loaded = [m.sem(f"d_loaded{s}") for s in range(2)]
        zeroed = m.sem("zeroed")
        wu_high, wu_low, wd_high, wd_low = m.sem("wu_high"), m.sem("wu_low"), m.sem("wd_high"), m.sem("wd_low")
        up_done, relu_done, squared, u_high, u_low = (m.sem(x) for x in ("up_done", "relu_done", "squared", "u_high", "u_low"))
        down_done, added = m.sem("down_done"), m.sem("added")
        block = ctx.enter_context(nc.Block())
        HALVES = 2 * FC
        OUTS = TOK_TILES * 2

        def first(c):
            return isinstance(c, int) and c == 0

        def chunks(eng, up, down):
            up(0, 0)
            up(1, 1)
            down(0, 0)
            with eng.Fori(0, FF_CHUNKS // 2 - 1) as i:
                up(i * 2 + 2, 0)
                down(i * 2 + 1, 1)
                up(i * 2 + 3, 1)
                down(i * 2 + 2, 0)
            down(FF_CHUNKS - 1, 1)

        @block.sync
        def _(sp):
            with sp.Fori(0, FF_TILES // 2) as i:
                for s in range(2):
                    sp.wait_ge(wu_low, i * 2)
                    sp.dma_start(raw_u[s][:, :, :], w_up[ds(i * 2 + s, 1)].squeeze(0)).then_inc(u_loaded[s], 16)
                    sp.wait_ge(wd_low, i * 2)
                    sp.dma_start(raw_d[s][:, :], w_down[ds(i * 2 + s, 1)].squeeze(0)).then_inc(d_loaded[s], 16)

        @block.scalar
        def _(act):
            def up(c, s):
                for f in range(FC):
                    act.wait_ge(u_loaded[f], c * 16 + 16)
                    if not first(c):
                        act.wait_ge(up_done, c * HALVES + (2 * f - 2))
                    act.activation(wuh[f][:, :, :], raw_u[f][:, :, :], ACT.Copy).then_inc(wu_high, 1)
                    act.wait_ge(d_loaded[f], c * 16 + 16)
                    if not first(c):
                        act.wait_ge(down_done, (c - 1) * OUTS)
                    act.activation(wdh[s][:, f, :], raw_d[f][:, :], ACT.Copy).then_inc(wd_high, 1)
                for j in range(HALVES):
                    f, half = divmod(j, 2)
                    cols = slice(half * 512, half * 512 + 512)
                    act.wait_ge(up_done, c * HALVES + (j + 1))
                    if not (first(c) and j < 2):
                        act.wait_ge(u_low, c * HALVES + (j - 1))
                    act.activation(relu[j % 2][:, :], ups[j][:, :], ACT.Relu).then_inc(relu_done, 1)
                    act.wait_ge(squared, c * HALVES + (j + 1))
                    act.activation(uh[s][:, f, cols], relu[j % 2][:, :], ACT.Copy).then_inc(u_high, 1)
            chunks(act, up, lambda c, s: None)

        @block.gpsimd
        def _(pool):
            pool.memset(acc[:, :, :], 0.0).then_inc(zeroed, 1)

            def up(c, s):
                for j in range(HALVES):
                    f, half = divmod(j, 2)
                    cols = slice(half * 512, half * 512 + 512)
                    pool.wait_ge(u_high, c * HALVES + (j + 1))
                    pool.tensor_tensor(ul[s][:, f, cols], relu[j % 2][:, :], uh[s][:, f, cols].bitcast(F32),
                                       ALU.subtract).then_inc(u_low, 1)
            chunks(pool, up, lambda c, s: None)

        @block.vector
        def _(dve):
            dve.wait_ge(zeroed, 1)

            def up(c, s):
                for f in range(FC):
                    dve.wait_ge(wu_high, c * FC + (f + 1))
                    dve.tensor_tensor(wul[f][:, :, :], raw_u[f][:, :, :], wuh[f][:, :, :].bitcast(F32), ALU.subtract).then_inc(wu_low, 1)
                    dve.wait_ge(wd_high, c * FC + (f + 1))
                    dve.tensor_tensor(wdl[s][:, f, :], raw_d[f][:, :], wdh[s][:, f, :].bitcast(F32), ALU.subtract).then_inc(wd_low, 1)
                for j in range(HALVES):
                    dve.wait_ge(relu_done, c * HALVES + (j + 1))
                    dve.tensor_tensor(relu[j % 2][:, :], relu[j % 2][:, :], relu[j % 2][:, :], ALU.mult).then_inc(squared, 1)

            def down(c, s):
                for t in range(TOK_TILES):
                    for g in range(2):
                        o = 2 * t + g
                        sl = acc[:, t, g * 512:g * 512 + 512]
                        dve.wait_ge(down_done, c * OUTS + (o + 1))
                        dve.wait_ge(added, c * OUTS)
                        dve.tensor_tensor(sl, sl, downs[o % 4][:, :], ALU.add).then_inc(added, 1)
            chunks(dve, up, down)

        @block.tensor
        def _(pe):
            def up(c, s):
                for j in range(HALVES):
                    f, half = divmod(j, 2)
                    pe.wait_ge(wu_low, c * FC + (f + 1))
                    if not first(c):
                        pe.wait_ge(relu_done, (c - 1) * HALVES + (j + 1))
                    cols = slice(half * 512, half * 512 + 512)
                    for k in range(KD):
                        for jj, (w, xx) in enumerate([(wuh, mh), (wuh, ml), (wul, mh)]):
                            last = pe.matmul(ups[j][:, :], w[f][:, k, :], xx[:, k, cols],
                                             start=(k == 0 and jj == 0), stop=(k == KD - 1 and jj == 2))
                    last.then_inc(up_done, 1)

            def down(c, s):
                pe.wait_ge(wd_low, c * FC + FC)
                pe.wait_ge(u_low, c * HALVES + HALVES)
                for t in range(TOK_TILES):
                    for g in range(2):
                        o = 2 * t + g
                        if not (first(c) and o < 4):
                            pe.wait_ge(added, c * OUTS + (o - 3))
                        for f in range(FC):
                            for jj, (u, w) in enumerate([(uh, wdh), (uh, wdl), (ul, wdh)]):
                                last = pe.matmul(downs[o % 4][:, :], u[s][:, f, t * P:(t + 1) * P],
                                                 w[s][:, f, g * 512:g * 512 + 512],
                                                 start=(f == 0 and jj == 0), stop=(f == FC - 1 and jj == 2))
                        last.then_inc(down_done, 1)
            chunks(pe, up, down)


def stage_finish(nc, acc, h_dram, gain_row, out_dram):
    with ExitStack() as ctx:
        m = Mem(nc, ctx, "fin")
        gain = m.sb("gain", [P, D])
        square = m.sb("square", [P, D])
        h = [m.sb(f"h{s}", [P, D]) for s in range(2)]
        o = [m.sb(f"o{s}", [P, D]) for s in range(2)]
        ss = m.sb("ss", [P, TOK_TILES])
        root = m.sb("root", [P, TOK_TILES])
        eps = m.sb("eps", [P, 1])
        loaded = [m.sem(f"loaded{s}") for s in range(2)]
        stored = [m.sem(f"stored{s}") for s in range(2)]
        gain_loaded, init, squared, rooted, inverted, normed, added = (m.sem(x) for x in (
            "gain_loaded", "init", "squared", "rooted", "inverted", "normed", "added"))
        block = ctx.enter_context(nc.Block())

        @block.sync
        def _(sp):
            sp.dma_start(gain[:, :], gain_row.broadcast_to((P, D))).then_inc(gain_loaded, 16)
            for s in range(2):
                sp.dma_start(h[s][:, :], h_dram[s * P:(s + 1) * P, :]).then_inc(loaded[s], 16)
            for t in range(TOK_TILES):
                sp.wait_ge(added, t + 1)
                sp.dma_start(out_dram[t * P:(t + 1) * P, :], o[t % 2][:, :]).then_inc(stored[t % 2], 16)
                if t + 2 < TOK_TILES:
                    sp.dma_start(h[t % 2][:, :], h_dram[(t + 2) * P:(t + 3) * P, :]).then_inc(loaded[t % 2], 16)
            for s in range(2):
                sp.wait_ge(stored[s], 16 * (TOK_TILES // 2))

        @block.scalar
        def _(act):
            act.wait_ge(init, 1)
            for t in range(TOK_TILES):
                act.activation(square[:, :], acc[:, t, :], ACT.Square, accum_out=ss[:, t:t + 1]).then_inc(squared, 1)
                act.wait_ge(squared, t + 1)
                act.activation(root[:, t:t + 1], ss[:, t:t + 1], ACT.Sqrt, scale=1.0 / D, bias=eps[:, :]).then_inc(rooted, 1)

        @block.vector
        def _(dve):
            dve.memset(eps[:, :], RMS_EPS).then_inc(init, 1)
            dve.wait_ge(gain_loaded, 16)
            for t in range(TOK_TILES):
                dve.wait_ge(rooted, t + 1)
                dve.reciprocal(root[:, t:t + 1], root[:, t:t + 1]).then_inc(inverted, 1)
                dve.wait_ge(inverted, t + 1)
                if t >= 2:
                    dve.wait_ge(stored[t % 2], 16 * (t // 2))
                dve.scalar_tensor_tensor(o[t % 2][:, :], acc[:, t, :], root[:, t:t + 1], gain[:, :], ALU.mult, ALU.mult).then_inc(normed, 1)
                dve.wait_ge(normed, t + 1)
                dve.wait_ge(loaded[t % 2], 16 * (t // 2 + 1))
                dve.tensor_tensor(o[t % 2][:, :], o[t % 2][:, :], h[t % 2][:, :], ALU.add).then_inc(added, 1)


def build(nc, x, meta, w_in, w_out, w_up, w_down, g_pre_mix, g_pre_ffn, g_post_mix, g_post_ffn,
          rwkv_vecs, mu_low, head_vecs, w_decay_up, w_a_up, w_g_up, out):
    p_dram = nc.dram_tensor("p_scratch", [IN_TILES, P, TPAD], F32, kind="Internal").ap()
    chunk_dram = nc.dram_tensor("chunk_scratch", [PAIRS, CHUNKS, P, 5 * CH], F32, kind="Internal").ap()
    gate_dram = nc.dram_tensor("gate_scratch", [PAIRS, P, SEQ], F32, kind="Internal").ap()
    bonus_dram = nc.dram_tensor("bonus_scratch", [PAIRS, P, SEQ], F32, kind="Internal").ap()
    h_dram = nc.dram_tensor("h_scratch", [SEQ, D], F32, kind="Internal").ap()
    with ExitStack() as whole:
        g = Mem(nc, whole, "all")
        ident = g.sb("ident", [P, P])
        with ExitStack() as heads:
            hm = Mem(nc, heads, "heads")
            ones_bd = hm.sb("ones_bd", [P, P])
            pc = hm.sb("pc", [P, PAIRS, CHUNKS])
            stage_constants(nc, ident, ones_bd)
            with ExitStack() as c:
                m = Mem(nc, c, "xn")
                xh, xl = m.sb("xh", [P, KD, T], F32R), m.sb("xl", [P, KD, T], F32R)
                stage_norm_transpose(nc, "pre", lambda row: x[ds(row, P), :], meta, g_pre_mix, ident, xh, xl)
                stage_in_proj(nc, w_in, p_dram, xh, xl)
            stage_rwkv_prep(nc, p_dram, rwkv_vecs, mu_low, w_decay_up, w_a_up, w_g_up, chunk_dram, gate_dram,
                            bonus_dram, pc, ones_bd)
            with ExitStack() as c:
                m = Mem(nc, c, "mixed")
                y_sb, o_sb = m.sb("y", [P, PAIRS, TPAD]), m.sb("o", [P, PAIRS, SEQ])
                stage_stick_breaking(nc, p_dram, o_sb, ident)
                with ExitStack() as c2:
                    masks = Mem(nc, c2, "scanm").sb("masks", [P, N_MASKS, P])
                    stage_rwkv_masks(nc, masks)
                    stage_rwkv_scan(nc, chunk_dram, masks, ident, pc, y_sb)
                stage_post_heads(nc, y_sb, o_sb, head_vecs, gate_dram, bonus_dram, ones_bd)
                stage_out_proj(nc, y_sb, o_sb, w_out, x, g_post_mix, h_dram)
        acc = g.sb("acc", [P, TOK_TILES, D])
        with ExitStack() as c:
            m = Mem(nc, c, "mn")
            mh, ml = m.sb("mh", [P, KD, SEQ], F32R), m.sb("ml", [P, KD, SEQ], F32R)
            stage_norm_transpose(nc, "preffn", lambda row: h_dram[ds(row, P), :], None, g_pre_ffn, ident, mh, ml)
            stage_ffn(nc, mh, ml, w_up, w_down, acc)
        stage_finish(nc, acc, h_dram, g_post_ffn, out)


def kernel(**inputs):
    import numpy as np
    import concourse.bacc as bacc
    from concourse.bass_utils import run_bass_kernel_spmd

    get = lambda name: np.asarray(inputs[name])
    by_tile = lambda a: np.ascontiguousarray(a.reshape(-1, P).T)
    by_pair = lambda *vs: np.ascontiguousarray(np.stack([v.reshape(PAIRS, P) for v in vs], axis=-1))
    mu = get("tshift_mu")[0]
    arrays = {
        "x": get("x")[0], "meta": get("meta_tokens"),
        "w_in": get("w_in")[0].reshape(KD, P, IN_TILES, P).transpose(2, 1, 0, 3),
        "w_out": get("w_out")[0].reshape(KD, P, D),
        "w_up": get("w_ffn_up")[0].reshape(KD, P, FF_TILES, P).transpose(2, 1, 0, 3),
        "w_down": get("w_ffn_down")[0].reshape(FF_TILES, P, D),
        "g_pre_mix": by_tile(get("g_pre_mix")[0]), "g_pre_ffn": by_tile(get("g_pre_ffn")[0]),
        "g_post_mix": get("g_post_mix"), "g_post_ffn": get("g_post_ffn"),
        "rwkv_vecs": by_pair(mu[0:RW], mu[RW:2 * RW], mu[2 * RW:3 * RW], get("decay_bias")[0], get("a_bias")[0],
                             get("k_k")[0], get("k_a")[0], get("r_k")[0].reshape(-1)),
        "mu_low": by_tile(mu[3 * RW:]),
        "head_vecs": by_pair(get("lnx_gain")[0], get("lnx_bias")[0], get("sb_out_gain")[0]).transpose(1, 0, 2),
        "w_decay_up": get("w_decay_up")[0], "w_a_up": get("w_a_up")[0], "w_g_up": get("w_g_up")[0],
    }
    arrays = {name: np.ascontiguousarray(a) for name, a in arrays.items()}
    nc = bacc.Bacc("TRN2", target_bir_lowering=False, num_devices=1)
    args = {name: nc.dram_tensor(f"in_{name}", a.shape, mybir.dt.from_np(a.dtype), kind="ExternalInput").ap()
            for name, a in arrays.items()}
    args["out"] = nc.dram_tensor("out", (SEQ, D), F32, kind="ExternalOutput").ap()
    build(nc, **args)
    r = run_bass_kernel_spmd(nc, [{f"in_{name}": a for name, a in arrays.items()}], core_ids=[0])
    return r.results[0]["out"].reshape(1, SEQ, D)
```

```python
import concourse.bass as bass
from concourse import mybir
from contextlib import ExitStack

F32 = mybir.dt.float32
F32R = mybir.dt.float32r
ALU = mybir.AluOpType
ACT = mybir.ActivationFunctionType
ds = bass.ds

P = 128
D = 1024
KD = D // P
META = 16
SEQ = 1024
T = META + SEQ
HD = 64
RW = 512
PAIRS = RW // P
CH = 64
TPAD = 1088
PAD = TPAD - T
CHUNKS = TPAD // CH
IN_TILES = 26
T_R, T_K, T_V, T_DA, T_G, T_SQ, T_SK, T_SV = 0, 4, 8, 12, 13, 14, 18, 22
FF = 4 * D
FF_TILES = FF // P
TOK_TILES = SEQ // P
RMS_EPS = 1e-6
GN_EPS = 1e-5 * HD
TOK_GROUPS = [(0, 348), (348, 346), (694, 346)]


class Mem:

    def __init__(self, nc, ctx, stage):
        self.nc, self.ctx, self.stage = nc, ctx, stage

    def sb(self, name, shape, dt=F32, side="left"):
        return self.ctx.enter_context(self.nc.sbuf_tensor(f"{self.stage}_{name}", shape, dt, side=side))

    def ps(self, name, shape=(P, 512)):
        return self.ctx.enter_context(self.nc.psum_tensor(f"{self.stage}_{name}", list(shape), F32))

    def sem(self, name):
        return self.ctx.enter_context(self.nc.semaphore(f"{self.stage}_{name}"))


def stage_constants(nc, ident, ones_bd):
    with ExitStack() as ctx:
        m = Mem(nc, ctx, "const")
        filled, zeroed, done = m.sem("filled"), m.sem("zeroed"), m.sem("done")
        block = ctx.enter_context(nc.Block())

        @block.gpsimd
        def _(pool):
            pool.memset(ident[:, :], 0.0).then_inc(filled, 1)
            pool.wait_ge(filled, 1)
            pool.affine_select(out=ident[:, :], in_=ident[:, :], compare_op=ALU.not_equal, fill=1.0,
                               base=0, pattern=[[-1, P]], channel_multiplier=1).then_inc(done, 1)

        @block.vector
        def _(dve):
            dve.memset(ones_bd[:, :], 0.0).then_inc(zeroed, 1)
            dve.wait_ge(zeroed, 1)
            for h in range(2):
                half = ones_bd[h * HD:(h + 1) * HD, h * HD:(h + 1) * HD]
                dve.memset(half, 1.0).then_inc(done, 1)
            dve.wait_ge(done, 3)


def stage_norm_transpose(nc, name, rows_of, rows0, gain_cols, ident, xh, xl):
    first = rows0.shape[0] if rows0 is not None else 0
    lead = 1 if first else 0
    with ExitStack() as ctx:
        m = Mem(nc, ctx, name)
        x = [m.sb(f"x{s}", [P, D]) for s in range(2)]
        xs = [m.sb(f"xs{s}", [P, D]) for s in range(2)]
        xf = [m.sb(f"xf{s}", [P, KD, P]) for s in range(2)]
        square = m.sb("square", [P, D])
        sumsq = [m.sb(f"sumsq{s}", [P, 1]) for s in range(2)]
        root = [m.sb(f"root{s}", [P, 1]) for s in range(2)]
        rinv = [m.sb(f"rinv{s}", [P, 1]) for s in range(2)]
        gain = m.sb("gain", [P, KD])
        eps = m.sb("eps", [P, 1])
        tp = [[m.ps(f"tp{s}{b}") for b in range(2)] for s in range(2)]
        loaded = [m.sem(f"loaded{s}") for s in range(2)]
        gain_loaded, eps_set = m.sem("gain_loaded"), m.sem("eps_set")
        x_free = m.sem("x_free")
        squared, rooted, inverted, scaled = m.sem("squared"), m.sem("rooted"), m.sem("inverted"), m.sem("scaled")
        turned, gained, high, low = m.sem("turned"), m.sem("gained"), m.sem("high"), m.sem("low")
        block = ctx.enter_context(nc.Block())

        def each(eng, step):
            if lead:
                step(0, 0, 0, first, 0)
            with eng.Fori(0, TOK_TILES // 2) as i:
                for s in range(2):
                    slot = (s + lead) % 2
                    step(slot, i + (1 if lead and slot == 0 else 0), i * 2 + (s + lead), P,
                         i * 2 * P + (first + s * P))

        @block.sync
        def _(sp):
            sp.dma_start(gain[:, :], gain_cols).then_inc(gain_loaded, 16)

            def load(s, i, n, rows, c0):
                sp.wait_ge(x_free, n)
                src = rows0 if rows != P else rows_of(c0 - first if lead else c0)
                sp.dma_start(x[s][0:rows, :], src).then_inc(loaded[s], 16)
            each(sp, load)

        @block.scalar
        def _(act):
            act.wait_ge(eps_set, 1)

            def norm(s, i, n, rows, c0):
                act.wait_ge(loaded[s], i * 16 + 16)
                act.wait_ge(inverted, n)
                act.activation(square[0:rows, :], x[s][0:rows, :], ACT.Square,
                               accum_out=sumsq[s][0:rows, :]).then_inc(squared, 1)
                act.wait_ge(squared, n + 1)
                act.activation(root[s][0:rows, :], sumsq[s][0:rows, :], ACT.Sqrt,
                               scale=1.0 / D, bias=eps[0:rows, :]).then_inc(rooted, 1)
                act.wait_ge(gained, n * 2 + 2)
                act.activation(xh[:, :, ds(c0, rows)], xf[s][:, :, 0:rows], ACT.Copy).then_inc(high, 1)
            each(act, norm)

        @block.vector
        def _(dve):
            dve.memset(eps[:, :], RMS_EPS).then_inc(eps_set, 1)
            dve.wait_ge(gain_loaded, 16)

            def scale(s, i, n, rows, c0):
                dve.wait_ge(rooted, n + 1)
                dve.reciprocal(rinv[s][0:rows, :], root[s][0:rows, :]).then_inc(inverted, 1)
                dve.wait_ge(inverted, n + 1)
                dve.wait_ge(turned, n)
                dve.tensor_scalar(xs[s][0:rows, :], x[s][0:rows, :], rinv[s][0:rows, :], None,
                                  ALU.mult).then_inc(scaled, 1)
                dve.wait_ge(scaled, n + 1)
                dve.sem_inc(x_free, 1)
                dve.wait_ge(turned, n + 1)
                dve.wait_ge(low, n)
                for b in range(2):
                    half = tp[s][b][:, :].rearrange("p (k c) -> p k c", k=4)[:, :, 0:rows]
                    g = gain[:, 4 * b:4 * b + 4].unsqueeze(2).broadcast_to((P, 4, rows))
                    dve.tensor_tensor(xf[s][:, 4 * b:4 * b + 4, 0:rows], half, g, ALU.mult).then_inc(gained, 1)
            each(dve, scale)

        @block.tensor
        def _(pe):
            def turn(s, i, n, rows, c0):
                pe.wait_ge(scaled, n + 1)
                pe.wait_ge(gained, n * 2)
                for k in range(KD):
                    last = pe.transpose(tp[s][k // 4][:, (k % 4) * P:(k % 4) * P + rows],
                                        xs[s][0:rows, k * P:(k + 1) * P], ident[0:rows, 0:rows])
                last.then_inc(turned, 1)
            each(pe, turn)

        @block.gpsimd
        def _(pool):
            def remainder(s, i, n, rows, c0):
                pool.wait_ge(high, n + 1)
                pool.tensor_tensor(xl[:, :, ds(c0, rows)], xf[s][:, :, 0:rows],
                                   xh[:, :, ds(c0, rows)].bitcast(F32), ALU.subtract).then_inc(low, 1)
            each(pool, remainder)


def stage_in_proj(nc, w_in, p_dram, xh, xl):
    with ExitStack() as ctx:
        m = Mem(nc, ctx, "inproj")
        raw = [m.sb(f"raw{s}", [P, KD, P]) for s in range(2)]
        wh = [m.sb(f"wh{s}", [P, KD, P], F32R) for s in range(2)]
        wl = [m.sb(f"wl{s}", [P, KD, P], F32R) for s in range(2)]
        out = [m.sb(f"out{s}", [P, T]) for s in range(2)]
        acc = [[m.ps(f"acc{s}{g}") for g in range(3)] for s in range(2)]
        loaded = [m.sem(f"loaded{s}") for s in range(2)]
        stored = [m.sem(f"stored{s}") for s in range(2)]
        raw_free = m.sem("raw_free")
        w_high, w_low = m.sem("w_high"), m.sem("w_low")
        w_free = m.sem("w_free")
        group_done = m.sem("group_done")
        group_read = m.sem("group_read")
        AHEAD = 5
        block = ctx.enter_context(nc.Block())

        @block.sync
        def _(sp):
            for s in range(2):
                sp.dma_start(raw[s][:, :, :], w_in[s]).then_inc(loaded[s], 16)
            with sp.Fori(0, IN_TILES // 2 - 1) as i:
                for s in range(2):
                    sp.wait_ge(raw_free, i * 2 + (s + 1))
                    sp.dma_start(raw[s][:, :, :], w_in[ds(i * 2 + (s + 2), 1)].squeeze(0)).then_inc(loaded[s], 16)

        @block.gpsimd
        def _(pool):
            with pool.Fori(0, IN_TILES // 2) as i:
                for s in range(2):
                    pool.wait_ge(group_read, i * 6 + (3 * (s + 1) + AHEAD))
                    pool.dma_start(p_dram[ds(i * 2 + s, 1)].squeeze(0)[:, PAD:TPAD],
                                   out[s][:, :]).then_inc(stored[s], 16)
            for s in range(2):
                pool.wait_ge(stored[s], 16 * (IN_TILES // 2))

        @block.scalar
        def _(act):
            def high(s, i):
                act.wait_ge(loaded[s], i * 16 + 16)
                act.wait_ge(w_free, i * 2 + (s + 1))
                act.activation(wh[s][:, :, :], raw[s][:, :, :], ACT.Copy).then_inc(w_high, 1)

            act.sem_inc(group_read, AHEAD)
            high(0, 0)
            def drain(s, i):
                act.wait_ge(stored[s], i * 16)
                for g, (c, n) in enumerate(TOK_GROUPS):
                    act.wait_ge(group_done, i * 6 + (3 * s + g + 1))
                    act.activation(out[s][:, c:c + n], acc[s][g][:, 0:n], ACT.Copy).then_inc(group_read, 1)

            with act.Fori(0, IN_TILES // 2 - 1) as i:
                high(1, i)
                drain(0, i)
                high(0, i + 1)
                drain(1, i)
            high(1, IN_TILES // 2 - 1)
            drain(0, IN_TILES // 2 - 1)
            drain(1, IN_TILES // 2 - 1)

        @block.vector
        def _(dve):
            with dve.Fori(0, IN_TILES // 2) as i:
                for s in range(2):
                    dve.wait_ge(w_high, i * 2 + (s + 1))
                    dve.tensor_tensor(wl[s][:, :, :], raw[s][:, :, :], wh[s][:, :, :].bitcast(F32),
                                      ALU.subtract).then_inc(w_low, 1)
                    dve.wait_ge(w_low, i * 2 + (s + 1))
                    dve.sem_inc(raw_free, 1)

        @block.tensor
        def _(pe):
            pe.sem_inc(w_free, 2)
            with pe.Fori(0, IN_TILES // 2) as i:
                for s in range(2):
                    pe.wait_ge(w_high, i * 2 + (s + 1))
                    pe.wait_ge(w_low, i * 2 + (s + 1))
                    for g, (c, n) in enumerate(TOK_GROUPS):
                        pe.wait_ge(group_read, i * 6 + (3 * s + g))
                        for k in range(KD):
                            for j, (w, xx) in enumerate([(wh, xh), (wh, xl), (wl, xh)]):
                                last = pe.matmul(acc[s][g][:, 0:n], w[s][:, k, :], xx[:, k, c:c + n],
                                                 start=(k == 0 and j == 0), stop=(k == KD - 1 and j == 2))
                        last.then_inc(group_done, 1)
                    pe.sem_inc(w_free, 1)
import math

DECAY_C = math.exp(-0.5)
PGROUPS = [(0, 364), (364, 362), (726, 362)]
XGROUPS = [(CH, 512), (CH + 512, 512)]
V_MU, V_DB, V_AB, V_KK, V_KA, V_RK = 0, 3, 4, 5, 6, 7
NV = 8
F_A, F_R, F_B, F_K, F_V = range(5)


def stand_alone(eng):
    eng.nop(nofuse=True)


class Steps:

    def __init__(self, sem, names, back=1):
        self.sem, self.names, self.back, self.seen = sem, names.split(), back, 0

    def open(self, eng):
        eng.sem_inc(self.sem, self.back * len(self.names))

    def at(self, i, name, laps_ago=0):
        assert 0 <= laps_ago <= self.back
        return i * len(self.names) + ((self.back - laps_ago) * len(self.names) + self.names.index(name) + 1)

    def done(self, ins, name):
        assert self.names[self.seen % len(self.names)] == name, (name, self.names[self.seen % len(self.names)])
        self.seen += 1
        ins.then_inc(self.sem, 1)

    def wait(self, eng, i, name, laps_ago=0):
        eng.wait_ge(self.sem, self.at(i, name, laps_ago))

    def wait_lap_before(self, eng, i):
        self.wait(eng, i, self.names[-1], 1)


def stage_rwkv_prep(nc, p_dram, vecs, mu_low, w_decay_up, w_a_up, w_g_up, chunk_dram, gate_dram, bonus_dram,
                    pc, ones_bd):
    with ExitStack() as ctx:
        m = Mem(nc, ctx, "prep")
        low = m.sb("low", [P, 2, TPAD + 1])
        rkv = m.sb("rkv", [P, 3, TPAD + 1])
        mul = m.sb("mul", [P, 2])
        omul = m.sb("omul", [P, 2])
        tl = m.sb("tl", [P, TPAD])
        sg = m.sb("sg", [P, TPAD])
        wlow = m.sb("wlow", [P, 3, P])
        vec = m.sb("vec", [P, NV])
        omv = m.sb("omv", [P, 4])
        prev = [m.sb(f"prev{j}", [P, TPAD]) for j in range(3)]
        r = m.sb("r", [P, TPAD])
        k = m.sb("k", [P, TPAD])
        sw = m.sb("sw", [P, TPAD])
        aa = m.sb("aa", [P, TPAD])
        gate = m.sb("gate", [P, SEQ])
        bv = m.sb("bv", [P, SEQ])
        cum = m.sb("cum", [P, TPAD])
        grow = m.sb("grow", [P, CHUNKS, CH])
        fade = m.sb("fade", [P, CHUNKS, CH + 1])
        keep = m.sb("keep", [P, CHUNKS, CH])
        kk = m.sb("kk", [P, TPAD])
        sq = m.sb("sq", [P, TPAD])
        root = m.sb("root", [P, TPAD])
        fields = m.sb("fields", [P, CHUNKS, 5, CH])
        tiny = m.sb("tiny", [P, 1])
        bank = [m.ps(f"bank{b}") for b in range(5)]
        loaded, low_loaded, stored = m.sem("loaded"), m.sem("low_loaded"), m.sem("stored")
        init, lowp, lowa = m.sem("init"), m.sem("lowp"), m.sem("lowa")
        V = Steps(m.sem("vec_done"), "om omka r k v t1 kmod scan rinv A B rk bv0 bv1")
        A = Steps(m.sem("act_done"), "w0 w1 w2 a0 a1 a2 g0 g1 sq fade grow pc root0 root1 root2")
        G = Steps(m.sem("pool_done"), "p0 p1 p2 kk kkn R ka K")
        M = Steps(m.sem("mm_done"), "w0 w1 w2 a0 a1 a2 g0 g1 n0 n1 n2 b0 b1")
        block = ctx.enter_context(nc.Block())
        c3 = lambda t: t[:, :].rearrange("p (c n) -> p c n", n=CH)

        @block.sync
        def _(sp):
            sp.wait_ge(init, 7)
            for j, t in enumerate((T_DA, T_G)):
                sp.dma_start(low[:, j, 1 + PAD:], p_dram[t, :, PAD:TPAD]).then_inc(low_loaded, 16)
            sp.dma_start(mul[:, :], mu_low).then_inc(low_loaded, 16)
            with sp.Fori(0, PAIRS) as i:
                for steps in (V, G, M):
                    steps.wait_lap_before(sp, i)
                    stand_alone(sp)
                for j, t in enumerate((T_R, T_K, T_V)):
                    sp.dma_start(rkv[:, j, 1 + PAD:], p_dram[ds(i + t, 1)].squeeze(0)[:, PAD:TPAD]).then_inc(loaded, 16)
                sp.dma_start(vec[:, :], vecs[ds(i, 1)].squeeze(0)).then_inc(loaded, 16)
                sp.dma_start(wlow[0:HD, 0, :], w_decay_up[:, ds(i * P, P)]).then_inc(loaded, 16)
                sp.dma_start(wlow[HD:P, 1, :], w_a_up[:, ds(i * P, P)]).then_inc(loaded, 16)
                sp.dma_start(wlow[:, 2, :], w_g_up[:, ds(i * P, P)]).then_inc(loaded, 16)
                for steps, name in ((V, "bv1"), (G, "K"), (A, "root2")):
                    steps.wait(sp, i, name)
                    stand_alone(sp)
                sp.dma_start(chunk_dram[ds(i, 1)].squeeze(0).rearrange("c p f -> p c f"),
                             fields[:, :, :, :].rearrange("p c f n -> p c (f n)")).then_inc(stored, 16)
                sp.dma_start(gate_dram[ds(i, 1)].squeeze(0), gate[:, :]).then_inc(stored, 16)
                sp.dma_start(bonus_dram[ds(i, 1)].squeeze(0), bv[:, :]).then_inc(stored, 16)
                sp.wait_ge(stored, i * 48 + 48)
                stand_alone(sp)

        @block.gpsimd
        def _(pool):
            G.open(pool)
            pool.wait_ge(low_loaded, 48)
            for j in range(2):
                pool.tensor_scalar(prev[j][:, :], low[:, j, 0:TPAD], mul[:, j:j + 1], None, ALU.mult).then_inc(lowp, 1)
            pool.wait_ge(lowa, 2)
            with pool.Fori(0, PAIRS) as i:
                pool.wait_ge(loaded, i * 112 + 112)
                V.wait(pool, i, "om")
                stand_alone(pool)
                for j in range(3):
                    G.done(pool.tensor_scalar(prev[j][:, :], rkv[:, j, 0:TPAD], vec[:, V_MU + j:V_MU + j + 1],
                                              None, ALU.mult), f"p{j}")
                V.wait(pool, i, "k")
                stand_alone(pool)
                G.done(pool.tensor_scalar(kk[:, :], k[:, :], vec[:, V_KK:V_KK + 1], None, ALU.mult), "kk")
                V.wait(pool, i, "rinv")
                G.wait(pool, i, "kk")
                G.done(pool.tensor_tensor(kk[:, :], kk[:, :], root[:, :], ALU.mult), "kkn")
                A.wait(pool, i, "pc")
                G.done(pool.tensor_tensor(fields[:, :, F_R, :], c3(r), fade[:, :, 1:], ALU.mult), "R")
                G.wait(pool, i, "kkn")
                G.done(pool.tensor_tensor(sq[:, :], kk[:, :], aa[:, :], ALU.mult), "ka")
                G.done(pool.tensor_tensor(fields[:, :, F_K, :], c3(k), grow[:, :, :], ALU.mult), "K")

        @block.scalar
        def _(act):
            A.open(act)
            act.wait_ge(lowp, 5)
            act.activation(tl[0:HD, :], tl[0:HD, :], ACT.Tanh).then_inc(lowa, 1)
            act.activation(sg[:, :], sg[:, :], ACT.Sigmoid).then_inc(lowa, 1)
            with act.Fori(0, PAIRS) as i:
                V.wait_lap_before(act, i)
                G.wait_lap_before(act, i)
                act.wait_ge(loaded, i * 112 + 112)
                for g, (c, n) in enumerate(PGROUPS):
                    M.wait(act, i, f"w{g}")
                    A.done(act.activation(sw[:, c:c + n], bank[g][:, 0:n], ACT.Sigmoid, bias=vec[:, V_DB:V_DB + 1]), f"w{g}")
                for g, (c, n) in enumerate(PGROUPS):
                    M.wait(act, i, f"a{g}")
                    A.done(act.activation(aa[:, c:c + n], bank[g][:, 0:n], ACT.Sigmoid, bias=vec[:, V_AB:V_AB + 1]), f"a{g}")
                act.wait_ge(stored, i * 48)
                for g, (c, n) in enumerate(XGROUPS):
                    M.wait(act, i, f"g{g}")
                    A.done(act.activation(gate[:, c - CH:c - CH + n], bank[3 + g][:, 0:n], ACT.Copy), f"g{g}")
                G.wait(act, i, "kk")
                A.done(act.activation(sq[:, :], kk[:, :], ACT.Square), "sq")
                V.wait(act, i, "scan")
                A.done(act.activation(fade[:, :, 1:], c3(cum), ACT.Exp, scale=-DECAY_C), "fade")
                A.done(act.activation(grow[:, :, :], c3(cum), ACT.Exp, scale=DECAY_C), "grow")
                A.wait(act, i, "fade")
                A.done(act.activation(pc[:, ds(i, 1), :].squeeze(1), fade[:, :, CH], ACT.Copy), "pc")
                for g, (c, n) in enumerate(PGROUPS):
                    M.wait(act, i, f"n{g}")
                    A.done(act.activation(root[:, c:c + n], bank[g][:, 0:n], ACT.Sqrt, bias=tiny[:, :]), f"root{g}")

        @block.vector
        def _(dve):
            V.open(dve)
            dve.memset(low[:, :, 0:1 + PAD], 0.0).then_inc(init, 1)
            dve.memset(rkv[:, :, 0:1 + PAD], 0.0).then_inc(init, 1)
            dve.memset(wlow[:, 0:2, :], 0.0).then_inc(init, 1)
            dve.memset(fade[:, :, 0:1], 1.0).then_inc(init, 1)
            dve.memset(tiny[:, :], 1e-12).then_inc(init, 1)
            dve.memset(keep[:, :, :], 1.0).then_inc(init, 1)
            dve.wait_ge(init, 6)
            dve.memset(keep[:, :, 0:1], 0.0).then_inc(init, 1)
            dve.wait_ge(low_loaded, 48)
            dve.tensor_scalar(omul[:, :], mul[:, :], -1.0, 1.0, ALU.mult, ALU.add).then_inc(lowp, 1)
            dve.wait_ge(lowp, 3)
            for j, t in enumerate((tl, sg)):
                dve.scalar_tensor_tensor(t[:, :], low[:, j, 1:], omul[:, j:j + 1], prev[j][:, :],
                                         ALU.mult, ALU.add).then_inc(lowp, 1)
            with dve.Fori(0, PAIRS) as i:
                dve.wait_ge(loaded, i * 112 + 112)
                V.done(dve.tensor_scalar(omv[:, 0:3], vec[:, V_MU:V_MU + 3], -1.0, 1.0, ALU.mult, ALU.add), "om")
                V.done(dve.tensor_scalar(omv[:, 3:4], vec[:, V_KA:V_KA + 1], -1.0, 1.0, ALU.mult, ALU.add), "omka")
                V.wait(dve, i, "omka")
                dve.wait_ge(stored, i * 48)
                for j, (t, name) in enumerate(((r[:, :], "r"), (k[:, :], "k"), (fields[:, :, F_V, :], "v"))):
                    G.wait(dve, i, f"p{j}")
                    cur, before = rkv[:, j, 1:], prev[j][:, :]
                    if name == "v":
                        cur, before = (a.rearrange("p (c n) -> p c n", n=CH) for a in (cur, before))
                    V.done(dve.scalar_tensor_tensor(t, cur, omv[:, j:j + 1], before, ALU.mult, ALU.add), name)
                V.wait(dve, i, "v")
                A.wait(dve, i, "a2")
                V.done(dve.tensor_scalar(prev[0][:, :], aa[:, :], vec[:, V_KA:V_KA + 1], omv[:, 3:4], ALU.mult, ALU.add), "t1")
                V.wait(dve, i, "t1")
                G.wait(dve, i, "kk")
                V.done(dve.tensor_tensor(k[:, :], k[:, :], prev[0][:, :], ALU.mult), "kmod")
                V.done(dve.tensor_tensor_scan(cum[:, :], keep[:, :, :].rearrange("p c n -> p (c n)"), sw[:, :], 0.0,
                                              ALU.mult, ALU.add), "scan")
                A.wait(dve, i, "root2")
                V.done(dve.reciprocal(root[:, :], root[:, :]), "rinv")
                G.wait(dve, i, "kkn")
                V.done(dve.scalar_tensor_tensor(fields[:, :, F_A, :], c3(kk), -1.0, fade[:, :, 0:CH], ALU.mult, ALU.mult), "A")
                G.wait(dve, i, "ka")
                V.done(dve.tensor_tensor(fields[:, :, F_B, :], c3(sq), grow[:, :, :], ALU.mult), "B")
                V.done(dve.scalar_tensor_tensor(prev[1][:, :], r[:, :], vec[:, V_RK:V_RK + 1], k[:, :], ALU.mult, ALU.mult), "rk")
                for g, (c, n) in enumerate(XGROUPS):
                    M.wait(dve, i, f"b{g}")
                    vv = fields[:, c // CH:(c + n) // CH, F_V, :]
                    V.done(dve.tensor_tensor(bv[:, c - CH:c - CH + n].rearrange("p (c n) -> p c n", n=CH),
                                             bank[3 + g][:, 0:n].rearrange("p (c n) -> p c n", n=CH), vv, ALU.mult), f"bv{g}")

        @block.tensor
        def _(pe):
            M.open(pe)
            pe.wait_ge(lowa, 2)
            pe.wait_ge(lowp, 5)
            with pe.Fori(0, PAIRS) as i:
                pe.wait_ge(loaded, i * 112 + 112)
                V.wait_lap_before(pe, i)
                A.wait_lap_before(pe, i)
                for g, (c, n) in enumerate(PGROUPS):
                    M.done(pe.matmul(bank[g][:, 0:n], wlow[:, 0, :], tl[:, c:c + n], start=True, stop=True), f"w{g}")
                for g, (c, n) in enumerate(PGROUPS):
                    A.wait(pe, i, f"w{g}")
                    M.done(pe.matmul(bank[g][:, 0:n], wlow[:, 1, :], tl[:, c:c + n], start=True, stop=True), f"a{g}")
                for g, (c, n) in enumerate(XGROUPS):
                    M.done(pe.matmul(bank[3 + g][:, 0:n], wlow[:, 2, :], sg[:, c:c + n], start=True, stop=True), f"g{g}")
                A.wait(pe, i, "sq")
                for g, (c, n) in enumerate(PGROUPS):
                    M.done(pe.matmul(bank[g][:, 0:n], ones_bd[:, :], sq[:, c:c + n], start=True, stop=True), f"n{g}")
                V.wait(pe, i, "rk")
                for g, (c, n) in enumerate(XGROUPS):
                    M.done(pe.matmul(bank[3 + g][:, 0:n], ones_bd[:, :], prev[1][:, c:c + n], start=True, stop=True), f"b{g}")

LEVELS = [2, 4, 8, 16, 32]
M_N, M_K, M_R, M_L1T, M_LEVEL = 0, 1, 2, 3, 4
N_MASKS = M_LEVEL + len(LEVELS)

SB_CLAMP = 40.0
SBW = 512
GROUPS = SEQ // SBW


class Tally:

    def __init__(self, sem, per):
        self.sem, self.per = sem, per

    def open(self, eng):
        eng.sem_inc(self.sem, self.per)

    def wait(self, eng, i, n):
        assert -self.per <= n < self.per
        eng.wait_ge(self.sem, i * self.per + (self.per + n + 1))


def sb_tasks():
    tasks = []
    for h in range(2):
        for g in reversed(range(GROUPS)):
            for b in range((g + 1) * SBW // P, -1, -1):
                tasks.append((h, g, b, max(0, (b - 1) * P - g * SBW), b > g * SBW // P))
    return tasks


def sb_keys(b):
    return (0, CH) if b == 0 else (CH + (b - 1) * P, P)


SCAN_STEPS = 6 + 3 * len(LEVELS)
LAPS = 4
SB_LAG = 6
SB_HEAD = 5


def interleave(scans, sticks):
    total = LAPS * SCAN_STEPS
    quarters = 4 * (len(sb_tasks()) + SB_LAG) + 1
    k = given = 0
    for scan in scans:
        for _ in scan:
            k += 1
            due = max(0, k - SB_HEAD) * quarters // (total - SB_HEAD)
            for _ in range(due - given):
                next(sticks)
            given = due
    assert k == total and given == quarters and next(sticks, "end") == "end"


def stage_rwkv_masks(nc, masks):
    with ExitStack() as ctx:
        m = Mem(nc, ctx, "masks")
        step = m.sem("step")
        ones = m.sem("ones")
        block = ctx.enter_context(nc.Block())
        count = [0]

        @block.vector
        def _(dve):
            dve.memset(masks[:, :, :], 1.0).then_inc(ones, 1)

        @block.gpsimd
        def _(pool):
            pool.wait_ge(ones, 1)

            def select(view, pattern, base, mult, op=ALU.is_ge):
                pool.affine_select(out=view, in_=view, compare_op=op, fill=0.0, base=base, pattern=pattern,
                                   channel_multiplier=mult).then_inc(step, 1)
                count[0] += 1
                pool.wait_ge(step, count[0])

            def heads(k):
                return masks[:, k, :].rearrange("p (h n) -> p h n", h=2)

            for k in (M_N, M_K, M_R):
                op = ALU.is_ge if k == M_R else ALU.is_gt
                for h in range(2):
                    rows = slice(h * HD, (h + 1) * HD)
                    v = masks[rows, k, :].rearrange("p (h n) -> p h n", h=2)
                    select(v, [[0, 2], [1, CH]], 0, -1, op)
            select(heads(M_N), [[-CH, 2], [0, CH]], 0, 1)
            select(heads(M_N), [[CH, 2], [0, CH]], CH - 1, -1)
            select(masks[0:HD, M_K, 0:CH], [[0, CH]], -1, 0)
            select(masks[HD:P, M_K, CH:P], [[0, CH]], -1, 0)
            pairs2 = lambda k, b: masks[:, k, :].rearrange("p (j c) -> p j c", c=b)
            def block_diag(view, n, b):
                select(view, [[-b, n], [0, b]], 0, 1)
                select(view, [[b, n], [0, b]], b - 1, -1)
            block_diag(pairs2(M_L1T, 2), P // 2, 2)
            select(masks[:, M_L1T, :], [[1, P]], 0, -1, ALU.is_gt)
            for j, l in enumerate(LEVELS):
                k = M_LEVEL + j
                b = 2 * l
                v = pairs2(k, b)
                select(v, [[-b, P // b], [0, b]], -l, 1)
                select(v, [[b, P // b], [0, b]], b - 1, -1)
                select(v, [[0, P // b], [-1, b]], l - 1, 0)


def stage_mix(nc, chunk_dram, p_dram, masks, ident, pc, y_sb, o_sb, w_out, w_raw):
    tasks = sb_tasks()
    N = len(tasks)
    diag_at = [n for n in range(N) if tasks[n][4]]
    ends = [n for n in range(N) if tasks[n][2] == 0]
    with ExitStack() as ctx:
        m = Mem(nc, ctx, "mix")
        ar = [m.sb(f"ar{s}", [P, PAIRS, 3, 2, CH]) for s in range(2)]
        bkb = [m.sb(f"bkb{s}", [P, PAIRS, 3, CH]) for s in range(2)]
        v2 = [m.sb(f"v2{s}", [P, PAIRS, 2, CH]) for s in range(2)]
        nl = m.sb("nl", [P, PAIRS, 2, P])
        rb = m.sb("rb", [P, PAIRS, 2, 2, CH])
        x = m.sb("x", [P, PAIRS, P])
        xt = m.sb("xt", [P, PAIRS, P])
        lvl = m.sb("lvl", [P, PAIRS, P])
        ak = m.sb("ak", [P, PAIRS, 2, CH])
        wuv = m.sb("wuv", [P, PAIRS, 2, 2, CH])
        qm = m.sb("qm", [P, PAIRS, 2, 2, CH])
        state = m.sb("state", [P, PAIRS, CH])
        bank = [m.ps(f"bank{q}") for q in range(PAIRS)]
        qz = m.sb("qz", [P, 2, SEQ])
        kt = m.sb("kt", [P, TPAD])
        vt = m.sb("vt", [P, TPAD])
        v = m.sb("v", [P, 9, P])
        tri = m.sb("tri", [P, P])
        rest = m.sb("rest", [P, P])
        z = [m.sb(f"z{i}", [P, SBW]) for i in range(4)]
        w = [m.sb(f"w{i}", [P, SBW]) for i in range(4)]
        a = [m.sb(f"a{i}", [P, SBW]) for i in range(3)]
        zb = [m.ps(f"zb{i}") for i in range(2)]
        cb = m.ps("cb")
        ob = m.ps("ob")

        loaded = [m.sem(f"loaded{s}") for s in range(2)]
        zeroed = m.sem("zeroed")
        qs = range(PAIRS)
        every = lambda names: " ".join(f"{n}{q}" for n in names.split() for q in qs)
        V = Steps(m.sem("vec_done"), every(f"nl rl x1a x1b {' '.join(f'z{l} x{l}' for l in LEVELS)} qm0 qm1 s"))
        A = Steps(m.sem("act_done"), every(f"ta0 ta1 tv0 tv1 tbk lv x0 {' '.join(f't{l}' for l in LEVELS)} w0 w1 y"))
        M = Steps(m.sem("mm_done"), every(f"tp g lv x0 {' '.join(f'n{l} x{l} t{l}' for l in LEVELS)} wu qm sy"))
        LOADS = 8 * 16
        ZEROED = 10
        sb_loaded, tri_set, w_loaded = m.sem("sb_loaded"), m.sem("tri_set"), m.sem("w_loaded")
        SB_LOADS = 4 * 16
        v_turned, v_copied = Tally(m.sem("v_turned"), 1), Tally(m.sem("v_copied"), 1)
        (z_done, z_copied, clamped, exp_done, ln_done, soft, tri_done, exponent, rest_done, weights, pv_done) = (
            Tally(m.sem(name), N) for name in ("z_done", "z_copied", "clamped", "exp_done", "ln_done", "soft", "tri_done",
                                               "exponent", "rest_done", "weights", "pv_done"))
        soft_masked, weights_masked = (Tally(m.sem(name), len(diag_at)) for name in ("soft_masked", "weights_masked"))
        o_copied = Tally(m.sem("o_copied"), len(ends))
        block = ctx.enter_context(nc.Block())

        def program(eng, lap, sticks):
            for _ in lap(0, 0, 0):
                pass
            with eng.Fori(0, PAIRS) as i:
                interleave([lap(i * LAPS + (1 + l), (1 + l) % 2, i * 2 + (1 + l) // 2) for l in range(LAPS)], sticks(i))

        def task(n):
            if not 0 <= n < N:
                return None
            h, g, b, off, diag = tasks[n]
            return h, g, b, off, sb_keys(b)[1], diag

        @block.sync
        def _(sp):
            def load(n, s):
                src = chunk_dram[:, ds(n, 1)].squeeze(1).rearrange("q p f -> p q f")
                for h in range(2):
                    rows = slice(h * HD, (h + 1) * HD)
                    for f in (F_A, F_R):
                        sp.dma_start(ar[s][rows, :, f, h, :], src[rows, :, f * CH:(f + 1) * CH]).then_inc(loaded[s], 16)
                sp.dma_start(bkb[s][:, :, 0:2, :].rearrange("p q f n -> p q (f n)"),
                             src[:, :, 2 * CH:4 * CH]).then_inc(loaded[s], 16)
                sp.dma_start(bkb[s][:, :, 2, :], src[:, :, 2 * CH:3 * CH]).then_inc(loaded[s], 16)
                for h in range(2):
                    sp.dma_start(v2[s][:, :, h, :], src[:, :, 4 * CH:]).then_inc(loaded[s], 16)

            def reload(n, s, last):
                for steps in (V, M):
                    steps.wait(sp, last, steps.names[-1])
                    stand_alone(sp)
                load(n, s)

            sp.wait_ge(zeroed, ZEROED)
            load(0, 0)
            load(1, 1)
            for k in range(KD):
                sp.dma_start(w_raw[:, k, :], w_out[k]).then_inc(w_loaded, 16)
            with sp.Fori(1, CHUNKS // 2) as i:
                for s in range(2):
                    reload(i * 2 + s, s, i * 2 + (s - 2))
            reload(CHUNKS - 1, 0, CHUNKS - 3)
            sp.wait_ge(w_loaded, 16 * KD)

        @block.gpsimd
        def _(pool):
            soft_masked.open(pool)
            weights_masked.open(pool)
            pool.wait_ge(zeroed, ZEROED)
            pool.affine_select(out=tri[:, :], in_=tri[:, :], compare_op=ALU.is_ge, fill=0.0, base=0,
                               pattern=[[-1, P]], channel_multiplier=1).then_inc(tri_set, 1)
            pool.affine_select(out=rest[:, :], in_=rest[:, :], compare_op=ALU.is_gt, fill=0.0, base=0,
                               pattern=[[1, P]], channel_multiplier=-1).then_inc(tri_set, 1)

            def mask(tile, off, tally):
                stand_alone(pool)
                part = tile[:, off:off + P]
                pool.affine_select(out=part, in_=part, compare_op=ALU.is_gt, fill=0.0, base=0,
                                   pattern=[[1, P]], channel_multiplier=-1).then_inc(tally.sem, 1)

            with pool.Fori(0, PAIRS) as i:
                z_done.wait(pool, i, -1)
                stand_alone(pool)
                for h in range(2):
                    half = slice(h * HD, (h + 1) * HD)
                    pool.dma_start(qz[half, h, :], p_dram[ds(i + T_SQ, 1)].squeeze(0)[half, CH:TPAD]).then_inc(sb_loaded, 16)
                pool.dma_start(kt[:, PAD:], p_dram[ds(i + T_SK, 1)].squeeze(0)[:, PAD:TPAD]).then_inc(sb_loaded, 16)
                pool.dma_start(vt[:, PAD:], p_dram[ds(i + T_SV, 1)].squeeze(0)[:, PAD:TPAD]).then_inc(sb_loaded, 16)
                for t in range(N + SB_LAG):
                    n = t - 4
                    if task(n) and task(n)[5]:
                        weights.wait(pool, i, n)
                        mask(a[n % 3], task(n)[3], weights_masked)
                    n = t - 2
                    if task(n) and task(n)[5]:
                        soft.wait(pool, i, n)
                        mask(w[n % 4], task(n)[3], soft_masked)

        @block.scalar
        def _(act):
            A.open(act)
            for tally in (v_copied, z_copied, exp_done, ln_done, weights, o_copied):
                tally.open(act)
            act.preload_act_table_set("natural_log_exp_and_others")
            act.wait_ge(zeroed, ZEROED)

            def lap(n, s, use):
                def copy(out, in_, name):
                    A.done(act.activation(out, in_, ACT.Copy), name)
                lo, hi = slice(0, HD), slice(HD, P)
                for q in qs:
                    M.wait(act, n, f"tp{q}")
                    copy(ak[lo, q, 0, :], bank[q][lo, 0:CH], f"ta0{q}")
                for q in qs:
                    copy(ak[hi, q, 0, :], bank[q][hi, CH:2 * CH], f"ta1{q}")
                for q in qs:
                    copy(wuv[hi, q, 1, 0, :], bank[q][hi, P:P + CH], f"tv0{q}")
                for q in qs:
                    copy(wuv[lo, q, 1, 1, :], bank[q][lo, P + CH:2 * P], f"tv1{q}")
                for q in qs:
                    t = bank[q][:, 2 * P:4 * P].rearrange("p (t n) -> p t n", n=CH)[:, 0:4:3, :]
                    copy(rb[:, q, 1, :, :], t, f"tbk{q}")
                yield "tp"
                yield "g"
                for q in qs:
                    M.wait(act, n, f"lv{q}")
                    copy(ak[:, q, 1, :], bank[q][:, 0:CH], f"lv{q}")
                yield "lv"
                for q in qs:
                    M.wait(act, n, f"x0{q}")
                    copy(x[:, q, :], bank[q][:, 0:P], f"x0{q}")
                yield "x0"
                for l in LEVELS:
                    yield "n"
                    yield "x"
                    for q in qs:
                        M.wait(act, n, f"t{l}{q}")
                        copy(xt[:, q, :], bank[q][:, 0:P], f"t{l}{q}")
                    yield "t"
                for h in range(2):
                    rows = slice(h * HD, (h + 1) * HD)
                    for q in qs:
                        M.wait(act, n, f"wu{q}")
                        copy(wuv[rows, q, :, h, :], bank[q][rows, 0:P].rearrange("p (f n) -> p f n", f=2), f"w{h}{q}")
                yield "wu"
                for q in qs:
                    M.wait(act, n, f"sy{q}")
                    copy(y_sb[:, q, ds(n * CH, CH)], bank[q][:, CH:P], f"y{q}")
                yield "qm sy"

            def sticks(i):
                v_turned.wait(act, i, 0)
                act.activation(v[:, 1:5, :], zb[0][:, :].rearrange("p (b n) -> p b n", n=P), ACT.Copy)
                act.activation(v[:, 5:9, :], zb[1][:, :].rearrange("p (b n) -> p b n", n=P), ACT.Copy)
                act.activation(v[0:CH, 0, :], cb[0:CH, 0:P], ACT.Copy).then_inc(v_copied.sem, 1)
                yield
                for t in range(N + SB_LAG):
                    n = t - 1
                    if task(n):
                        h, g, b, off, r, diag = task(n)
                        z_done.wait(act, i, n)
                        exponent.wait(act, i, n - 4)
                        act.activation(z[n % 4][0:r, off:], zb[n % 2][0:r, off:], ACT.Copy, scale=HD ** -0.5).then_inc(z_copied.sem, 1)
                    yield
                    n = t - 2
                    if task(n):
                        h, g, b, off, r, diag = task(n)
                        part = w[n % 4][0:r, off:]
                        clamped.wait(act, i, n)
                        act.activation(part, part, ACT.Exp).then_inc(exp_done.sem, 1)
                        exp_done.wait(act, i, n)
                        act.activation(part, part, ACT.Ln, bias=1.0).then_inc(ln_done.sem, 1)
                    yield
                    n = t - 6
                    if n in ends:
                        h, g = tasks[n][0:2]
                        half = slice(h * HD, (h + 1) * HD)
                        pv_done.wait(act, i, n)
                        act.activation(o_sb[half, ds(i, 1), g * SBW:(g + 1) * SBW].squeeze(1), ob[half, :],
                                       ACT.Copy).then_inc(o_copied.sem, 1)
                    yield
                    n = t - 4
                    if task(n):
                        h, g, b, off, r, diag = task(n)
                        part = a[n % 3][0:r, off:]
                        exponent.wait(act, i, n)
                        act.activation(part, part, ACT.Exp).then_inc(weights.sem, 1)
                    yield
            program(act, lap, sticks)

        @block.vector
        def _(dve):
            V.open(dve)
            for tally in (clamped, soft, exponent):
                tally.open(dve)
            for s in range(2):
                dve.memset(ar[s][:, :, 0:2, :, :].rearrange("p q f h n -> p q (f h n)"), 0.0).then_inc(zeroed, 1)
                for h in range(2):
                    same = ident[:, :].rearrange("p (h n) -> p h n", h=2)
                    rows = slice(h * HD, (h + 1) * HD)
                    for q in qs:
                        last = dve.tensor_copy(ar[s][rows, q, 2, h, :], same[rows, h, :])
                last.then_inc(zeroed, 1)
            dve.memset(wuv[:, :, :, :, :], 0.0)
            dve.memset(qm[:, :, :, :, :], 0.0)
            dve.memset(state[:, :, :], 0.0).then_inc(zeroed, 1)
            dve.memset(qz[:, :, :], 0.0).then_inc(zeroed, 1)
            dve.memset(kt[:, 0:PAD], 0.0).then_inc(zeroed, 1)
            dve.memset(vt[:, 0:PAD], 0.0).then_inc(zeroed, 1)
            dve.memset(tri[:, :], 1.0).then_inc(zeroed, 1)
            dve.memset(rest[:, :], 1.0).then_inc(zeroed, 1)
            dve.wait_ge(zeroed, ZEROED)

            def lap(n, s, use):
                yield "tp"
                for q in qs:
                    M.wait(dve, n, f"g{q}")
                    both = bank[q][:, 0:P].unsqueeze(1).broadcast_to((P, 2, P))
                    V.done(dve.tensor_tensor(nl[:, q, :, :], both, masks[:, M_N:M_N + 2, :], ALU.mult), f"nl{q}")
                for q in qs:
                    V.done(dve.tensor_tensor(rb[:, q, 0, :, :].rearrange("p h n -> p (h n)"), bank[q][:, P:2 * P],
                                             masks[:, M_R, :], ALU.mult), f"rl{q}")
                for q in qs:
                    V.wait(dve, n, f"nl{q}")
                    V.done(dve.tensor_tensor(xt[:, q, :], nl[:, q, 0, :], masks[:, M_L1T, :], ALU.mult), f"x1a{q}")
                for q in qs:
                    V.wait(dve, n, f"x1a{q}")
                    V.done(dve.tensor_tensor(xt[:, q, :], xt[:, q, :], ident[:, :], ALU.add), f"x1b{q}")
                yield "g"
                yield "lv"
                yield "x0"
                for j, l in enumerate(LEVELS):
                    for q in qs:
                        M.wait(dve, n, f"n{l}{q}")
                        V.done(dve.tensor_tensor(lvl[:, q, :], bank[q][:, 0:P], masks[:, M_LEVEL + j, :], ALU.mult), f"z{l}{q}")
                    yield "n"
                    for q in qs:
                        M.wait(dve, n, f"x{l}{q}")
                        V.done(dve.tensor_tensor(x[:, q, :], x[:, q, :], bank[q][:, 0:P], ALU.add), f"x{l}{q}")
                    yield "x"
                    yield "t"
                yield "wu"
                for h in range(2):
                    rows = slice(h * HD, (h + 1) * HD)
                    for q in qs:
                        M.wait(dve, n, f"qm{q}")
                        V.done(dve.tensor_tensor(
                            qm[rows, q, :, h, :], bank[q][rows, 0:2 * P].rearrange("p (f h n) -> p f h n", f=2, h=2)[:, :, h, :],
                            ar[s][rows, q, 1:3, h, :], ALU.add), f"qm{h}{q}")
                for q in qs:
                    A.wait(dve, n, f"y{q}")
                    V.done(dve.tensor_scalar(state[:, q, :], bank[q][:, 0:CH], pc[:, q, ds(n, 1)], None, ALU.mult), f"s{q}")
                yield "qm sy"

            def sticks(i):
                yield
                for t in range(N + SB_LAG):
                    n = t - 1
                    if task(n):
                        h, g, b, off, r, diag = task(n)
                        z_copied.wait(dve, i, n)
                        rest_done.wait(dve, i, n - 4)
                        dve.tensor_scalar(w[n % 4][0:r, off:], z[n % 4][0:r, off:], SB_CLAMP, None, ALU.min).then_inc(clamped.sem, 1)
                    yield
                    yield
                    n = t - 2
                    if task(n):
                        h, g, b, off, r, diag = task(n)
                        part = w[n % 4][0:r, off:]
                        ln_done.wait(dve, i, n)
                        dve.tensor_tensor(part, z[n % 4][0:r, off:], part, ALU.max).then_inc(soft.sem, 1)
                    yield
                    n = t - 3
                    if task(n):
                        h, g, b, off, r, diag = task(n)
                        tri_done.wait(dve, i, n)
                        pv_done.wait(dve, i, n - 3)
                        dve.tensor_tensor(a[n % 3][0:r, off:], z[n % 4][0:r, off:], cb[0:r, off:], ALU.subtract).then_inc(exponent.sem, 1)
                    yield
            program(dve, lap, sticks)

        @block.tensor
        def _(pe):
            M.open(pe)
            for tally in (v_turned, z_done, tri_done, rest_done, pv_done):
                tally.open(pe)
            pe.wait_ge(zeroed, ZEROED)
            pe.wait_ge(tri_set, 2)

            def lap(n, s, use):
                pe.wait_ge(loaded[s], use * LOADS + LOADS)
                for q in qs:
                    V.wait(pe, n, f"s{q}", 1)
                    tp = bank[q]
                    pe.transpose(tp[:, 0:P], ar[s][:, q, 0, :, :].rearrange("p h n -> p (h n)"), ident[:, :])
                    pe.transpose(tp[:, P:2 * P], v2[s][:, q, :, :].rearrange("p f n -> p (f n)"), ident[:, :])
                    pe.transpose(tp[:, 2 * P:3 * P], bkb[s][:, q, 0:2, :].rearrange("p f n -> p (f n)"), ident[:, :])
                    M.done(pe.transpose(tp[:, 3 * P:4 * P], bkb[s][:, q, 1:3, :].rearrange("p f n -> p (f n)"), ident[:, :]), f"tp{q}")
                yield "tp"
                for q in qs:
                    A.wait(pe, n, f"tbk{q}")
                    for h in range(2):
                        out = bank[q][:, 0:2 * P].rearrange("p (f h n) -> p f h n", f=2, h=2)[:, :, h, :]
                        last = pe.matmul(out, bkb[s][:, q, h:h + 2, :].rearrange("p f n -> p (f n)"),
                                         ar[s][:, q, 0:2, h, :], start=True, stop=True)
                    M.done(last, f"g{q}")
                yield "g"
                for q in qs:
                    V.wait(pe, n, f"rl{q}")
                    for h in range(2):
                        last = pe.matmul(bank[q][h * HD:(h + 1) * HD, 0:CH], nl[:, q, 1, h * CH:(h + 1) * CH],
                                         wuv[:, q, 1, h, :], start=True, stop=True)
                    M.done(last, f"lv{q}")
                yield "lv"
                for q in qs:
                    V.wait(pe, n, f"x1b{q}")
                    A.wait(pe, n, f"lv{q}")
                    M.done(pe.transpose(bank[q][:, 0:P], xt[:, q, :], ident[:, :]), f"x0{q}")
                yield "x0"
                before = "x0"
                for l in LEVELS:
                    for q in qs:
                        A.wait(pe, n, f"{before}{q}")
                        M.done(pe.matmul(bank[q][:, 0:P], nl[:, q, 0, :], x[:, q, :], start=True, stop=True), f"n{l}{q}")
                    yield "n"
                    for q in qs:
                        V.wait(pe, n, f"z{l}{q}")
                        M.done(pe.matmul(bank[q][:, 0:P], xt[:, q, :], lvl[:, q, :], start=True, stop=True), f"x{l}{q}")
                    yield "x"
                    for q in qs:
                        V.wait(pe, n, f"x{l}{q}")
                        M.done(pe.transpose(bank[q][:, 0:P], x[:, q, :], ident[:, :]), f"t{l}{q}")
                    yield "t"
                    before = f"t{l}"
                for q in qs:
                    A.wait(pe, n, f"{before}{q}")
                    M.done(pe.matmul(bank[q][:, 0:P], xt[:, q, :], ak[:, q, :, :].rearrange("p f n -> p (f n)"),
                                     start=True, stop=True), f"wu{q}")
                yield "wu"
                for q in qs:
                    A.wait(pe, n, f"w1{q}")
                    M.done(pe.matmul(bank[q][:, 0:2 * P], wuv[:, q, 0, :, :].rearrange("p h n -> p (h n)"),
                                     rb[:, q, :, :, :].rearrange("p f h n -> p (f h n)"), start=True, stop=True), f"qm{q}")
                for q in qs:
                    V.wait(pe, n, f"qm1{q}")
                    for h in range(2):
                        s_out = bank[q][h * HD:(h + 1) * HD, 0:CH]
                        pe.matmul(s_out, rb[:, q, 1, h, :], wuv[:, q, 1, h, :], start=True, stop=False)
                        pe.matmul(s_out, qm[:, q, 1, h, :], state[:, q, :], start=False, stop=True)
                    for h in range(2):
                        y_out = bank[q][h * HD:(h + 1) * HD, CH:P]
                        pe.matmul(y_out, state[:, q, :], qm[:, q, 0, h, :], start=True, stop=False)
                        last = pe.matmul(y_out, wuv[:, q, 1, h, :], rb[:, q, 0, h, :], start=False, stop=True)
                    M.done(last, f"sy{q}")
                yield "qm sy"

            def sticks(i):
                pe.wait_ge(sb_loaded, i * SB_LOADS + SB_LOADS)
                z_copied.wait(pe, i, -1)
                exponent.wait(pe, i, -1)
                for j in range(9):
                    c, r = sb_keys((j + 1) % 9)
                    dst = (zb[0], zb[1], cb)[j // 4]
                    last = pe.transpose(dst[0:r, (j % 4) * P:(j % 4 + 1) * P], vt[:, c:c + r], ident[:, :])
                last.then_inc(v_turned.sem, 1)
                yield
                for t in range(N + SB_LAG):
                    n = t
                    if task(n):
                        h, g, b, off, r, diag = task(n)
                        c, _ = sb_keys(b)
                        if n < 2:
                            v_copied.wait(pe, i, 0)
                        else:
                            z_copied.wait(pe, i, n - 2)
                        pe.matmul(zb[n % 2][0:r, off:], kt[:, c:c + r], qz[:, h, g * SBW + off:(g + 1) * SBW],
                                  start=True, stop=True).then_inc(z_done.sem, 1)
                    yield
                    n = t - 4
                    if task(n):
                        h, g, b, off, r, diag = task(n)
                        exponent.wait(pe, i, n)
                        if b:
                            pe.matmul(cb[:, off:], rest[0:r, :], w[n % 4][0:r, off:], start=False, stop=True,
                                      skip_group_check=True).then_inc(rest_done.sem, 1)
                        else:
                            pe.sem_inc(rest_done.sem, 1)
                    yield
                    n = t - 3
                    if task(n):
                        h, g, b, off, r, diag = task(n)
                        if diag:
                            soft_masked.wait(pe, i, diag_at.index(n))
                        else:
                            soft.wait(pe, i, n)
                        if r == CH:
                            stand_alone(pe)
                        pe.matmul(cb[0:r, off:], tri[0:r, 0:r], w[n % 4][0:r, off:], start=(b == (g + 1) * SBW // P),
                                  stop=True, skip_group_check=True).then_inc(tri_done.sem, 1)
                    yield
                    n = t - 5
                    if task(n):
                        h, g, b, off, r, diag = task(n)
                        first = b == (g + 1) * SBW // P
                        if diag:
                            weights_masked.wait(pe, i, diag_at.index(n))
                        else:
                            weights.wait(pe, i, n)
                        if first:
                            o_copied.wait(pe, i, sum(e < n for e in ends) - 1)
                        if r == CH:
                            stand_alone(pe)
                        pe.matmul(ob[h * HD:(h + 1) * HD, off:], v[0:r, b, h * HD:(h + 1) * HD], a[n % 3][0:r, off:],
                                  start=first, stop=(b == 0), skip_group_check=True).then_inc(pv_done.sem, 1)
                    yield
            program(pe, lap, sticks)

V_LG, V_LB, V_SG = 0, 1, 2


def stage_post_heads(nc, y_sb, o_sb, vecs, gate_dram, bonus_dram, ones_bd, w_raw, wh, wl):
    with ExitStack() as ctx:
        m = Mem(nc, ctx, "post")
        qs = range(PAIRS)
        dev = [m.sb(f"dev{q}", [P, SEQ])[:, :] for q in qs]
        rs = [m.sb(f"rs{q}", [P, SEQ])[:, :] for q in qs]
        ors = [m.sb(f"ors{q}", [P, SEQ]) for q in qs]
        gate = [m.sb(f"gate{s}", [P, SEQ]) for s in range(2)]
        bonus = [m.sb(f"bonus{s}", [P, SEQ]) for s in range(2)]
        vec = m.sb("vec", [P, PAIRS, 3])
        eps = m.sb("eps", [P, 2])
        sums = [m.ps(f"sums{q}", (P, SEQ)) for q in qs]
        loaded = [m.sem(f"loaded{s}") for s in range(2)]
        vec_loaded, eps_set = m.sem("vec_loaded"), m.sem("eps_set")
        (mean_done, var_done, osum_done, dev_done, dev_squared, o_squared, rs_ln, rs_done, ors_ln, ors_done,
         scaled, with_bonus, gated, o_scaled, w_high, w_low) = (m.sem(name) for name in (
            "mean_done", "var_done", "osum_done", "dev_done", "dev_squared", "o_squared", "rs_ln", "rs_done", "ors_ln",
            "ors_done", "scaled", "with_bonus", "gated", "o_scaled", "w_high", "w_low"))
        block = ctx.enter_context(nc.Block())
        half = lambda g: slice(g * 512, g * 512 + 512)

        @block.sync
        def _(sp):
            sp.dma_start(vec[:, :, :], vecs).then_inc(vec_loaded, 16)
            for q in qs:
                if q >= 2:
                    sp.wait_ge(gated, q - 1)
                sp.dma_start(bonus[q % 2][:, :], bonus_dram[q]).then_inc(loaded[q % 2], 16)
                sp.dma_start(gate[q % 2][:, :], gate_dram[q]).then_inc(loaded[q % 2], 16)

        @block.tensor
        def _(pe):
            for q in qs:
                for g in range(2):
                    last = pe.matmul(sums[q][:, half(g)], ones_bd[:, :], y_sb[:, q, CH + g * 512:CH + g * 512 + 512],
                                     start=True, stop=True)
                last.then_inc(mean_done, 1)
            for q in qs:
                pe.wait_ge(dev_squared, q + 1)
                for g in range(2):
                    last = pe.matmul(sums[q][:, half(g)], ones_bd[:, :], rs[q][:, half(g)], start=True, stop=True)
                last.then_inc(var_done, 1)
            for q in qs:
                pe.wait_ge(o_squared, q + 1)
                pe.wait_ge(rs_ln, q + 1)
                for g in range(2):
                    last = pe.matmul(sums[q][:, half(g)], ones_bd[:, :], ors[q][:, half(g)], start=True, stop=True)
                last.then_inc(osum_done, 1)

        @block.scalar
        def _(act):
            act.preload_act_table_set("natural_log_exp_and_others")
            for q in qs:
                act.activation(ors[q][:, :], o_sb[:, q, :], ACT.Square).then_inc(o_squared, 1)
            for q in qs:
                act.wait_ge(dev_done, q + 1)
                act.activation(rs[q], dev[q], ACT.Square).then_inc(dev_squared, 1)
            act.wait_ge(eps_set, 2)
            for q in qs:
                act.wait_ge(var_done, q + 1)
                act.activation(rs[q], sums[q][:, :], ACT.Ln, scale=1.0 / HD, bias=eps[:, 0:1]).then_inc(rs_ln, 1)
                act.wait_ge(rs_ln, q + 1)
                act.activation(rs[q], rs[q], ACT.Exp, scale=-0.5).then_inc(rs_done, 1)
            for q in qs:
                act.wait_ge(osum_done, q + 1)
                act.activation(ors[q][:, :], sums[q][:, :], ACT.Ln, scale=1.0 / HD, bias=eps[:, 1:2]).then_inc(ors_ln, 1)
                act.wait_ge(ors_ln, q + 1)
                act.activation(ors[q][:, :], ors[q][:, :], ACT.Exp, scale=-0.5).then_inc(ors_done, 1)

        @block.vector
        def _(dve):
            dve.memset(eps[:, 0:1], GN_EPS).then_inc(eps_set, 1)
            dve.memset(eps[:, 1:2], RMS_EPS).then_inc(eps_set, 1)
            for q in qs:
                dve.wait_ge(mean_done, q + 1)
                dve.scalar_tensor_tensor(dev[q], sums[q][:, :], -1.0 / HD, y_sb[:, q, CH:TPAD],
                                         ALU.mult, ALU.add).then_inc(dev_done, 1)
            for k in range(KD):
                dve.tensor_copy(wh[:, k, :], w_raw[:, k, :]).then_inc(w_high, 1)
            dve.wait_ge(vec_loaded, 16)
            for q in qs:
                gain, bias = (vec[:, q, j:j + 1] for j in (V_LG, V_LB))
                dve.wait_ge(rs_done, q + 1)
                dve.scalar_tensor_tensor(dev[q], dev[q], gain, rs[q], ALU.mult, ALU.mult).then_inc(scaled, 1)
                dve.wait_ge(scaled, q + 1)
                dve.wait_ge(loaded[q % 2], 32 * (q // 2 + 1))
                dve.scalar_tensor_tensor(dev[q], dev[q], bias, bonus[q % 2][:, :], ALU.add, ALU.add).then_inc(with_bonus, 1)
                dve.wait_ge(with_bonus, q + 1)
                dve.tensor_tensor(y_sb[:, q, CH:TPAD], dev[q], gate[q % 2][:, :], ALU.mult).then_inc(gated, 1)
            for q in qs:
                dve.wait_ge(ors_done, q + 1)
                dve.scalar_tensor_tensor(o_sb[:, q, :], o_sb[:, q, :], vec[:, q, V_SG:V_SG + 1], ors[q][:, :],
                                         ALU.mult, ALU.mult).then_inc(o_scaled, 1)

        @block.gpsimd
        def _(pool):
            for k in range(KD):
                pool.wait_ge(w_high, k + 1)
                pool.tensor_tensor(wl[:, k, :], w_raw[:, k, :], wh[:, k, :].bitcast(F32),
                                   ALU.subtract).then_inc(w_low, 1)


def stage_out_proj(nc, y_sb, o_sb, wh, wl, x_dram, gain_row, gain_cols, ident, h_dram, mh, ml):
    with ExitStack() as ctx:
        m = Mem(nc, ctx, "oproj")
        yh = [m.sb(f"yh{s}", [P, KD, P], F32R) for s in range(2)]
        yl = [m.sb(f"yl{s}", [P, KD, P], F32R) for s in range(2)]
        h = [m.sb(f"h{s}", [P, D]) for s in range(2)]
        t = [m.sb(f"t{s}", [P, D]) for s in range(2)]
        xf = [m.sb(f"xf{s}", [P, KD, P]) for s in range(2)]
        gain_r = m.sb("gain_r", [P, D])
        gain_c = m.sb("gain_c", [P, KD])
        ss = [m.sb(f"ss{s}", [P, 2]) for s in range(2)]
        rs = [m.sb(f"rs{s}", [P, 2]) for s in range(2)]
        eps = m.sb("eps", [P, 1])
        acc = [m.ps(f"acc{s}", (P, D)) for s in range(2)]
        tp = [m.ps(f"tp{s}", (P, D)) for s in range(2)]
        x_loaded = [m.sem(f"x_loaded{s}") for s in range(2)]
        stored = [m.sem(f"stored{s}") for s in range(2)]
        gains_loaded, eps_set = m.sem("gains_loaded"), m.sem("eps_set")
        steps = lambda name, names: Steps(m.sem(name), names, back=2)
        y_high, y_low = steps("y_high", "y o"), steps("y_low", "y o")
        products, turned = steps("products", "all"), steps("turned", "all")
        A = steps("act_done", "sq ln rs hsq hln hrs")
        V = steps("vec_done", "norm h scaled")
        gained, high, low = steps("gained", "all"), steps("high", "all"), steps("low", "all")
        block = ctx.enter_context(nc.Block())

        def each(eng, split, project, turn):
            def call(step, i, j):
                step(i * 2 + j, j % 2, i * 2 * P + j * P)
            call(split, 0, 0)
            call(split, 0, 1)
            call(project, 0, 0)
            with eng.Fori(0, TOK_TILES // 2 - 1) as i:
                for j in range(2):
                    call(split, i, j + 2)
                    call(project, i, j + 1)
                    call(turn, i, j)
            call(project, TOK_TILES // 2 - 1, 1)
            call(turn, TOK_TILES // 2 - 1, 0)
            call(turn, TOK_TILES // 2 - 1, 1)

        nothing = lambda n, s, c0: None

        @block.sync
        def _(sp):
            sp.dma_start(gain_r[:, :], gain_row.broadcast_to((P, D))).then_inc(gains_loaded, 16)
            sp.dma_start(gain_c[:, :], gain_cols).then_inc(gains_loaded, 16)
            for s in range(2):
                sp.dma_start(h[s][:, :], x_dram[s * P:(s + 1) * P, :]).then_inc(x_loaded[s], 16)

            def store(n, s, row):
                V.wait(sp, n, "h")
                stand_alone(sp)
                sp.dma_start(h_dram[ds(row, P), :], h[s][:, :]).then_inc(stored[s], 16)

            with sp.Fori(0, TOK_TILES // 2 - 1) as i:
                for s in range(2):
                    store(i * 2 + s, s, i * 2 * P + s * P)
                    V.wait(sp, i * 2 + s, "scaled")
                    sp.wait_ge(stored[s], i * 16 + 16)
                    stand_alone(sp)
                    sp.dma_start(h[s][:, :], x_dram[ds(i * 2 * P + (s + 2) * P, P), :]).then_inc(x_loaded[s], 16)
            for s in range(2):
                store(TOK_TILES - 2 + s, s, (TOK_TILES - 2 + s) * P)
            for s in range(2):
                sp.wait_ge(stored[s], 16 * (TOK_TILES // 2))

        @block.scalar
        def _(act):
            for x in (y_high, A, high):
                x.open(act)
            act.preload_act_table_set("natural_log_exp_and_others")
            act.wait_ge(eps_set, 1)

            def split(n, s, c0):
                products.wait(act, n, "all", 2)
                y_high.done(act.activation(yh[s][:, 0:PAIRS, :], y_sb[:, :, ds(c0 + CH, P)], ACT.Copy), "y")
                y_high.done(act.activation(yh[s][:, PAIRS:, :], o_sb[:, :, ds(c0, P)], ACT.Copy), "o")

            def inverse_root(n, s, j, before, names):
                A.wait(act, n, before)
                A.done(act.activation(rs[s][:, j:j + 1], ss[s][:, j:j + 1], ACT.Ln, scale=1.0 / D, bias=eps[:, :]), names[0])
                A.wait(act, n, names[0])
                A.done(act.activation(rs[s][:, j:j + 1], rs[s][:, j:j + 1], ACT.Exp, scale=-0.5), names[1])

            def project(n, s, c0):
                products.wait(act, n, "all")
                turned.wait(act, n, "all", 2)
                A.done(act.activation(t[s][:, :], acc[s][:, :], ACT.Square, accum_out=ss[s][:, 0:1]), "sq")
                inverse_root(n, s, 0, "sq", ("ln", "rs"))
                V.wait(act, n, "h")
                A.done(act.activation(t[s][:, :], h[s][:, :], ACT.Square, accum_out=ss[s][:, 1:2]), "hsq")
                inverse_root(n, s, 1, "hsq", ("hln", "hrs"))

            def turn(n, s, c0):
                gained.wait(act, n, "all")
                high.done(act.activation(mh[:, :, ds(c0, P)], xf[s][:, :, :], ACT.Copy), "all")
            each(act, split, project, turn)

        @block.gpsimd
        def _(pool):
            for x in (y_low, low):
                x.open(pool)

            def split(n, s, c0):
                y_high.wait(pool, n, "o")
                stand_alone(pool)
                y_low.done(pool.tensor_tensor(yl[s][:, 0:PAIRS, :], y_sb[:, :, ds(c0 + CH, P)],
                                              yh[s][:, 0:PAIRS, :].bitcast(F32), ALU.subtract), "y")
                y_low.done(pool.tensor_tensor(yl[s][:, PAIRS:, :], o_sb[:, :, ds(c0, P)],
                                              yh[s][:, PAIRS:, :].bitcast(F32), ALU.subtract), "o")

            def turn(n, s, c0):
                high.wait(pool, n, "all")
                stand_alone(pool)
                low.done(pool.tensor_tensor(ml[:, :, ds(c0, P)], xf[s][:, :, :], mh[:, :, ds(c0, P)].bitcast(F32),
                                            ALU.subtract), "all")
            each(pool, split, nothing, turn)

        @block.vector
        def _(dve):
            for x in (V, gained):
                x.open(dve)
            dve.memset(eps[:, :], RMS_EPS).then_inc(eps_set, 1)
            dve.wait_ge(gains_loaded, 32)

            def project(n, s, c0):
                A.wait(dve, n, "rs")
                V.done(dve.scalar_tensor_tensor(t[s][:, :], acc[s][:, :], rs[s][:, 0:1], gain_r[:, :], ALU.mult, ALU.mult), "norm")
                V.wait(dve, n, "norm")
                dve.wait_ge(x_loaded[s], (n - s) * 8 + 16)
                V.done(dve.tensor_tensor(h[s][:, :], h[s][:, :], t[s][:, :], ALU.add), "h")
                A.wait(dve, n, "hrs")
                V.wait(dve, n, "h")
                V.done(dve.tensor_scalar(t[s][:, :], h[s][:, :], rs[s][:, 1:2], None, ALU.mult), "scaled")

            def turn(n, s, c0):
                turned.wait(dve, n, "all")
                low.wait(dve, n, "all", 2)
                gained.done(dve.tensor_tensor(xf[s][:, :, :], tp[s][:, :].rearrange("p (k c) -> p k c", k=KD),
                                              gain_c[:, :].unsqueeze(2).broadcast_to((P, KD, P)), ALU.mult), "all")
            each(dve, nothing, project, turn)

        @block.tensor
        def _(pe):
            for x in (products, turned):
                x.open(pe)

            def project(n, s, c0):
                y_low.wait(pe, n, "o")
                V.wait(pe, n, "norm", 2)
                for g in range(2):
                    c = slice(g * 512, g * 512 + 512)
                    for k in range(KD):
                        for j, (yy, w) in enumerate([(yh, wh), (yh, wl), (yl, wh)]):
                            last = pe.matmul(acc[s][:, c], yy[s][:, k, :], w[:, k, c],
                                             start=(k == 0 and j == 0), stop=(k == KD - 1 and j == 2))
                products.done(last, "all")

            def turn(n, s, c0):
                V.wait(pe, n, "scaled")
                gained.wait(pe, n, "all", 2)
                for k in range(KD):
                    last = pe.transpose(tp[s][:, k * P:(k + 1) * P], t[s][:, k * P:(k + 1) * P], ident[:, :])
                turned.done(last, "all")
            each(pe, nothing, project, turn)


FC = 2
FF_CHUNKS = FF_TILES // FC


def stage_ffn(nc, mh, ml, w_up, w_down, acc):
    with ExitStack() as ctx:
        m = Mem(nc, ctx, "ffn")
        raw_u = [m.sb(f"raw_u{s}", [P, KD, P]) for s in range(2)]
        raw_d = [m.sb(f"raw_d{s}", [P, D]) for s in range(2)]
        wuh = [m.sb(f"wuh{s}", [P, KD, P], F32R) for s in range(2)]
        wul = [m.sb(f"wul{s}", [P, KD, P], F32R) for s in range(2)]
        wdh = [m.sb(f"wdh{s}", [P, FC, D], F32R) for s in range(2)]
        wdl = [m.sb(f"wdl{s}", [P, FC, D], F32R) for s in range(2)]
        uh = [m.sb(f"uh{s}", [P, FC, SEQ], F32R) for s in range(2)]
        ul = [m.sb(f"ul{s}", [P, FC, SEQ], F32R) for s in range(2)]
        relu = [m.sb(f"relu{s}", [P, 512]) for s in range(2)]
        ups = [m.ps(f"up{b}") for b in range(4)]
        downs = [m.ps(f"down{b}") for b in range(4)]
        u_loaded = [m.sem(f"u_loaded{s}") for s in range(2)]
        d_loaded = [m.sem(f"d_loaded{s}") for s in range(2)]
        zeroed = m.sem("zeroed")
        wu_high, wu_low, wd_high, wd_low = m.sem("wu_high"), m.sem("wu_low"), m.sem("wd_high"), m.sem("wd_low")
        up_done, relu_done, squared, u_high, u_low = (m.sem(x) for x in ("up_done", "relu_done", "squared", "u_high", "u_low"))
        down_done, added = m.sem("down_done"), m.sem("added")
        block = ctx.enter_context(nc.Block())
        HALVES = 2 * FC
        OUTS = TOK_TILES * 2

        def first(c):
            return isinstance(c, int) and c == 0

        def chunks(eng, up, down):
            up(0, 0)
            up(1, 1)
            down(0, 0)
            with eng.Fori(0, FF_CHUNKS // 2 - 1) as i:
                up(i * 2 + 2, 0)
                down(i * 2 + 1, 1)
                up(i * 2 + 3, 1)
                down(i * 2 + 2, 0)
            down(FF_CHUNKS - 1, 1)

        @block.sync
        def _(sp):
            with sp.Fori(0, FF_TILES // 2) as i:
                for s in range(2):
                    sp.wait_ge(wu_low, i * 2)
                    sp.dma_start(raw_u[s][:, :, :], w_up[ds(i * 2 + s, 1)].squeeze(0)).then_inc(u_loaded[s], 16)
                    sp.wait_ge(wd_low, i * 2)
                    sp.dma_start(raw_d[s][:, :], w_down[ds(i * 2 + s, 1)].squeeze(0)).then_inc(d_loaded[s], 16)

        @block.scalar
        def _(act):
            def up(c, s):
                for f in range(FC):
                    act.wait_ge(u_loaded[f], c * 16 + 16)
                    if not first(c):
                        act.wait_ge(up_done, c * HALVES + (2 * f - 2))
                    act.activation(wuh[f][:, :, :], raw_u[f][:, :, :], ACT.Copy).then_inc(wu_high, 1)
                    act.wait_ge(d_loaded[f], c * 16 + 16)
                    if not first(c):
                        act.wait_ge(down_done, (c - 1) * OUTS)
                    act.activation(wdh[s][:, f, :], raw_d[f][:, :], ACT.Copy).then_inc(wd_high, 1)
                for j in range(HALVES):
                    f, half = divmod(j, 2)
                    cols = slice(half * 512, half * 512 + 512)
                    act.wait_ge(up_done, c * HALVES + (j + 1))
                    if not (first(c) and j < 2):
                        act.wait_ge(u_low, c * HALVES + (j - 1))
                    act.activation(relu[j % 2][:, :], ups[j][:, :], ACT.Relu).then_inc(relu_done, 1)
                    act.wait_ge(squared, c * HALVES + (j + 1))
                    act.activation(uh[s][:, f, cols], relu[j % 2][:, :], ACT.Copy).then_inc(u_high, 1)
            chunks(act, up, lambda c, s: None)

        @block.gpsimd
        def _(pool):
            pool.memset(acc[:, :, :], 0.0).then_inc(zeroed, 1)

            def up(c, s):
                for j in range(HALVES):
                    f, half = divmod(j, 2)
                    cols = slice(half * 512, half * 512 + 512)
                    pool.wait_ge(u_high, c * HALVES + (j + 1))
                    pool.tensor_tensor(ul[s][:, f, cols], relu[j % 2][:, :], uh[s][:, f, cols].bitcast(F32),
                                       ALU.subtract).then_inc(u_low, 1)
            chunks(pool, up, lambda c, s: None)

        @block.vector
        def _(dve):
            dve.wait_ge(zeroed, 1)

            def up(c, s):
                for f in range(FC):
                    dve.wait_ge(wu_high, c * FC + (f + 1))
                    dve.tensor_tensor(wul[f][:, :, :], raw_u[f][:, :, :], wuh[f][:, :, :].bitcast(F32), ALU.subtract).then_inc(wu_low, 1)
                    dve.wait_ge(wd_high, c * FC + (f + 1))
                    dve.tensor_tensor(wdl[s][:, f, :], raw_d[f][:, :], wdh[s][:, f, :].bitcast(F32), ALU.subtract).then_inc(wd_low, 1)
                for j in range(HALVES):
                    dve.wait_ge(relu_done, c * HALVES + (j + 1))
                    dve.tensor_tensor(relu[j % 2][:, :], relu[j % 2][:, :], relu[j % 2][:, :], ALU.mult).then_inc(squared, 1)

            def down(c, s):
                for t in range(TOK_TILES):
                    for g in range(2):
                        o = 2 * t + g
                        sl = acc[:, t, g * 512:g * 512 + 512]
                        dve.wait_ge(down_done, c * OUTS + (o + 1))
                        dve.wait_ge(added, c * OUTS)
                        dve.tensor_tensor(sl, sl, downs[o % 4][:, :], ALU.add).then_inc(added, 1)
            chunks(dve, up, down)

        @block.tensor
        def _(pe):
            def up(c, s):
                for j in range(HALVES):
                    f, half = divmod(j, 2)
                    pe.wait_ge(wu_low, c * FC + (f + 1))
                    if not first(c):
                        pe.wait_ge(relu_done, (c - 1) * HALVES + (j + 1))
                    cols = slice(half * 512, half * 512 + 512)
                    for k in range(KD):
                        for jj, (w, xx) in enumerate([(wuh, mh), (wuh, ml), (wul, mh)]):
                            last = pe.matmul(ups[j][:, :], w[f][:, k, :], xx[:, k, cols],
                                             start=(k == 0 and jj == 0), stop=(k == KD - 1 and jj == 2))
                    last.then_inc(up_done, 1)

            def down(c, s):
                pe.wait_ge(wd_low, c * FC + FC)
                pe.wait_ge(u_low, c * HALVES + HALVES)
                for t in range(TOK_TILES):
                    for g in range(2):
                        o = 2 * t + g
                        if not (first(c) and o < 4):
                            pe.wait_ge(added, c * OUTS + (o - 3))
                        for f in range(FC):
                            for jj, (u, w) in enumerate([(uh, wdh), (uh, wdl), (ul, wdh)]):
                                last = pe.matmul(downs[o % 4][:, :], u[s][:, f, t * P:(t + 1) * P],
                                                 w[s][:, f, g * 512:g * 512 + 512],
                                                 start=(f == 0 and jj == 0), stop=(f == FC - 1 and jj == 2))
                        last.then_inc(down_done, 1)
            chunks(pe, up, down)


def stage_finish(nc, acc, h_dram, gain_row, out_dram):
    with ExitStack() as ctx:
        m = Mem(nc, ctx, "fin")
        gain = m.sb("gain", [P, D])
        square = m.sb("square", [P, D])
        h = [m.sb(f"h{s}", [P, D]) for s in range(2)]
        o = [m.sb(f"o{s}", [P, D]) for s in range(2)]
        ss = m.sb("ss", [P, TOK_TILES])
        root = m.sb("root", [P, TOK_TILES])
        eps = m.sb("eps", [P, 1])
        loaded = [m.sem(f"loaded{s}") for s in range(2)]
        stored = [m.sem(f"stored{s}") for s in range(2)]
        gain_loaded, init, squared, rooted, inverted, normed, added = (m.sem(x) for x in (
            "gain_loaded", "init", "squared", "rooted", "inverted", "normed", "added"))
        block = ctx.enter_context(nc.Block())

        @block.sync
        def _(sp):
            sp.dma_start(gain[:, :], gain_row.broadcast_to((P, D))).then_inc(gain_loaded, 16)
            for s in range(2):
                sp.dma_start(h[s][:, :], h_dram[s * P:(s + 1) * P, :]).then_inc(loaded[s], 16)
            for t in range(TOK_TILES):
                sp.wait_ge(added, t + 1)
                sp.dma_start(out_dram[t * P:(t + 1) * P, :], o[t % 2][:, :]).then_inc(stored[t % 2], 16)
                if t + 2 < TOK_TILES:
                    sp.dma_start(h[t % 2][:, :], h_dram[(t + 2) * P:(t + 3) * P, :]).then_inc(loaded[t % 2], 16)
            for s in range(2):
                sp.wait_ge(stored[s], 16 * (TOK_TILES // 2))

        @block.scalar
        def _(act):
            act.wait_ge(init, 1)
            for t in range(TOK_TILES):
                act.activation(square[:, :], acc[:, t, :], ACT.Square, accum_out=ss[:, t:t + 1]).then_inc(squared, 1)
                act.wait_ge(squared, t + 1)
                act.activation(root[:, t:t + 1], ss[:, t:t + 1], ACT.Sqrt, scale=1.0 / D, bias=eps[:, :]).then_inc(rooted, 1)

        @block.vector
        def _(dve):
            dve.memset(eps[:, :], RMS_EPS).then_inc(init, 1)
            dve.wait_ge(gain_loaded, 16)
            for t in range(TOK_TILES):
                dve.wait_ge(rooted, t + 1)
                dve.reciprocal(root[:, t:t + 1], root[:, t:t + 1]).then_inc(inverted, 1)
                dve.wait_ge(inverted, t + 1)
                if t >= 2:
                    dve.wait_ge(stored[t % 2], 16 * (t // 2))
                dve.scalar_tensor_tensor(o[t % 2][:, :], acc[:, t, :], root[:, t:t + 1], gain[:, :], ALU.mult, ALU.mult).then_inc(normed, 1)
                dve.wait_ge(normed, t + 1)
                dve.wait_ge(loaded[t % 2], 16 * (t // 2 + 1))
                dve.tensor_tensor(o[t % 2][:, :], o[t % 2][:, :], h[t % 2][:, :], ALU.add).then_inc(added, 1)


def build(nc, x, meta, w_in, w_out, w_up, w_down, g_pre_mix, g_pre_ffn, g_post_mix, g_post_ffn,
          rwkv_vecs, mu_low, head_vecs, w_decay_up, w_a_up, w_g_up, out):
    p_dram = nc.dram_tensor("p_scratch", [IN_TILES, P, TPAD], F32, kind="Internal").ap()
    chunk_dram = nc.dram_tensor("chunk_scratch", [PAIRS, CHUNKS, P, 5 * CH], F32, kind="Internal").ap()
    gate_dram = nc.dram_tensor("gate_scratch", [PAIRS, P, SEQ], F32, kind="Internal").ap()
    bonus_dram = nc.dram_tensor("bonus_scratch", [PAIRS, P, SEQ], F32, kind="Internal").ap()
    h_dram = nc.dram_tensor("h_scratch", [SEQ, D], F32, kind="Internal").ap()
    with ExitStack() as whole:
        g = Mem(nc, whole, "all")
        ident = g.sb("ident", [P, P])
        ones_bd = g.sb("ones_bd", [P, P])
        pc = g.sb("pc", [P, PAIRS, CHUNKS])
        stage_constants(nc, ident, ones_bd)
        with ExitStack() as c:
            m = Mem(nc, c, "xn")
            xh, xl = m.sb("xh", [P, KD, T], F32R), m.sb("xl", [P, KD, T], F32R)
            stage_norm_transpose(nc, "pre", lambda row: x[ds(row, P), :], meta, g_pre_mix, ident, xh, xl)
            stage_in_proj(nc, w_in, p_dram, xh, xl)
        stage_rwkv_prep(nc, p_dram, rwkv_vecs, mu_low, w_decay_up, w_a_up, w_g_up, chunk_dram, gate_dram,
                        bonus_dram, pc, ones_bd)
        with ExitStack() as c:
            m = Mem(nc, c, "mixed")
            y_sb, o_sb = m.sb("y", [P, PAIRS, TPAD], side="right"), m.sb("o", [P, PAIRS, SEQ], side="right")
            with ExitStack() as c2:
                w_raw = Mem(nc, c2, "wout").sb("raw", [P, KD, D])
                with ExitStack() as c3:
                    masks = Mem(nc, c3, "maskm").sb("masks", [P, N_MASKS, P])
                    stage_rwkv_masks(nc, masks)
                    stage_mix(nc, chunk_dram, p_dram, masks, ident, pc, y_sb, o_sb, w_out, w_raw)
                wh, wl = m.sb("wh", [P, KD, D], F32R, side="right"), m.sb("wl", [P, KD, D], F32R, side="right")
                stage_post_heads(nc, y_sb, o_sb, head_vecs, gate_dram, bonus_dram, ones_bd, w_raw, wh, wl)
            mh, ml = g.sb("mh", [P, KD, SEQ], F32R), g.sb("ml", [P, KD, SEQ], F32R)
            stage_out_proj(nc, y_sb, o_sb, wh, wl, x, g_post_mix, g_pre_ffn, ident, h_dram, mh, ml)
        acc = g.sb("acc", [P, TOK_TILES, D])
        stage_ffn(nc, mh, ml, w_up, w_down, acc)
        stage_finish(nc, acc, h_dram, g_post_ffn, out)


def kernel(**inputs):
    import numpy as np
    import concourse.bacc as bacc
    from concourse.bass_utils import run_bass_kernel_spmd

    get = lambda name: np.asarray(inputs[name])
    by_tile = lambda a: np.ascontiguousarray(a.reshape(-1, P).T)
    by_pair = lambda *vs: np.ascontiguousarray(np.stack([v.reshape(PAIRS, P) for v in vs], axis=-1))
    mu = get("tshift_mu")[0]
    arrays = {
        "x": get("x")[0], "meta": get("meta_tokens"),
        "w_in": get("w_in")[0].reshape(KD, P, IN_TILES, P).transpose(2, 1, 0, 3),
        "w_out": get("w_out")[0].reshape(KD, P, D),
        "w_up": get("w_ffn_up")[0].reshape(KD, P, FF_TILES, P).transpose(2, 1, 0, 3),
        "w_down": get("w_ffn_down")[0].reshape(FF_TILES, P, D),
        "g_pre_mix": by_tile(get("g_pre_mix")[0]), "g_pre_ffn": by_tile(get("g_pre_ffn")[0]),
        "g_post_mix": get("g_post_mix"), "g_post_ffn": get("g_post_ffn"),
        "rwkv_vecs": by_pair(mu[0:RW], mu[RW:2 * RW], mu[2 * RW:3 * RW], get("decay_bias")[0], get("a_bias")[0],
                             get("k_k")[0], get("k_a")[0], get("r_k")[0].reshape(-1)),
        "mu_low": by_tile(mu[3 * RW:]),
        "head_vecs": by_pair(get("lnx_gain")[0], get("lnx_bias")[0], get("sb_out_gain")[0]).transpose(1, 0, 2),
        "w_decay_up": get("w_decay_up")[0], "w_a_up": get("w_a_up")[0], "w_g_up": get("w_g_up")[0],
    }
    arrays = {name: np.ascontiguousarray(a) for name, a in arrays.items()}
    nc = bacc.Bacc("TRN2", target_bir_lowering=False, num_devices=1)
    args = {name: nc.dram_tensor(f"in_{name}", a.shape, mybir.dt.from_np(a.dtype), kind="ExternalInput").ap()
            for name, a in arrays.items()}
    args["out"] = nc.dram_tensor("out", (SEQ, D), F32, kind="ExternalOutput").ap()
    build(nc, **args)
    r = run_bass_kernel_spmd(nc, [{f"in_{name}": a for name, a in arrays.items()}], core_ids=[0])
    return r.results[0]["out"].reshape(1, SEQ, D)
```

```python
import concourse.bass as bass
from concourse import mybir
from contextlib import ExitStack

F32 = mybir.dt.float32
F32R = mybir.dt.float32r
ALU = mybir.AluOpType
ACT = mybir.ActivationFunctionType
ds = bass.ds

P = 128
D = 1024
KD = D // P
META = 16
SEQ = 1024
T = META + SEQ
HD = 64
RW = 512
PAIRS = RW // P
CH = 64
TPAD = 1088
PAD = TPAD - T
CHUNKS = TPAD // CH
IN_TILES = 26
FF = 4 * D
FF_TILES = FF // P
TOK_TILES = SEQ // P
RMS_EPS = 1e-6
GN_EPS = 1e-5 * HD
TOK_GROUPS = [(0, 348), (348, 346), (694, 346)]


class Mem:

    def __init__(self, nc, ctx, stage):
        self.nc, self.ctx, self.stage = nc, ctx, stage

    def sb(self, name, shape, dt=F32, side="left"):
        return self.ctx.enter_context(self.nc.sbuf_tensor(f"{self.stage}_{name}", shape, dt, side=side))

    def ps(self, name, shape=(P, 512)):
        return self.ctx.enter_context(self.nc.psum_tensor(f"{self.stage}_{name}", list(shape), F32))

    def sem(self, name):
        return self.ctx.enter_context(self.nc.semaphore(f"{self.stage}_{name}"))


def stage_constants(nc, ident, ones_bd):
    with ExitStack() as ctx:
        m = Mem(nc, ctx, "const")
        filled, zeroed, done = m.sem("filled"), m.sem("zeroed"), m.sem("done")
        block = ctx.enter_context(nc.Block())

        @block.gpsimd
        def _(pool):
            pool.memset(ident[:, :], 0.0).then_inc(filled, 1)
            pool.wait_ge(filled, 1)
            pool.affine_select(out=ident[:, :], in_=ident[:, :], compare_op=ALU.not_equal, fill=1.0,
                               base=0, pattern=[[-1, P]], channel_multiplier=1).then_inc(done, 1)

        @block.vector
        def _(dve):
            dve.memset(ones_bd[:, :], 0.0).then_inc(zeroed, 1)
            dve.wait_ge(zeroed, 1)
            for h in range(2):
                half = ones_bd[h * HD:(h + 1) * HD, h * HD:(h + 1) * HD]
                dve.memset(half, 1.0).then_inc(done, 1)
            dve.wait_ge(done, 3)


def stage_norm_transpose(nc, x_dram, meta, gain_cols, ident, xh, xl, w_in, w_raw):
    tiles = [(0, META)] + [(META + t * P, P) for t in range(TOK_TILES)]
    N = len(tiles)
    with ExitStack() as ctx:
        m = Mem(nc, ctx, "pre")
        x = [m.sb(f"x{n}", [P, D]) for n in range(N)]
        xs = [m.sb(f"xs{s}", [P, D]) for s in range(2)]
        xf = [m.sb(f"xf{s}", [P, KD, P]) for s in range(2)]
        square = m.sb("square", [P, D])
        sumsq = m.sb("sumsq", [P, N])
        rs = m.sb("rs", [P, N])
        gain = m.sb("gain", [P, KD])
        eps = m.sb("eps", [P, 1])
        tp = [m.ps(f"tp{s}", (P, D)) for s in range(2)]
        loaded = [m.sem(f"loaded{n}") for n in range(N)]
        gain_loaded, w_loaded = m.sem("gain_loaded"), m.sem("w_loaded")
        eps_set, squared, logged, rooted, scaled, turned, gained, high, low = (m.sem(name) for name in (
            "eps_set", "squared", "logged", "rooted", "scaled", "turned", "gained", "high", "low"))
        block = ctx.enter_context(nc.Block())

        def each(front, back, ahead):
            for n in range(N + ahead):
                if n < N:
                    front(n, *tiles[n])
                if n >= ahead:
                    back(n - ahead, *tiles[n - ahead])

        @block.sync
        def _(sp):
            for n, (c, rows) in enumerate(tiles):
                src = meta if n == 0 else x_dram[(n - 1) * P:n * P, :]
                sp.dma_start(x[n][0:rows, :], src).then_inc(loaded[n], 16)
                if n == 0:
                    sp.dma_start(gain[:, :], gain_cols).then_inc(gain_loaded, 16)
            for s in range(2):
                sp.dma_start(w_raw[s][:, :, :], w_in[s]).then_inc(w_loaded, 16)
            sp.wait_ge(w_loaded, 32)

        @block.scalar
        def _(act):
            act.preload_act_table_set("natural_log_exp_and_others")
            act.wait_ge(eps_set, 1)

            def front(n, c, rows):
                act.wait_ge(loaded[n], 16)
                if n:
                    act.wait_ge(squared, n)
                act.activation(square[0:rows, :], x[n][0:rows, :], ACT.Square,
                               accum_out=sumsq[0:rows, n:n + 1]).then_inc(squared, 1)
                act.wait_ge(squared, n + 1)
                act.activation(rs[0:rows, n:n + 1], sumsq[0:rows, n:n + 1], ACT.Ln,
                               scale=1.0 / D, bias=eps[0:rows, :]).then_inc(logged, 1)
                act.wait_ge(logged, n + 1)
                act.activation(rs[0:rows, n:n + 1], rs[0:rows, n:n + 1], ACT.Exp, scale=-0.5).then_inc(rooted, 1)

            def back(n, c, rows):
                act.wait_ge(gained, n + 1)
                act.activation(xh[:, :, c:c + rows], xf[n % 2][:, :, 0:rows], ACT.Copy).then_inc(high, 1)
            each(front, back, 3)

        @block.vector
        def _(dve):
            dve.memset(eps[:, :], RMS_EPS).then_inc(eps_set, 1)

            def front(n, c, rows):
                dve.wait_ge(rooted, n + 1)
                if n >= 2:
                    dve.wait_ge(turned, n - 1)
                dve.tensor_scalar(xs[n % 2][0:rows, :], x[n][0:rows, :], rs[0:rows, n:n + 1], None,
                                  ALU.mult).then_inc(scaled, 1)

            def back(n, c, rows):
                if n == 0:
                    dve.wait_ge(gain_loaded, 16)
                dve.wait_ge(turned, n + 1)
                if n >= 2:
                    dve.wait_ge(low, n - 1)
                half = tp[n % 2][:, :].rearrange("p (k c) -> p k c", k=KD)[:, :, 0:rows]
                g = gain[:, :].unsqueeze(2).broadcast_to((P, KD, rows))
                dve.tensor_tensor(xf[n % 2][:, :, 0:rows], half, g, ALU.mult).then_inc(gained, 1)
            each(front, back, 1)

        @block.tensor
        def _(pe):
            for n, (c, rows) in enumerate(tiles):
                pe.wait_ge(scaled, n + 1)
                if n >= 2:
                    pe.wait_ge(gained, n - 1)
                for k in range(KD):
                    last = pe.transpose(tp[n % 2][:, k * P:k * P + rows], xs[n % 2][0:rows, k * P:(k + 1) * P],
                                        ident[0:rows, 0:rows])
                last.then_inc(turned, 1)

        @block.gpsimd
        def _(pool):
            for n, (c, rows) in enumerate(tiles):
                pool.wait_ge(high, n + 1)
                pool.tensor_tensor(xl[:, :, c:c + rows], xf[n % 2][:, :, 0:rows],
                                   xh[:, :, c:c + rows].bitcast(F32), ALU.subtract).then_inc(low, 1)
import math

DECAY_C = math.exp(-0.5)
PGROUPS = [(0, 364), (364, 362), (726, 362)]
FIRST_TILES, LAP_TILES, LAP_PLACES = 6, 5, 6
P_R, P_K, P_V = 0, 1, 2
P_LOW = 3
P_SK, P_SQ = 9, 10
P_SV = 23
P_PLACES = P_SV + LAP_PLACES
FIRST_PLACES = [P_LOW, P_LOW + 1, P_R, P_K, P_V, P_SV]
XGROUPS = [(CH, 512), (CH + 512, 512)]
LEVELS = [2, 4, 8, 16, 32]
M_N, M_K, M_R, M_L1T, M_LEVEL = 0, 1, 2, 3, 4
N_MASKS = M_LEVEL + len(LEVELS)
V_MU, V_DB, V_AB, V_KK, V_KA, V_RK = 0, 3, 4, 5, 6, 7
NV = 8
F_A, F_R, F_B, F_K, F_V = range(5)


def stand_alone(eng):
    eng.nop(nofuse=True)


class Steps:

    def __init__(self, sem, names, back=1):
        self.sem, self.names, self.back, self.seen = sem, names.split(), back, 0

    def open(self, eng):
        eng.sem_inc(self.sem, self.back * len(self.names))

    def at(self, i, name, laps_ago=0):
        assert 0 <= laps_ago <= self.back
        return i * len(self.names) + ((self.back - laps_ago) * len(self.names) + self.names.index(name) + 1)

    def done(self, ins, name):
        assert self.names[self.seen % len(self.names)] == name, (name, self.names[self.seen % len(self.names)])
        self.seen += 1
        ins.then_inc(self.sem, 1)

    def wait(self, eng, i, name, laps_ago=0):
        eng.wait_ge(self.sem, self.at(i, name, laps_ago))

    def wait_lap_before(self, eng, i):
        self.wait(eng, i, self.names[-1], 1)


def w_in_order():
    r, k, v, low, sq, sk, sv = 0, PAIRS, 2 * PAIRS, 3 * PAIRS, 3 * PAIRS + 2, 4 * PAIRS + 2, 5 * PAIRS + 2
    order = [low, low + 1, r, k, v, sv]
    for q in range(PAIRS - 1):
        order += [r + q + 1, k + q + 1, v + q + 1, sk + q, sq + q]
    order += [sv + 1, sv + 2, sv + 3, sk + PAIRS - 1, sq + PAIRS - 1]
    return order + order[:2]


def side_by_side(slots, tiles, other):
    due = next(other)
    for slot in range(slots):
        while due is not None and due <= slot:
            due = next(other, None)
        next(tiles)
    assert due is None and next(tiles, None) is None


def scan_masks(pool, masks, step):
    pool.memset(masks[:, :, :], 1.0).then_inc(step, 1)
    pool.wait_ge(step, 1)
    count = [1]

    def select(view, pattern, base, mult, op=ALU.is_ge):
        pool.affine_select(out=view, in_=view, compare_op=op, fill=0.0, base=base, pattern=pattern,
                           channel_multiplier=mult).then_inc(step, 1)
        count[0] += 1
        pool.wait_ge(step, count[0])

    def heads(k):
        return masks[:, k, :].rearrange("p (h n) -> p h n", h=2)

    for k in (M_N, M_K, M_R):
        op = ALU.is_ge if k == M_R else ALU.is_gt
        for h in range(2):
            rows = slice(h * HD, (h + 1) * HD)
            v = masks[rows, k, :].rearrange("p (h n) -> p h n", h=2)
            select(v, [[0, 2], [1, CH]], 0, -1, op)
    select(heads(M_N), [[-CH, 2], [0, CH]], 0, 1)
    select(heads(M_N), [[CH, 2], [0, CH]], CH - 1, -1)
    select(masks[0:HD, M_K, 0:CH], [[0, CH]], -1, 0)
    select(masks[HD:P, M_K, CH:P], [[0, CH]], -1, 0)
    pairs2 = lambda k, b: masks[:, k, :].rearrange("p (j c) -> p j c", c=b)
    def block_diag(view, n, b):
        select(view, [[-b, n], [0, b]], 0, 1)
        select(view, [[b, n], [0, b]], b - 1, -1)
    block_diag(pairs2(M_L1T, 2), P // 2, 2)
    select(masks[:, M_L1T, :], [[1, P]], 0, -1, ALU.is_gt)
    for j, l in enumerate(LEVELS):
        k = M_LEVEL + j
        b = 2 * l
        v = pairs2(k, b)
        select(v, [[-b, P // b], [0, b]], -l, 1)
        select(v, [[b, P // b], [0, b]], b - 1, -1)
        select(v, [[0, P // b], [-1, b]], l - 1, 0)


def stage_in_proj(nc, w_in, raw, masks, p_dram, xh, xl, vecs, mu_low, w_decay_up, w_a_up, w_g_up, chunk_dram, gate_dram,
                  bonus_dram, pc, ones_bd):
    with ExitStack() as ctx:
        m = Mem(nc, ctx, "inproj")
        wh = [m.sb(f"wh{s}", [P, KD, P], F32R) for s in range(2)]
        wl = [m.sb(f"wl{s}", [P, KD, P], F32R) for s in range(2)]
        out = [m.sb(f"out{s}", [P, T]) for s in range(2)]
        acc = [m.ps(f"acc{g}") for g in range(3)]
        loaded = [m.sem(f"loaded{s}") for s in range(2)]
        stored = [m.sem(f"stored{s}") for s in range(2)]
        w_high, w_low = Steps(m.sem("w_high"), "all"), Steps(m.sem("w_low"), "all")
        group_done, group_read = Steps(m.sem("group_done"), "0 1 2", back=2), Steps(m.sem("group_read"), "0 1 2")
        rkv = m.sb("rkv", [P, 3, TPAD + 1])
        low = rkv
        mul = m.sb("mul", [P, 2])
        omul = m.sb("omul", [P, 2])
        tl = m.sb("tl", [P, TPAD])
        sg = m.sb("sg", [P, TPAD])
        wlow = m.sb("wlow", [P, 3, P])
        vec = m.sb("vec", [P, NV])
        omv = m.sb("omv", [P, 4])
        prev = [m.sb(f"prev{j}", [P, TPAD]) for j in range(3)]
        scale_k, rk, bv = prev[0], prev[1], prev[2]
        rinv = prev[0]
        r = m.sb("r", [P, TPAD])
        k = m.sb("k", [P, TPAD])
        sw = m.sb("sw", [P, TPAD])
        aa = m.sb("aa", [P, TPAD])
        gate = m.sb("gate", [P, SEQ])
        cum = m.sb("cum", [P, TPAD])
        grow = m.sb("grow", [P, CHUNKS, CH])
        fade = m.sb("fade", [P, CHUNKS, CH + 1])
        keep = m.sb("keep", [P, CHUNKS, CH])
        kk = m.sb("kk", [P, TPAD])
        sq = m.sb("sq", [P, TPAD])
        fields = m.sb("fields", [P, CHUNKS, 5, CH])
        tiny = m.sb("tiny", [P, 1])
        bank = [m.ps(f"bank{b}") for b in range(5)]
        init, low_loaded, lowp, lowa = m.sem("init"), m.sem("low_loaded"), m.sem("lowp"), m.sem("lowa")
        rkv_loaded, vec_loaded, left = m.sem("rkv_loaded"), m.sem("vec_loaded"), m.sem("left")
        V = Steps(m.sem("vec_done"), "om omka scan k r v t1 kmod rk bv0 bv1 A B")
        A = Steps(m.sem("act_done"), "w0 w1 w2 g0 g1 a0 a1 a2 fade grow pc sq ln0 ln1 ln2 rinv")
        G = Steps(m.sem("pool_done"), "p1 p0 p2 kk K kkn ka R")
        M = Steps(m.sem("mm_done"), "w0 w1 w2 g0 g1 a0 a1 a2 n0 n1 n2 b0 b1")
        masked = m.sem("masked")
        LEFT = 3 * 16
        block = ctx.enter_context(nc.Block())
        c3 = lambda t: t[:, :].rearrange("p (c n) -> p c n", n=CH)

        def program(eng, tile, before, prepare):
            def tiles(h, cs, places):
                for c, place in zip(cs, places):
                    yield from tile(h, c, place)
            side_by_side(3 * FIRST_TILES, tiles(0, range(FIRST_TILES), FIRST_PLACES), before())
            with eng.Fori(0, PAIRS // 2) as h:
                for u in range(2):
                    cs = range(FIRST_TILES + u * LAP_TILES, FIRST_TILES + (u + 1) * LAP_TILES)
                    places = [h * (2 * LAP_PLACES) + ((u + 1) * LAP_PLACES + j) for j in range(LAP_TILES)]
                    side_by_side(3 * LAP_TILES, tiles(h, cs, places), prepare(h, u))

        def number(h, c):
            return h * (2 * LAP_TILES) + c, c % 2, h * LAP_TILES + c // 2

        @block.sync
        def _(sp):
            def load_w(h, c):
                n, s, uses = number(h, c)
                src = w_in[n] if isinstance(n, int) else w_in[ds(n, 1)].squeeze(0)
                sp.dma_start(raw[s][:, :, :], src).then_inc(loaded[s], 16)

            def tile(h, c, place):
                n, s, uses = number(h, c)
                w_low.wait(sp, n, "all")
                stand_alone(sp)
                load_w(h, c + 2)
                for _ in range(3):
                    yield

            def before():
                yield 0
                sp.dma_start(mul[:, :], mu_low).then_inc(low_loaded, 16)
                sp.wait_ge(init, 6)
                yield 7
                for j in range(2):
                    sp.wait_ge(stored[j], 16)
                for j in range(2):
                    sp.dma_start(low[:, j, 1 + PAD:], p_dram[P_LOW + j, :, PAD:TPAD]).then_inc(low_loaded, 16)
                yield 17
                sp.wait_ge(lowp, 5)

            def prepare(h, u):
                i = h * 2 + u
                yield 0
                M.wait_lap_before(sp, i)
                stand_alone(sp)
                sp.dma_start(wlow[0:HD, 0, :], w_decay_up[:, ds(i * P, P)]).then_inc(vec_loaded, 16)
                sp.dma_start(wlow[HD:P, 1, :], w_a_up[:, ds(i * P, P)]).then_inc(vec_loaded, 16)
                sp.dma_start(wlow[:, 2, :], w_g_up[:, ds(i * P, P)]).then_inc(vec_loaded, 16)
                for steps in (V, G):
                    steps.wait_lap_before(sp, i)
                    stand_alone(sp)
                sp.dma_start(vec[:, :], vecs[ds(i, 1)].squeeze(0)).then_inc(vec_loaded, 16)
                for s in range(2):
                    sp.wait_ge(stored[s], h * (16 * LAP_TILES) + 16 * ((LAP_TILES * (u + 1) + 1 - s) // 2))
                    stand_alone(sp)
                for j, t in ((1, P_K), (0, P_R), (2, P_V)):
                    sp.dma_start(rkv[:, j, 1 + PAD:], p_dram[ds(i * LAP_PLACES + t, 1)].squeeze(0)[:, PAD:TPAD]).then_inc(rkv_loaded, 16)
                yield 11
                for steps in (V, G, A):
                    steps.wait(sp, i, steps.names[-1])
                    stand_alone(sp)
                sp.dma_start(chunk_dram[ds(i, 1)].squeeze(0).rearrange("c p f -> p c f"),
                             fields[:, :, :, :].rearrange("p c f n -> p c (f n)")).then_inc(left, 16)
                sp.dma_start(gate_dram[ds(i, 1)].squeeze(0), gate[:, :]).then_inc(left, 16)
                sp.dma_start(bonus_dram[ds(i, 1)].squeeze(0), bv[:, 0:SEQ]).then_inc(left, 16)
            sp.sem_inc(left, LEFT)
            for s in range(2):
                sp.sem_inc(loaded[s], 16)
            program(sp, tile, before, prepare)
            sp.wait_ge(left, (PAIRS + 1) * LEFT)
            for s in range(2):
                sp.wait_ge(stored[s], 16 * (IN_TILES // 2))
                sp.wait_ge(loaded[s], 16 * (IN_TILES // 2 + 1))

        @block.gpsimd
        def _(pool):
            G.open(pool)
            scan_masks(pool, masks, masked)

            def before():
                yield 10
                pool.wait_ge(low_loaded, 48)
                for j in range(2):
                    pool.tensor_scalar(prev[j][:, :], low[:, j, 0:TPAD], mul[:, j:j + 1], None, ALU.mult).then_inc(lowp, 1)
                yield 17
                pool.wait_ge(lowa, 2)

            def prepare(h, u):
                i = h * 2 + u
                yield 2
                pool.wait_ge(rkv_loaded, i * 48 + 48)
                V.wait(pool, i, "om")
                pool.wait_ge(left, i * LEFT + LEFT)
                stand_alone(pool)
                for j in (1, 0, 2):
                    G.done(pool.tensor_scalar(prev[j][:, :], rkv[:, j, 0:TPAD], vec[:, V_MU + j:V_MU + j + 1],
                                              None, ALU.mult), f"p{j}")
                V.wait(pool, i, "k")
                stand_alone(pool)
                G.done(pool.tensor_scalar(kk[:, :], k[:, :], vec[:, V_KK:V_KK + 1], None, ALU.mult), "kk")
                V.wait(pool, i, "kmod")
                A.wait(pool, i, "grow")
                G.done(pool.tensor_tensor(fields[:, :, F_K, :], c3(k), grow[:, :, :], ALU.mult), "K")
                A.wait(pool, i, "rinv")
                G.wait(pool, i, "kk")
                G.done(pool.tensor_tensor(kk[:, :], kk[:, :], rinv[:, :], ALU.mult), "kkn")
                G.wait(pool, i, "kkn")
                G.done(pool.tensor_tensor(sq[:, :], kk[:, :], aa[:, :], ALU.mult), "ka")
                G.done(pool.tensor_tensor(fields[:, :, F_R, :], c3(r), fade[:, :, 1:], ALU.mult), "R")

            def tile(h, c, place):
                for _ in range(3):
                    yield
            program(pool, tile, before, prepare)

        @block.scalar
        def _(act):
            for x in (w_high, group_read, A):
                x.open(act)

            def high(h, c):
                n, s, uses = number(h, c)
                act.wait_ge(loaded[s], uses * 16 + 16)
                group_done.wait(act, n, "2", 2)
                w_high.done(act.activation(wh[s][:, :, :], raw[s][:, :, :], ACT.Copy), "all")

            def tile(h, c, place):
                n, s, uses = number(h, c)
                high(h, c + 1)
                if not (isinstance(uses, int) and uses == 0):
                    act.wait_ge(stored[s], uses * 16)
                for g, (col, size) in enumerate(TOK_GROUPS):
                    group_done.wait(act, n, f"{g}")
                    group_read.done(act.activation(out[s][:, col:col + size], acc[g][:, 0:size], ACT.Copy), f"{g}")
                    if g == 2:
                        group_read.wait(act, n, "2")
                        dst = p_dram[place] if isinstance(place, int) else p_dram[ds(place, 1)].squeeze(0)
                        act.dma_start(dst[:, PAD:TPAD], out[s][:, :]).then_inc(stored[s], 16)
                    yield

            def before():
                yield 14
                act.wait_ge(lowp, 5)
                act.activation(tl[0:HD, :], tl[0:HD, :], ACT.Tanh).then_inc(lowa, 1)
                act.activation(sg[:, :], sg[:, :], ACT.Sigmoid).then_inc(lowa, 1)

            def prepare(h, u):
                i = h * 2 + u
                yield 1
                V.wait_lap_before(act, i)
                G.wait_lap_before(act, i)
                act.wait_ge(vec_loaded, i * 64 + 64)
                for g, (c, n) in enumerate(PGROUPS):
                    M.wait(act, i, f"w{g}")
                    A.done(act.activation(sw[:, c:c + n], bank[g][:, 0:n], ACT.Sigmoid, bias=vec[:, V_DB:V_DB + 1]), f"w{g}")
                yield 2
                act.wait_ge(left, i * LEFT + LEFT)
                for g, (c, n) in enumerate(XGROUPS):
                    M.wait(act, i, f"g{g}")
                    A.done(act.activation(gate[:, c - CH:c - CH + n], bank[3 + g][:, 0:n], ACT.Copy), f"g{g}")
                yield 3
                for g, (c, n) in enumerate(PGROUPS):
                    M.wait(act, i, f"a{g}")
                    A.done(act.activation(aa[:, c:c + n], bank[g][:, 0:n], ACT.Sigmoid, bias=vec[:, V_AB:V_AB + 1]), f"a{g}")
                yield 4
                V.wait(act, i, "scan")
                A.done(act.activation(fade[:, :, 1:], c3(cum), ACT.Exp, scale=-DECAY_C), "fade")
                A.done(act.activation(grow[:, :, :], c3(cum), ACT.Exp, scale=DECAY_C), "grow")
                A.wait(act, i, "fade")
                A.done(act.activation(pc[:, ds(i, 1), :].squeeze(1), fade[:, :, CH], ACT.Copy), "pc")
                yield 5
                G.wait(act, i, "kk")
                A.done(act.activation(sq[:, :], kk[:, :], ACT.Square), "sq")
                yield 7
                V.wait(act, i, "kmod")
                for g, (c, n) in enumerate(PGROUPS):
                    M.wait(act, i, f"n{g}")
                    A.done(act.activation(rinv[:, c:c + n], bank[g][:, 0:n], ACT.Ln, bias=tiny[:, :]), f"ln{g}")
                A.wait(act, i, "ln2")
                A.done(act.activation(rinv[:, :], rinv[:, :], ACT.Exp, scale=-0.5), "rinv")
            high(0, 0)
            program(act, tile, before, prepare)

        @block.vector
        def _(dve):
            for x in (w_low, V):
                x.open(dve)

            def split(h, c):
                n, s, uses = number(h, c)
                w_high.wait(dve, n, "all")
                w_low.done(dve.tensor_tensor(wl[s][:, :, :], raw[s][:, :, :], wh[s][:, :, :].bitcast(F32), ALU.subtract), "all")

            def tile(h, c, place):
                split(h, c + 1)
                for _ in range(3):
                    yield

            def before():
                yield 0
                dve.memset(rkv[:, :, 0:1 + PAD], 0.0).then_inc(init, 1)
                dve.memset(wlow[:, 0:2, :], 0.0).then_inc(init, 1)
                dve.memset(fade[:, :, 0:1], 1.0).then_inc(init, 1)
                dve.memset(tiny[:, :], 1e-12).then_inc(init, 1)
                dve.memset(keep[:, :, :], 1.0).then_inc(init, 1)
                dve.wait_ge(init, 5)
                dve.memset(keep[:, :, 0:1], 0.0).then_inc(init, 1)
                dve.wait_ge(init, 6)
                yield 12
                dve.wait_ge(low_loaded, 48)
                dve.tensor_scalar(omul[:, :], mul[:, :], -1.0, 1.0, ALU.mult, ALU.add).then_inc(lowp, 1)
                dve.wait_ge(lowp, 3)
                for j, t in enumerate((tl, sg)):
                    dve.scalar_tensor_tensor(t[:, :], low[:, j, 1:], omul[:, j:j + 1], prev[j][:, :],
                                             ALU.mult, ALU.add).then_inc(lowp, 1)

            def prepare(h, u):
                i = h * 2 + u
                yield 1
                dve.wait_ge(vec_loaded, i * 64 + 64)
                V.done(dve.tensor_scalar(omv[:, 0:3], vec[:, V_MU:V_MU + 3], -1.0, 1.0, ALU.mult, ALU.add), "om")
                V.done(dve.tensor_scalar(omv[:, 3:4], vec[:, V_KA:V_KA + 1], -1.0, 1.0, ALU.mult, ALU.add), "omka")
                V.wait(dve, i, "omka")
                A.wait(dve, i, "w2")
                V.done(dve.tensor_tensor_scan(cum[:, :], keep[:, :, :].rearrange("p c n -> p (c n)"), sw[:, :], 0.0,
                                              ALU.mult, ALU.add), "scan")
                yield 3
                dve.wait_ge(left, i * LEFT + LEFT)
                for j, (t, name) in ((1, (k[:, :], "k")), (0, (r[:, :], "r")), (2, (fields[:, :, F_V, :], "v"))):
                    G.wait(dve, i, f"p{j}")
                    cur, before = rkv[:, j, 1:], prev[j][:, :]
                    if name == "v":
                        cur, before = (a.rearrange("p (c n) -> p c n", n=CH) for a in (cur, before))
                    V.done(dve.scalar_tensor_tensor(t, cur, omv[:, j:j + 1], before, ALU.mult, ALU.add), name)
                yield 5
                V.wait(dve, i, "v")
                A.wait(dve, i, "a2")
                V.done(dve.tensor_scalar(scale_k[:, :], aa[:, :], vec[:, V_KA:V_KA + 1], omv[:, 3:4], ALU.mult, ALU.add), "t1")
                V.wait(dve, i, "t1")
                G.wait(dve, i, "kk")
                V.done(dve.tensor_tensor(k[:, :], k[:, :], scale_k[:, :], ALU.mult), "kmod")
                V.wait(dve, i, "kmod")
                V.done(dve.scalar_tensor_tensor(rk[:, :], r[:, :], vec[:, V_RK:V_RK + 1], k[:, :], ALU.mult, ALU.mult), "rk")
                yield 8
                for g, (c, n) in enumerate(XGROUPS):
                    M.wait(dve, i, f"b{g}")
                    vv = fields[:, c // CH:(c + n) // CH, F_V, :]
                    V.done(dve.tensor_tensor(bv[:, c - CH:c - CH + n].rearrange("p (c n) -> p c n", n=CH),
                                             bank[3 + g][:, 0:n].rearrange("p (c n) -> p c n", n=CH), vv, ALU.mult), f"bv{g}")
                yield 9
                G.wait(dve, i, "kkn")
                V.done(dve.scalar_tensor_tensor(fields[:, :, F_A, :], c3(kk), -1.0, fade[:, :, 0:CH], ALU.mult, ALU.mult), "A")
                G.wait(dve, i, "ka")
                V.done(dve.tensor_tensor(fields[:, :, F_B, :], c3(sq), grow[:, :, :], ALU.mult), "B")
            split(0, 0)
            program(dve, tile, before, prepare)

        @block.tensor
        def _(pe):
            for x in (group_done, M):
                x.open(pe)

            def tile(h, c, place):
                n, s, uses = number(h, c)
                w_high.wait(pe, n, "all")
                w_low.wait(pe, n, "all")
                for g, (col, size) in enumerate(TOK_GROUPS):
                    group_read.wait(pe, n, f"{g}", 1)
                    for kt in range(KD):
                        for j, (w, xx) in enumerate([(wh, xh), (wh, xl), (wl, xh)]):
                            last = pe.matmul(acc[g][:, 0:size], w[s][:, kt, :], xx[:, kt, col:col + size],
                                             start=(kt == 0 and j == 0), stop=(kt == KD - 1 and j == 2))
                    group_done.done(last, f"{g}")
                    yield

            def before():
                yield 17
                pe.wait_ge(lowa, 2)
                pe.wait_ge(lowp, 5)

            def prepare(h, u):
                i = h * 2 + u
                yield 1
                pe.wait_ge(vec_loaded, i * 64 + 64)
                V.wait_lap_before(pe, i)
                A.wait_lap_before(pe, i)
                for g, (c, n) in enumerate(PGROUPS):
                    M.done(pe.matmul(bank[g][:, 0:n], wlow[:, 0, :], tl[:, c:c + n], start=True, stop=True), f"w{g}")
                yield 2
                for g, (c, n) in enumerate(XGROUPS):
                    M.done(pe.matmul(bank[3 + g][:, 0:n], wlow[:, 2, :], sg[:, c:c + n], start=True, stop=True), f"g{g}")
                yield 3
                for g, (c, n) in enumerate(PGROUPS):
                    A.wait(pe, i, f"w{g}")
                    M.done(pe.matmul(bank[g][:, 0:n], wlow[:, 1, :], tl[:, c:c + n], start=True, stop=True), f"a{g}")
                yield 7
                A.wait(pe, i, "sq")
                for g, (c, n) in enumerate(PGROUPS):
                    M.done(pe.matmul(bank[g][:, 0:n], ones_bd[:, :], sq[:, c:c + n], start=True, stop=True), f"n{g}")
                yield 8
                V.wait(pe, i, "rk")
                for g, (c, n) in enumerate(XGROUPS):
                    M.done(pe.matmul(bank[3 + g][:, 0:n], ones_bd[:, :], rk[:, c:c + n], start=True, stop=True), f"b{g}")
            program(pe, tile, before, prepare)

SB_CLAMP = 40.0
SBW = 512
GROUPS = SEQ // SBW


class Tally:

    def __init__(self, sem, per, back=1):
        self.sem, self.per, self.back = sem, per, back

    def open(self, eng):
        eng.sem_inc(self.sem, self.back * self.per)

    def wait(self, eng, i, n):
        assert -self.back * self.per <= n < self.per
        eng.wait_ge(self.sem, i * self.per + (self.back * self.per + n + 1))


def sb_tasks():
    tasks = []
    for h in range(2):
        for g in reversed(range(GROUPS)):
            for b in range((g + 1) * SBW // P, -1, -1):
                tasks.append((h, g, b, max(0, (b - 1) * P - g * SBW), b > g * SBW // P))
    return tasks


def sb_keys(b):
    return (0, CH) if b == 0 else (CH + (b - 1) * P, P)


SCAN_STEPS = 6 + 3 * len(LEVELS)
LAPS = 4
SB_LAG = 7
SB_HEAD = 4


def interleave(scans, sticks):
    total = LAPS * SCAN_STEPS
    quarters = 4 * (len(sb_tasks()) + SB_LAG) + 3
    k = given = 0
    for scan in scans:
        for _ in scan:
            k += 1
            due = max(0, k - SB_HEAD) * quarters // (total - SB_HEAD)
            for _ in range(due - given):
                next(sticks)
            given = due
    assert k == total and given == quarters and next(sticks, "end") == "end"


def stage_mix(nc, chunk_dram, p_dram, masks, ident, pc, y_sb, o_sb, w_out, w_raw):
    tasks = sb_tasks()
    N = len(tasks)
    diag_at = [n for n in range(N) if tasks[n][4]]
    ends = [n for n in range(N) if tasks[n][2] == 0]
    with ExitStack() as ctx:
        m = Mem(nc, ctx, "mix")
        ar = [m.sb(f"ar{s}", [P, PAIRS, 3, 2, CH]) for s in range(2)]
        bkb = [m.sb(f"bkb{s}", [P, PAIRS, 3, CH]) for s in range(2)]
        v2 = [m.sb(f"v2{s}", [P, PAIRS, 2, CH]) for s in range(2)]
        nl = m.sb("nl", [P, PAIRS, 2, P])
        rb = m.sb("rb", [P, PAIRS, 2, 2, CH])
        x = m.sb("x", [P, PAIRS, P])
        xt = m.sb("xt", [P, PAIRS, P])
        lvl = m.sb("lvl", [P, PAIRS, P])
        ak = m.sb("ak", [P, PAIRS, 2, CH])
        wuv = m.sb("wuv", [P, PAIRS, 2, 2, CH])
        qm = m.sb("qm", [P, PAIRS, 2, 2, CH])
        state = m.sb("state", [P, PAIRS, CH])
        bank = [m.ps(f"bank{q}") for q in range(PAIRS)]
        q2 = m.sb("q2", [P, 2, SEQ])
        k2 = m.sb("k2", [P, 2, TPAD])
        qh, ql = m.sb("qh", [P, 2, SEQ], F32R), m.sb("ql", [P, 2, SEQ], F32R)
        ks = m.sb("ks", [P, 2, TPAD], F32R)
        vt = m.sb("vt", [P, TPAD])
        v = m.sb("v", [P, 9, P])
        tri = m.sb("tri", [P, P])
        rest = m.sb("rest", [P, P])
        tri_r, rest_r = m.sb("tri_r", [P, P], F32R), m.sb("rest_r", [P, P], F32R)
        z = [m.sb(f"z{i}", [P, SBW]) for i in range(4)]
        w = [m.sb(f"w{i}", [P, SBW]) for i in range(5)]
        wsh = [m.sb(f"wsh{i}", [P, SBW], F32R) for i in range(4)]
        wsl = [m.sb(f"wsl{i}", [P, SBW], F32R) for i in range(4)]
        a = [m.sb(f"a{i}", [P, SBW]) for i in range(3)]
        zb = [m.ps(f"zb{i}") for i in range(2)]
        cb = m.ps("cb")
        ob = m.ps("ob")

        loaded = [m.sem(f"loaded{s}") for s in range(2)]
        ar_zeroed, zeroed = m.sem("ar_zeroed"), m.sem("zeroed")
        qs = range(PAIRS)
        every = lambda names: " ".join(f"{n}{q}" for n in names.split() for q in qs)
        V = Steps(m.sem("vec_done"), every(f"nl rl x1a x1b {' '.join(f'z{l} x{l}' for l in LEVELS)} qm0 qm1 s"))
        A = Steps(m.sem("act_done"), every(f"ta0 ta1 tv0 tv1 tbk lv x0 {' '.join(f't{l}' for l in LEVELS)} w0 w1 y"))
        M = Steps(m.sem("mm_done"), every(f"tp g lv x0 {' '.join(f'n{l} x{l} t{l}' for l in LEVELS)} wu qm sy"))
        LOADS = 8 * 16
        ZEROED = 8
        sb_loaded, tri_set, w_loaded = m.sem("sb_loaded"), m.sem("tri_set"), m.sem("w_loaded")
        SB_LOADS = 9 * 16
        v_turned, v_copied = Tally(m.sem("v_turned"), 1), Tally(m.sem("v_copied"), 1)
        (z_done, z_copied, clamped, exp_done, ln_done, soft, tri_done, exponent, rest_done, weights, pv_done) = (
            Tally(m.sem(name), N) for name in ("z_done", "z_copied", "clamped", "exp_done", "ln_done", "soft", "tri_done",
                                               "exponent", "rest_done", "weights", "pv_done"))
        soft_masked, weights_masked = (Tally(m.sem(name), len(diag_at)) for name in ("soft_masked", "weights_masked"))
        soft_high, soft_low = Tally(m.sem("soft_high"), N), Tally(m.sem("soft_low"), N)
        qk_high, qk_low = Tally(m.sem("qk_high"), 4), Tally(m.sem("qk_low"), 4)
        o_copied = Tally(m.sem("o_copied"), len(ends))
        block = ctx.enter_context(nc.Block())

        def program(eng, lap, sticks):
            for _ in lap(0, 0, 0):
                pass
            with eng.Fori(0, PAIRS) as i:
                interleave([lap(i * LAPS + (1 + l), (1 + l) % 2, i * 2 + (1 + l) // 2) for l in range(LAPS)], sticks(i))

        def task(n):
            if not 0 <= n < N:
                return None
            h, g, b, off, diag = tasks[n]
            return h, g, b, off, sb_keys(b)[1], diag

        @block.sync
        def _(sp):
            def load(n, s):
                src = chunk_dram[:, ds(n, 1)].squeeze(1).rearrange("q p f -> p q f")
                for h in range(2):
                    rows = slice(h * HD, (h + 1) * HD)
                    for f in (F_A, F_R):
                        sp.dma_start(ar[s][rows, :, f, h, :], src[rows, :, f * CH:(f + 1) * CH]).then_inc(loaded[s], 16)
                sp.dma_start(bkb[s][:, :, 0:2, :].rearrange("p q f n -> p q (f n)"),
                             src[:, :, 2 * CH:4 * CH]).then_inc(loaded[s], 16)
                sp.dma_start(bkb[s][:, :, 2, :], src[:, :, 2 * CH:3 * CH]).then_inc(loaded[s], 16)
                for h in range(2):
                    sp.dma_start(v2[s][:, :, h, :], src[:, :, 4 * CH:]).then_inc(loaded[s], 16)

            def reload(n, s, last):
                for steps in (V, M):
                    steps.wait(sp, last, steps.names[-1])
                    stand_alone(sp)
                load(n, s)

            for s in range(2):
                sp.wait_ge(ar_zeroed, s + 1)
                load(s, s)
            M.wait(sp, 0, M.names[-1])
            for k in range(KD // 2):
                sp.dma_start(w_raw[:, k, :], w_out[k]).then_inc(w_loaded, 16)
            with sp.Fori(1, CHUNKS // 2) as i:
                for s in range(2):
                    reload(i * 2 + s, s, i * 2 + (s - 2))
            reload(CHUNKS - 1, 0, CHUNKS - 3)
            sp.wait_ge(w_loaded, 16 * (KD // 2))

        @block.gpsimd
        def _(pool):
            for tally in (soft_masked, weights_masked, soft_high, soft_low):
                tally.open(pool)
            for t in (k2[:, :, 0:PAD], vt[:, 0:PAD]):
                pool.memset(t, 0.0).then_inc(zeroed, 1)
            for t in (tri, rest):
                pool.memset(t[:, :], 1.0).then_inc(zeroed, 1)
            pool.wait_ge(zeroed, ZEROED)
            pool.affine_select(out=tri[:, :], in_=tri[:, :], compare_op=ALU.is_ge, fill=0.0, base=0,
                               pattern=[[-1, P]], channel_multiplier=1).then_inc(tri_set, 1)
            pool.affine_select(out=rest[:, :], in_=rest[:, :], compare_op=ALU.is_gt, fill=0.0, base=0,
                               pattern=[[1, P]], channel_multiplier=-1).then_inc(tri_set, 1)
            pool.wait_ge(tri_set, 2)
            pool.tensor_copy(tri_r[:, :], tri[:, :]).then_inc(tri_set, 1)
            pool.tensor_copy(rest_r[:, :], rest[:, :]).then_inc(tri_set, 1)

            def mask(tile, off, tally):
                stand_alone(pool)
                part = tile[:, off:off + P]
                pool.affine_select(out=part, in_=part, compare_op=ALU.is_gt, fill=0.0, base=0,
                                   pattern=[[1, P]], channel_multiplier=-1).then_inc(tally.sem, 1)

            with pool.Fori(0, PAIRS) as i:
                qk_low.wait(pool, i, -1)
                v_turned.wait(pool, i, -1)
                stand_alone(pool)
                for h in range(2):
                    head = slice(h * HD, (h + 1) * HD)
                    for rows in (slice(0, HD), slice(HD, P)):
                        pool.dma_start(q2[rows, h, :], p_dram[ds(i * LAP_PLACES + P_SQ, 1)].squeeze(0)[head, CH:TPAD]).then_inc(sb_loaded, 16)
                        pool.dma_start(k2[rows, h, PAD:], p_dram[ds(i * LAP_PLACES + P_SK, 1)].squeeze(0)[head, PAD:TPAD]).then_inc(sb_loaded, 16)
                pool.dma_start(vt[:, PAD:], p_dram[ds(i + P_SV, 1)].squeeze(0)[:, PAD:TPAD]).then_inc(sb_loaded, 16)
                for t in range(N + SB_LAG):
                    n = t - 5
                    if task(n) and task(n)[5]:
                        weights.wait(pool, i, n)
                        mask(a[n % 3], task(n)[3], weights_masked)
                    n = t - 2
                    if task(n):
                        h, g, b, off, r, diag = task(n)
                        soft.wait(pool, i, n)
                        if diag:
                            mask(w[n % 5], off, soft_masked)
                            soft_masked.wait(pool, i, diag_at.index(n))
                        rest_done.wait(pool, i, n - 4)
                        stand_alone(pool)
                        if SBW - off >= 2 * P:
                            part, high, low = (x[0:r, off:] for x in (w[n % 5], wsh[n % 4], wsl[n % 4]))
                            pool.tensor_copy(high, part).then_inc(soft_high.sem, 1)
                            soft_high.wait(pool, i, n)
                            stand_alone(pool)
                            pool.tensor_tensor(low, part, high.bitcast(F32), ALU.subtract).then_inc(soft_low.sem, 1)
                        else:
                            pool.sem_inc(soft_high.sem, 1)
                            pool.sem_inc(soft_low.sem, 1)

        @block.scalar
        def _(act):
            A.open(act)
            for tally in (qk_high, v_copied, z_copied, exp_done, ln_done, weights, o_copied):
                tally.open(act)
            act.preload_act_table_set("natural_log_exp_and_others")
            act.wait_ge(zeroed, ZEROED)

            def lap(n, s, use):
                def copy(out, in_, name):
                    A.done(act.activation(out, in_, ACT.Copy), name)
                lo, hi = slice(0, HD), slice(HD, P)
                for q in qs:
                    M.wait(act, n, f"tp{q}")
                    copy(ak[lo, q, 0, :], bank[q][lo, 0:CH], f"ta0{q}")
                for q in qs:
                    copy(ak[hi, q, 0, :], bank[q][hi, CH:2 * CH], f"ta1{q}")
                for q in qs:
                    copy(wuv[hi, q, 1, 0, :], bank[q][hi, P:P + CH], f"tv0{q}")
                for q in qs:
                    copy(wuv[lo, q, 1, 1, :], bank[q][lo, P + CH:2 * P], f"tv1{q}")
                for q in qs:
                    t = bank[q][:, 2 * P:4 * P].rearrange("p (t n) -> p t n", n=CH)[:, 0:4:3, :]
                    copy(rb[:, q, 1, :, :], t, f"tbk{q}")
                yield "tp"
                yield "g"
                for q in qs:
                    M.wait(act, n, f"lv{q}")
                    copy(ak[:, q, 1, :], bank[q][:, 0:CH], f"lv{q}")
                yield "lv"
                for q in qs:
                    M.wait(act, n, f"x0{q}")
                    copy(x[:, q, :], bank[q][:, 0:P], f"x0{q}")
                yield "x0"
                for l in LEVELS:
                    yield "n"
                    yield "x"
                    for q in qs:
                        M.wait(act, n, f"t{l}{q}")
                        copy(xt[:, q, :], bank[q][:, 0:P], f"t{l}{q}")
                    yield "t"
                for h in range(2):
                    rows = slice(h * HD, (h + 1) * HD)
                    for q in qs:
                        M.wait(act, n, f"wu{q}")
                        copy(wuv[rows, q, :, h, :], bank[q][rows, 0:P].rearrange("p (f n) -> p f n", f=2), f"w{h}{q}")
                yield "wu"
                for q in qs:
                    M.wait(act, n, f"sy{q}")
                    copy(y_sb[:, q, ds(n * CH, CH)], bank[q][:, CH:P], f"y{q}")
                yield "qm sy"

            def sticks(i):
                act.wait_ge(sb_loaded, i * SB_LOADS + SB_LOADS)
                z_done.wait(act, i, -1)
                act.activation(qh[:, 0, :], q2[:, 0, :], ACT.Copy).then_inc(qk_high.sem, 1)
                yield
                act.activation(ks[:, 0, :], k2[:, 0, :], ACT.Copy).then_inc(qk_high.sem, 1)
                yield
                v_turned.wait(act, i, 0)
                act.activation(v[:, 1:5, :], zb[0][:, :].rearrange("p (b n) -> p b n", n=P), ACT.Copy)
                act.activation(v[:, 5:9, :], zb[1][:, :].rearrange("p (b n) -> p b n", n=P), ACT.Copy)
                act.activation(v[0:CH, 0, :], cb[0:CH, 0:P], ACT.Copy).then_inc(v_copied.sem, 1)
                yield
                for t in range(N + SB_LAG):
                    n = t - 1
                    if task(n):
                        h, g, b, off, r, diag = task(n)
                        z_done.wait(act, i, n)
                        exponent.wait(act, i, n - 4)
                        act.activation(z[n % 4][0:r, off:], zb[n % 2][0:r, off:], ACT.Copy, scale=HD ** -0.5).then_inc(z_copied.sem, 1)
                    yield
                    n = t - 2
                    if task(n):
                        h, g, b, off, r, diag = task(n)
                        part = w[n % 5][0:r, off:]
                        clamped.wait(act, i, n)
                        act.activation(part, part, ACT.Exp).then_inc(exp_done.sem, 1)
                        exp_done.wait(act, i, n)
                        act.activation(part, part, ACT.Ln, bias=1.0).then_inc(ln_done.sem, 1)
                    yield
                    if t == 4:
                        act.activation(qh[:, 1, :], q2[:, 1, :], ACT.Copy).then_inc(qk_high.sem, 1)
                    if t == 5:
                        act.activation(ks[:, 1, :], k2[:, 1, :], ACT.Copy).then_inc(qk_high.sem, 1)
                    n = t - 7
                    if n in ends:
                        h, g = tasks[n][0:2]
                        half = slice(h * HD, (h + 1) * HD)
                        pv_done.wait(act, i, n)
                        act.activation(o_sb[half, ds(i, 1), g * SBW:(g + 1) * SBW].squeeze(1), ob[half, :],
                                       ACT.Copy).then_inc(o_copied.sem, 1)
                    yield
                    n = t - 5
                    if task(n):
                        h, g, b, off, r, diag = task(n)
                        part = a[n % 3][0:r, off:]
                        exponent.wait(act, i, n)
                        act.activation(part, part, ACT.Exp).then_inc(weights.sem, 1)
                    yield
            program(act, lap, sticks)

        @block.vector
        def _(dve):
            V.open(dve)
            for tally in (qk_low, clamped, soft, exponent):
                tally.open(dve)
            for s in range(2):
                dve.memset(ar[s][:, :, 0:2, :, :].rearrange("p q f h n -> p q (f h n)"), 0.0).then_inc(ar_zeroed, 1)
            for s in range(2):
                for h in range(2):
                    same = ident[:, :].rearrange("p (h n) -> p h n", h=2)
                    rows = slice(h * HD, (h + 1) * HD)
                    for q in qs:
                        last = dve.tensor_copy(ar[s][rows, q, 2, h, :], same[rows, h, :])
            last.then_inc(zeroed, 1)
            dve.memset(wuv[:, :, :, :, :], 0.0).then_inc(zeroed, 1)
            dve.memset(qm[:, :, :, :, :], 0.0).then_inc(zeroed, 1)
            dve.memset(state[:, :, :], 0.0).then_inc(zeroed, 1)
            dve.wait_ge(zeroed, ZEROED)

            def lap(n, s, use):
                yield "tp"
                for q in qs:
                    M.wait(dve, n, f"g{q}")
                    both = bank[q][:, 0:P].unsqueeze(1).broadcast_to((P, 2, P))
                    V.done(dve.tensor_tensor(nl[:, q, :, :], both, masks[:, M_N:M_N + 2, :], ALU.mult), f"nl{q}")
                for q in qs:
                    V.done(dve.tensor_tensor(rb[:, q, 0, :, :].rearrange("p h n -> p (h n)"), bank[q][:, P:2 * P],
                                             masks[:, M_R, :], ALU.mult), f"rl{q}")
                for q in qs:
                    V.wait(dve, n, f"nl{q}")
                    V.done(dve.tensor_tensor(xt[:, q, :], nl[:, q, 0, :], masks[:, M_L1T, :], ALU.mult), f"x1a{q}")
                for q in qs:
                    V.wait(dve, n, f"x1a{q}")
                    V.done(dve.tensor_tensor(xt[:, q, :], xt[:, q, :], ident[:, :], ALU.add), f"x1b{q}")
                yield "g"
                yield "lv"
                yield "x0"
                for j, l in enumerate(LEVELS):
                    for q in qs:
                        M.wait(dve, n, f"n{l}{q}")
                        V.done(dve.tensor_tensor(lvl[:, q, :], bank[q][:, 0:P], masks[:, M_LEVEL + j, :], ALU.mult), f"z{l}{q}")
                    yield "n"
                    for q in qs:
                        M.wait(dve, n, f"x{l}{q}")
                        V.done(dve.tensor_tensor(x[:, q, :], x[:, q, :], bank[q][:, 0:P], ALU.add), f"x{l}{q}")
                    yield "x"
                    yield "t"
                yield "wu"
                for h in range(2):
                    rows = slice(h * HD, (h + 1) * HD)
                    for q in qs:
                        M.wait(dve, n, f"qm{q}")
                        V.done(dve.tensor_tensor(
                            qm[rows, q, :, h, :], bank[q][rows, 0:2 * P].rearrange("p (f h n) -> p f h n", f=2, h=2)[:, :, h, :],
                            ar[s][rows, q, 1:3, h, :], ALU.add), f"qm{h}{q}")
                for q in qs:
                    A.wait(dve, n, f"y{q}")
                    V.done(dve.tensor_scalar(state[:, q, :], bank[q][:, 0:CH], pc[:, q, ds(n, 1)], None, ALU.mult), f"s{q}")
                yield "qm sy"

            def sticks(i):
                def low_q(h):
                    qk_high.wait(dve, i, 2 * h)
                    dve.tensor_tensor(ql[:, h, :], q2[:, h, :], qh[:, h, :].bitcast(F32), ALU.subtract).then_inc(qk_low.sem, 1)

                def low_k(h):
                    qk_high.wait(dve, i, 2 * h + 1)
                    low = ks[HD:P, h, :]
                    dve.tensor_tensor(low, k2[HD:P, h, :], low.bitcast(F32), ALU.subtract).then_inc(qk_low.sem, 1)
                yield
                low_q(0)
                yield
                low_k(0)
                yield
                for t in range(N + SB_LAG):
                    n = t - 1
                    if task(n):
                        h, g, b, off, r, diag = task(n)
                        z_copied.wait(dve, i, n)
                        rest_done.wait(dve, i, n - 5)
                        dve.tensor_scalar(w[n % 5][0:r, off:], z[n % 4][0:r, off:], SB_CLAMP, None, ALU.min).then_inc(clamped.sem, 1)
                    yield
                    if t == 5:
                        low_q(1)
                    if t == 6:
                        low_k(1)
                    yield
                    n = t - 2
                    if task(n):
                        h, g, b, off, r, diag = task(n)
                        part = w[n % 5][0:r, off:]
                        ln_done.wait(dve, i, n)
                        dve.tensor_tensor(part, z[n % 4][0:r, off:], part, ALU.max).then_inc(soft.sem, 1)
                    yield
                    n = t - 4
                    if task(n):
                        h, g, b, off, r, diag = task(n)
                        tri_done.wait(dve, i, n)
                        pv_done.wait(dve, i, n - 3)
                        dve.tensor_tensor(a[n % 3][0:r, off:], z[n % 4][0:r, off:], cb[0:r, off:], ALU.subtract).then_inc(exponent.sem, 1)
                    yield
            program(dve, lap, sticks)

        @block.tensor
        def _(pe):
            M.open(pe)
            for tally in (v_turned, z_done, tri_done, rest_done, pv_done):
                tally.open(pe)
            pe.wait_ge(zeroed, ZEROED)
            pe.wait_ge(tri_set, 4)

            def lap(n, s, use):
                pe.wait_ge(loaded[s], use * LOADS + LOADS)
                for q in qs:
                    V.wait(pe, n, f"s{q}", 1)
                    tp = bank[q]
                    pe.transpose(tp[:, 0:P], ar[s][:, q, 0, :, :].rearrange("p h n -> p (h n)"), ident[:, :])
                    pe.transpose(tp[:, P:2 * P], v2[s][:, q, :, :].rearrange("p f n -> p (f n)"), ident[:, :])
                    pe.transpose(tp[:, 2 * P:3 * P], bkb[s][:, q, 0:2, :].rearrange("p f n -> p (f n)"), ident[:, :])
                    M.done(pe.transpose(tp[:, 3 * P:4 * P], bkb[s][:, q, 1:3, :].rearrange("p f n -> p (f n)"), ident[:, :]), f"tp{q}")
                yield "tp"
                for q in qs:
                    A.wait(pe, n, f"tbk{q}")
                    for h in range(2):
                        out = bank[q][:, 0:2 * P].rearrange("p (f h n) -> p f h n", f=2, h=2)[:, :, h, :]
                        last = pe.matmul(out, bkb[s][:, q, h:h + 2, :].rearrange("p f n -> p (f n)"),
                                         ar[s][:, q, 0:2, h, :], start=True, stop=True)
                    M.done(last, f"g{q}")
                yield "g"
                for q in qs:
                    V.wait(pe, n, f"rl{q}")
                    for h in range(2):
                        last = pe.matmul(bank[q][h * HD:(h + 1) * HD, 0:CH], nl[:, q, 1, h * CH:(h + 1) * CH],
                                         wuv[:, q, 1, h, :], start=True, stop=True)
                    M.done(last, f"lv{q}")
                yield "lv"
                for q in qs:
                    V.wait(pe, n, f"x1b{q}")
                    A.wait(pe, n, f"lv{q}")
                    M.done(pe.transpose(bank[q][:, 0:P], xt[:, q, :], ident[:, :]), f"x0{q}")
                yield "x0"
                before = "x0"
                for l in LEVELS:
                    for q in qs:
                        A.wait(pe, n, f"{before}{q}")
                        M.done(pe.matmul(bank[q][:, 0:P], nl[:, q, 0, :], x[:, q, :], start=True, stop=True), f"n{l}{q}")
                    yield "n"
                    for q in qs:
                        V.wait(pe, n, f"z{l}{q}")
                        M.done(pe.matmul(bank[q][:, 0:P], xt[:, q, :], lvl[:, q, :], start=True, stop=True), f"x{l}{q}")
                    yield "x"
                    for q in qs:
                        V.wait(pe, n, f"x{l}{q}")
                        M.done(pe.transpose(bank[q][:, 0:P], x[:, q, :], ident[:, :]), f"t{l}{q}")
                    yield "t"
                    before = f"t{l}"
                for q in qs:
                    A.wait(pe, n, f"{before}{q}")
                    M.done(pe.matmul(bank[q][:, 0:P], xt[:, q, :], ak[:, q, :, :].rearrange("p f n -> p (f n)"),
                                     start=True, stop=True), f"wu{q}")
                yield "wu"
                for q in qs:
                    A.wait(pe, n, f"w1{q}")
                    M.done(pe.matmul(bank[q][:, 0:2 * P], wuv[:, q, 0, :, :].rearrange("p h n -> p (h n)"),
                                     rb[:, q, :, :, :].rearrange("p f h n -> p (f h n)"), start=True, stop=True), f"qm{q}")
                for q in qs:
                    V.wait(pe, n, f"qm1{q}")
                    for h in range(2):
                        s_out = bank[q][h * HD:(h + 1) * HD, 0:CH]
                        pe.matmul(s_out, rb[:, q, 1, h, :], wuv[:, q, 1, h, :], start=True, stop=False)
                        pe.matmul(s_out, qm[:, q, 1, h, :], state[:, q, :], start=False, stop=True)
                    for h in range(2):
                        y_out = bank[q][h * HD:(h + 1) * HD, CH:P]
                        pe.matmul(y_out, state[:, q, :], qm[:, q, 0, h, :], start=True, stop=False)
                        last = pe.matmul(y_out, wuv[:, q, 1, h, :], rb[:, q, 0, h, :], start=False, stop=True)
                    M.done(last, f"sy{q}")
                yield "qm sy"

            def sums(out, ones, ones_r, cols, n, r, off, first):
                if r == CH:
                    stand_alone(pe)
                if SBW - off >= 2 * P:
                    pe.matmul(out, ones_r[0:r, cols], wsh[n % 4][0:r, off:], start=first, stop=False, skip_group_check=True)
                    return pe.matmul(out, ones_r[0:r, cols], wsl[n % 4][0:r, off:], start=False, stop=True, skip_group_check=True)
                return pe.matmul(out, ones[0:r, cols], w[n % 5][0:r, off:], start=first, stop=True, skip_group_check=True)

            def sticks(i):
                yield
                pe.wait_ge(sb_loaded, i * SB_LOADS + SB_LOADS)
                z_copied.wait(pe, i, -1)
                exponent.wait(pe, i, -1)
                for j in range(9):
                    c, r = sb_keys((j + 1) % 9)
                    dst = (zb[0], zb[1], cb)[j // 4]
                    last = pe.transpose(dst[0:r, (j % 4) * P:(j % 4 + 1) * P], vt[:, c:c + r], ident[:, :])
                last.then_inc(v_turned.sem, 1)
                yield
                yield
                for t in range(N + SB_LAG):
                    n = t
                    if task(n):
                        h, g, b, off, r, diag = task(n)
                        c, _ = sb_keys(b)
                        if n in (0, N // 2):
                            qk_low.wait(pe, i, 2 * h + 1)
                        if n < 2:
                            v_copied.wait(pe, i, 0)
                        else:
                            z_copied.wait(pe, i, n - 2)
                        wide = min(off, SBW - 2 * P)
                        for x in (qh, ql):
                            last = pe.matmul(zb[n % 2][0:r, wide:], ks[:, h, c:c + r], x[:, h, g * SBW + wide:(g + 1) * SBW],
                                             start=(x is qh), stop=(x is ql))
                        last.then_inc(z_done.sem, 1)
                    yield
                    n = t - 5
                    if task(n):
                        h, g, b, off, r, diag = task(n)
                        exponent.wait(pe, i, n)
                        if b:
                            sums(cb[:, off:], rest, rest_r, slice(0, P), n, r, off, False).then_inc(rest_done.sem, 1)
                        else:
                            pe.sem_inc(rest_done.sem, 1)
                    yield
                    n = t - 4
                    if task(n):
                        h, g, b, off, r, diag = task(n)
                        soft_low.wait(pe, i, n)
                        sums(cb[0:r, off:], tri, tri_r, slice(0, r), n, r, off,
                             b == (g + 1) * SBW // P).then_inc(tri_done.sem, 1)
                    yield
                    n = t - 6
                    if task(n):
                        h, g, b, off, r, diag = task(n)
                        first = b == (g + 1) * SBW // P
                        if diag:
                            weights_masked.wait(pe, i, diag_at.index(n))
                        else:
                            weights.wait(pe, i, n)
                        if first:
                            o_copied.wait(pe, i, sum(e < n for e in ends) - 1)
                        if r == CH:
                            stand_alone(pe)
                        pe.matmul(ob[h * HD:(h + 1) * HD, off:], v[0:r, b, h * HD:(h + 1) * HD], a[n % 3][0:r, off:],
                                  start=first, stop=(b == 0), skip_group_check=True).then_inc(pv_done.sem, 1)
                    yield
            program(pe, lap, sticks)

V_LG, V_LB, V_SG = 0, 1, 2


def stage_post_heads(nc, y_sb, o_sb, vecs, gate_dram, bonus_dram, ones_bd, w_out, w_raw, wh, wl):
    with ExitStack() as ctx:
        m = Mem(nc, ctx, "post")
        qs = range(PAIRS)
        dev = [m.sb(f"dev{q}", [P, SEQ])[:, :] for q in qs]
        rs = [m.sb(f"rs{q}", [P, SEQ])[:, :] for q in qs]
        ors = [m.sb(f"ors{q}", [P, SEQ]) for q in qs]
        gate = [m.sb(f"gate{s}", [P, SEQ]) for s in range(2)]
        bonus = [m.sb(f"bonus{s}", [P, SEQ]) for s in range(2)]
        w_rest = m.sb("w_rest", [P, KD // 2, D])
        w_tile = lambda k: (w_raw if k < KD // 2 else w_rest)[:, k % (KD // 2), :]
        vec = m.sb("vec", [P, PAIRS, 3])
        eps = m.sb("eps", [P, 2])
        sums = [m.ps(f"sums{q}", (P, SEQ)) for q in qs]
        loaded = [m.sem(f"loaded{s}") for s in range(2)]
        vec_loaded, w_loaded, eps_set = m.sem("vec_loaded"), m.sem("w_loaded"), m.sem("eps_set")
        (mean_done, var_done, osum_done, dev_done, dev_squared, o_squared, rs_ln, rs_done, ors_ln, ors_done,
         scaled, with_bonus, gated, o_scaled, w_high, w_low) = (m.sem(name) for name in (
            "mean_done", "var_done", "osum_done", "dev_done", "dev_squared", "o_squared", "rs_ln", "rs_done", "ors_ln",
            "ors_done", "scaled", "with_bonus", "gated", "o_scaled", "w_high", "w_low"))
        block = ctx.enter_context(nc.Block())
        half = lambda g: slice(g * 512, g * 512 + 512)

        @block.sync
        def _(sp):
            sp.dma_start(vec[:, :, :], vecs).then_inc(vec_loaded, 16)
            for q in qs:
                if q >= 2:
                    sp.wait_ge(gated, q - 1)
                sp.dma_start(bonus[q % 2][:, :], bonus_dram[q]).then_inc(loaded[q % 2], 16)
                sp.dma_start(gate[q % 2][:, :], gate_dram[q]).then_inc(loaded[q % 2], 16)
                if q == 0:
                    for k in range(KD // 2, KD):
                        sp.dma_start(w_tile(k), w_out[k]).then_inc(w_loaded, 16)

        @block.tensor
        def _(pe):
            for q in qs:
                for g in range(2):
                    last = pe.matmul(sums[q][:, half(g)], ones_bd[:, :], y_sb[:, q, CH + g * 512:CH + g * 512 + 512],
                                     start=True, stop=True)
                last.then_inc(mean_done, 1)
            for q in qs:
                pe.wait_ge(dev_squared, q + 1)
                for g in range(2):
                    last = pe.matmul(sums[q][:, half(g)], ones_bd[:, :], rs[q][:, half(g)], start=True, stop=True)
                last.then_inc(var_done, 1)
            for q in qs:
                pe.wait_ge(o_squared, q + 1)
                pe.wait_ge(rs_ln, q + 1)
                for g in range(2):
                    last = pe.matmul(sums[q][:, half(g)], ones_bd[:, :], ors[q][:, half(g)], start=True, stop=True)
                last.then_inc(osum_done, 1)

        @block.scalar
        def _(act):
            act.preload_act_table_set("natural_log_exp_and_others")
            for q in qs:
                act.activation(ors[q][:, :], o_sb[:, q, :], ACT.Square).then_inc(o_squared, 1)
            for q in qs:
                act.wait_ge(dev_done, q + 1)
                act.activation(rs[q], dev[q], ACT.Square).then_inc(dev_squared, 1)
            act.wait_ge(eps_set, 2)
            for q in qs:
                act.wait_ge(var_done, q + 1)
                act.activation(rs[q], sums[q][:, :], ACT.Ln, scale=1.0 / HD, bias=eps[:, 0:1]).then_inc(rs_ln, 1)
                act.wait_ge(rs_ln, q + 1)
                act.activation(rs[q], rs[q], ACT.Exp, scale=-0.5).then_inc(rs_done, 1)
            for q in qs:
                act.wait_ge(osum_done, q + 1)
                act.activation(ors[q][:, :], sums[q][:, :], ACT.Ln, scale=1.0 / HD, bias=eps[:, 1:2]).then_inc(ors_ln, 1)
                act.wait_ge(ors_ln, q + 1)
                act.activation(ors[q][:, :], ors[q][:, :], ACT.Exp, scale=-0.5).then_inc(ors_done, 1)

        @block.vector
        def _(dve):
            dve.memset(eps[:, 0:1], GN_EPS).then_inc(eps_set, 1)
            dve.memset(eps[:, 1:2], RMS_EPS).then_inc(eps_set, 1)
            for q in qs:
                dve.wait_ge(mean_done, q + 1)
                dve.scalar_tensor_tensor(dev[q], sums[q][:, :], -1.0 / HD, y_sb[:, q, CH:TPAD],
                                         ALU.mult, ALU.add).then_inc(dev_done, 1)
            for k in range(KD):
                if k == KD // 2:
                    dve.wait_ge(w_loaded, 16 * (KD // 2))
                dve.tensor_copy(wh[:, k, :], w_tile(k)).then_inc(w_high, 1)
            dve.wait_ge(vec_loaded, 16)
            for q in qs:
                gain, bias = (vec[:, q, j:j + 1] for j in (V_LG, V_LB))
                dve.wait_ge(rs_done, q + 1)
                dve.scalar_tensor_tensor(dev[q], dev[q], gain, rs[q], ALU.mult, ALU.mult).then_inc(scaled, 1)
                dve.wait_ge(scaled, q + 1)
                dve.wait_ge(loaded[q % 2], 32 * (q // 2 + 1))
                dve.scalar_tensor_tensor(dev[q], dev[q], bias, bonus[q % 2][:, :], ALU.add, ALU.add).then_inc(with_bonus, 1)
                dve.wait_ge(with_bonus, q + 1)
                dve.tensor_tensor(y_sb[:, q, CH:TPAD], dev[q], gate[q % 2][:, :], ALU.mult).then_inc(gated, 1)
            for q in qs:
                dve.wait_ge(ors_done, q + 1)
                dve.scalar_tensor_tensor(o_sb[:, q, :], o_sb[:, q, :], vec[:, q, V_SG:V_SG + 1], ors[q][:, :],
                                         ALU.mult, ALU.mult).then_inc(o_scaled, 1)

        @block.gpsimd
        def _(pool):
            for k in range(KD):
                pool.wait_ge(w_high, k + 1)
                pool.tensor_tensor(wl[:, k, :], w_tile(k), wh[:, k, :].bitcast(F32),
                                   ALU.subtract).then_inc(w_low, 1)


def stage_out_proj(nc, y_sb, o_sb, wh, wl, x_dram, gain_row, gain_cols, ident, h_dram, mh, ml):
    with ExitStack() as ctx:
        m = Mem(nc, ctx, "oproj")
        yh = [m.sb(f"yh{s}", [P, KD, P], F32R) for s in range(2)]
        yl = [m.sb(f"yl{s}", [P, KD, P], F32R) for s in range(2)]
        h = [m.sb(f"h{s}", [P, D]) for s in range(2)]
        t = [m.sb(f"t{s}", [P, D]) for s in range(2)]
        xf = [m.sb(f"xf{s}", [P, KD, P]) for s in range(2)]
        gain_r = m.sb("gain_r", [P, D])
        gain_c = m.sb("gain_c", [P, KD])
        ss = [m.sb(f"ss{s}", [P, 2]) for s in range(2)]
        rs = [m.sb(f"rs{s}", [P, 2]) for s in range(2)]
        eps = m.sb("eps", [P, 1])
        acc = [m.ps(f"acc{s}", (P, D)) for s in range(2)]
        tp = [m.ps(f"tp{s}", (P, D)) for s in range(2)]
        x_loaded = [m.sem(f"x_loaded{s}") for s in range(2)]
        stored = [m.sem(f"stored{s}") for s in range(2)]
        gains_loaded, eps_set = m.sem("gains_loaded"), m.sem("eps_set")
        steps = lambda name, names: Steps(m.sem(name), names, back=2)
        y_high, y_low = steps("y_high", "y o"), steps("y_low", "y o")
        products, turned = steps("products", "all"), steps("turned", "all")
        A = steps("act_done", "sq ln rs hsq hln hrs")
        V = steps("vec_done", "norm h scaled")
        gained, high, low = steps("gained", "all"), steps("high", "all"), steps("low", "all")
        block = ctx.enter_context(nc.Block())

        def each(eng, split, project, turn):
            def call(step, i, j, *more):
                step(i * 2 + j, j % 2, i * 2 * P + j * P, *more)
            call(split, 0, 0)
            call(split, 0, 1)
            call(project, 0, 0, True)
            with eng.Fori(0, TOK_TILES // 2 - 2) as i:
                for j in range(2):
                    call(project, i, j + 1, True)
                    call(turn, i, j)
            i = TOK_TILES // 2 - 2
            for j in range(3):
                call(project, i, j + 1, j == 0)
                call(turn, i, j)
            call(turn, i, 3)

        nothing = lambda n, s, c0, more=False: None

        @block.sync
        def _(sp):
            sp.dma_start(gain_r[:, :], gain_row.broadcast_to((P, D))).then_inc(gains_loaded, 16)
            sp.dma_start(gain_c[:, :], gain_cols).then_inc(gains_loaded, 16)
            for s in range(2):
                sp.dma_start(h[s][:, :], x_dram[s * P:(s + 1) * P, :]).then_inc(x_loaded[s], 16)

            def store(n, s, row):
                V.wait(sp, n, "h")
                stand_alone(sp)
                sp.dma_start(h_dram[ds(row, P), :], h[s][:, :]).then_inc(stored[s], 16)

            with sp.Fori(0, TOK_TILES // 2 - 1) as i:
                for s in range(2):
                    store(i * 2 + s, s, i * 2 * P + s * P)
                    V.wait(sp, i * 2 + s, "scaled")
                    sp.wait_ge(stored[s], i * 16 + 16)
                    stand_alone(sp)
                    sp.dma_start(h[s][:, :], x_dram[ds(i * 2 * P + (s + 2) * P, P), :]).then_inc(x_loaded[s], 16)
            for s in range(2):
                store(TOK_TILES - 2 + s, s, (TOK_TILES - 2 + s) * P)
            for s in range(2):
                sp.wait_ge(stored[s], 16 * (TOK_TILES // 2))

        @block.scalar
        def _(act):
            for x in (y_high, A, high):
                x.open(act)
            act.preload_act_table_set("natural_log_exp_and_others")
            act.wait_ge(eps_set, 1)

            def split(n, s, c0):
                products.wait(act, n, "all", 2)
                y_high.done(act.activation(yh[s][:, 0:PAIRS, :], y_sb[:, :, ds(c0 + CH, P)], ACT.Copy), "y")
                y_high.done(act.activation(yh[s][:, PAIRS:, :], o_sb[:, :, ds(c0, P)], ACT.Copy), "o")

            def inverse_root(n, s, j, before, names):
                A.wait(act, n, before)
                A.done(act.activation(rs[s][:, j:j + 1], ss[s][:, j:j + 1], ACT.Ln, scale=1.0 / D, bias=eps[:, :]), names[0])
                A.wait(act, n, names[0])
                A.done(act.activation(rs[s][:, j:j + 1], rs[s][:, j:j + 1], ACT.Exp, scale=-0.5), names[1])

            def project(n, s, c0, more):
                products.wait(act, n, "all")
                turned.wait(act, n, "all", 2)
                A.done(act.activation(t[s][:, :], acc[s][:, :], ACT.Square, accum_out=ss[s][:, 0:1]), "sq")
                inverse_root(n, s, 0, "sq", ("ln", "rs"))
                if more:
                    split(n + 2, s, c0 + 2 * P)
                V.wait(act, n, "h")
                A.done(act.activation(t[s][:, :], h[s][:, :], ACT.Square, accum_out=ss[s][:, 1:2]), "hsq")
                inverse_root(n, s, 1, "hsq", ("hln", "hrs"))

            def turn(n, s, c0):
                gained.wait(act, n, "all")
                high.done(act.activation(mh[:, :, ds(c0, P)], xf[s][:, :, :], ACT.Copy), "all")
            each(act, split, project, turn)

        @block.gpsimd
        def _(pool):
            for x in (y_low, low):
                x.open(pool)

            def split(n, s, c0):
                y_high.wait(pool, n, "o")
                stand_alone(pool)
                y_low.done(pool.tensor_tensor(yl[s][:, 0:PAIRS, :], y_sb[:, :, ds(c0 + CH, P)],
                                              yh[s][:, 0:PAIRS, :].bitcast(F32), ALU.subtract), "y")
                y_low.done(pool.tensor_tensor(yl[s][:, PAIRS:, :], o_sb[:, :, ds(c0, P)],
                                              yh[s][:, PAIRS:, :].bitcast(F32), ALU.subtract), "o")

            def turn(n, s, c0):
                high.wait(pool, n, "all")
                stand_alone(pool)
                low.done(pool.tensor_tensor(ml[:, :, ds(c0, P)], xf[s][:, :, :], mh[:, :, ds(c0, P)].bitcast(F32),
                                            ALU.subtract), "all")
            def project(n, s, c0, more):
                if more:
                    split(n + 2, s, c0 + 2 * P)
            each(pool, split, project, turn)

        @block.vector
        def _(dve):
            for x in (V, gained):
                x.open(dve)
            dve.memset(eps[:, :], RMS_EPS).then_inc(eps_set, 1)
            dve.wait_ge(gains_loaded, 32)

            def project(n, s, c0, more):
                A.wait(dve, n, "rs")
                V.done(dve.scalar_tensor_tensor(t[s][:, :], acc[s][:, :], rs[s][:, 0:1], gain_r[:, :], ALU.mult, ALU.mult), "norm")
                V.wait(dve, n, "norm")
                dve.wait_ge(x_loaded[s], (n - s) * 8 + 16)
                V.done(dve.tensor_tensor(h[s][:, :], h[s][:, :], t[s][:, :], ALU.add), "h")
                A.wait(dve, n, "hrs")
                V.wait(dve, n, "h")
                V.done(dve.tensor_scalar(t[s][:, :], h[s][:, :], rs[s][:, 1:2], None, ALU.mult), "scaled")

            def turn(n, s, c0):
                turned.wait(dve, n, "all")
                low.wait(dve, n, "all", 2)
                gained.done(dve.tensor_tensor(xf[s][:, :, :], tp[s][:, :].rearrange("p (k c) -> p k c", k=KD),
                                              gain_c[:, :].unsqueeze(2).broadcast_to((P, KD, P)), ALU.mult), "all")
            each(dve, nothing, project, turn)

        @block.tensor
        def _(pe):
            for x in (products, turned):
                x.open(pe)

            def project(n, s, c0, more):
                y_low.wait(pe, n, "o")
                V.wait(pe, n, "norm", 2)
                for g in range(2):
                    c = slice(g * 512, g * 512 + 512)
                    for k in range(KD):
                        for j, (yy, w) in enumerate([(yh, wh), (yh, wl), (yl, wh)]):
                            last = pe.matmul(acc[s][:, c], yy[s][:, k, :], w[:, k, c],
                                             start=(k == 0 and j == 0), stop=(k == KD - 1 and j == 2))
                products.done(last, "all")

            def turn(n, s, c0):
                V.wait(pe, n, "scaled")
                gained.wait(pe, n, "all", 2)
                for k in range(KD):
                    last = pe.transpose(tp[s][:, k * P:(k + 1) * P], t[s][:, k * P:(k + 1) * P], ident[:, :])
                turned.done(last, "all")
            each(pe, nothing, project, turn)


FC = 2
FF_CHUNKS = FF_TILES // FC


def stage_ffn(nc, mh, ml, w_up, w_down, acc, h_dram, gain_row, out_dram):
    with ExitStack() as ctx:
        m = Mem(nc, ctx, "ffn")
        raw_u = [m.sb(f"raw_u{f}", [P, KD, P]) for f in range(FC)]
        raw_d = [m.sb(f"raw_d{f}", [P, D]) for f in range(FC)]
        wuh = [m.sb(f"wuh{f}", [P, KD, P], F32R) for f in range(FC)]
        wul = [m.sb(f"wul{f}", [P, KD, P], F32R) for f in range(FC)]
        wdh = [m.sb(f"wdh{s}", [P, FC, D], F32R) for s in range(2)]
        wdl = [m.sb(f"wdl{s}", [P, FC, D], F32R) for s in range(2)]
        uh = [m.sb(f"uh{s}", [P, FC, SEQ], F32R) for s in range(2)]
        ul = [m.sb(f"ul{s}", [P, FC, SEQ], F32R) for s in range(2)]
        relu = [m.sb(f"relu{s}", [P, 512]) for s in range(2)]
        ups = [m.ps(f"up{b}") for b in range(4)]
        downs = [m.ps(f"down{b}") for b in range(4)]
        gain = m.sb("gain", [P, D])
        square = raw_d[0]
        h = [raw_u[s][:, :, :].rearrange("p k c -> p (k c)") for s in range(2)]
        ss = m.sb("ss", [P, TOK_TILES])
        eps = m.sb("eps", [P, 1])
        HALVES = 2 * FC
        OUTS = TOK_TILES * 2
        LAST = FF_CHUNKS - 1
        u_loaded = [m.sem(f"u_loaded{f}") for f in range(FC)]
        d_loaded = [m.sem(f"d_loaded{f}") for f in range(FC)]
        h_loaded = [m.sem(f"h_loaded{s}") for s in range(2)]
        stored = [m.sem(f"stored{s}") for s in range(2)]
        zeroed, gain_loaded = m.sem("zeroed"), m.sem("gain_loaded")
        wu_high, wu_low, wd_high, wd_low = (Tally(m.sem(name), FC) for name in ("wu_high", "wu_low", "wd_high", "wd_low"))
        up_done, relu_done, squared, u_high, u_low = (Tally(m.sem(name), HALVES) for name in (
            "up_done", "relu_done", "squared", "u_high", "u_low"))
        down_done, added = Tally(m.sem("down_done"), OUTS, back=2), Tally(m.sem("added"), OUTS)
        sum_squared, logged, rooted, normed, finished = (m.sem(name) for name in (
            "sum_squared", "logged", "rooted", "normed", "finished"))
        block = ctx.enter_context(nc.Block())

        def chunks(eng, up, down):
            up(0, 0, True)
            with eng.Fori(0, FF_CHUNKS // 2 - 1) as i:
                up(i * 2 + 1, 1, True)
                down(i * 2, 0)
                up(i * 2 + 2, 0, True)
                down(i * 2 + 1, 1)
            up(LAST, 1, False)
            down(LAST - 1, 0)
            down(LAST, 1)

        def nothing(c, s):
            pass

        @block.sync
        def _(sp):
            def load_up(c, first=False):
                for f in range(FC):
                    if not first:
                        wu_low.wait(sp, c, f - FC)
                        stand_alone(sp)
                    src = w_up[c * FC + f] if first else w_up[ds(c * FC + f, 1)].squeeze(0)
                    sp.dma_start(raw_u[f][:, :, :], src).then_inc(u_loaded[f], 16)

            def load_down(c):
                for f in range(FC):
                    wd_low.wait(sp, c, f - FC)
                    stand_alone(sp)
                    sp.dma_start(raw_d[f][:, :], w_down[ds(c * FC + f, 1)].squeeze(0)).then_inc(d_loaded[f], 16)

            load_up(0, first=True)
            with sp.Fori(0, LAST) as i:
                load_down(i)
                load_up(i + 1)
            load_down(LAST)
            sp.dma_start(gain[:, :], gain_row.broadcast_to((P, D))).then_inc(gain_loaded, 16)
            wu_low.wait(sp, LAST, FC - 1)
            for t in range(2):
                sp.dma_start(h[t], h_dram[t * P:(t + 1) * P, :]).then_inc(h_loaded[t], 16)
            for t in range(TOK_TILES):
                sp.wait_ge(finished, t + 1)
                sp.dma_start(out_dram[t * P:(t + 1) * P, :], acc[:, t, :]).then_inc(stored[t % 2], 16)
                if t + 2 < TOK_TILES:
                    sp.dma_start(h[t % 2], h_dram[(t + 2) * P:(t + 3) * P, :]).then_inc(h_loaded[t % 2], 16)
            for s in range(2):
                sp.wait_ge(stored[s], 16 * (TOK_TILES // 2))

        @block.scalar
        def _(act):
            for x in (wu_high, wd_high, relu_done, u_high):
                x.open(act)

            def up_high(c, f):
                act.wait_ge(u_loaded[f], c * 16 + 16)
                up_done.wait(act, c, 2 * f + 1 - HALVES)
                act.activation(wuh[f][:, :, :], raw_u[f][:, :, :], ACT.Copy).then_inc(wu_high.sem, 1)

            def up(c, s, more):
                for f in range(FC):
                    act.wait_ge(d_loaded[f], c * 16 + 16)
                    down_done.wait(act, c, -OUTS - 1)
                    act.activation(wdh[s][:, f, :], raw_d[f][:, :], ACT.Copy).then_inc(wd_high.sem, 1)
                for j in range(HALVES):
                    f, half = divmod(j, 2)
                    cols = slice(half * 512, half * 512 + 512)
                    up_done.wait(act, c, j)
                    u_low.wait(act, c, j - 2)
                    act.activation(relu[j % 2][:, :], ups[j][:, :], ACT.Relu).then_inc(relu_done.sem, 1)
                    squared.wait(act, c, j)
                    act.activation(uh[s][:, f, cols], relu[j % 2][:, :], ACT.Copy).then_inc(u_high.sem, 1)
                    if more and half == 1:
                        up_high(c + 1, f)
            for f in range(FC):
                up_high(0, f)
            chunks(act, up, nothing)
            act.preload_act_table_set("natural_log_exp_and_others")
            for t in range(TOK_TILES):
                added.wait(act, LAST, 2 * t + 1)
                if t:
                    act.wait_ge(sum_squared, t)
                act.activation(square[:, :], acc[:, t, :], ACT.Square, accum_out=ss[:, t:t + 1]).then_inc(sum_squared, 1)
                act.wait_ge(sum_squared, t + 1)
                act.activation(ss[:, t:t + 1], ss[:, t:t + 1], ACT.Ln, scale=1.0 / D, bias=eps[:, :]).then_inc(logged, 1)
                act.wait_ge(logged, t + 1)
                act.activation(ss[:, t:t + 1], ss[:, t:t + 1], ACT.Exp, scale=-0.5).then_inc(rooted, 1)

        @block.gpsimd
        def _(pool):
            u_low.open(pool)
            pool.memset(acc[:, :, :], 0.0).then_inc(zeroed, 1)

            def up(c, s, more):
                for j in range(HALVES):
                    f, half = divmod(j, 2)
                    cols = slice(half * 512, half * 512 + 512)
                    u_high.wait(pool, c, j)
                    stand_alone(pool)
                    pool.tensor_tensor(ul[s][:, f, cols], relu[j % 2][:, :], uh[s][:, f, cols].bitcast(F32),
                                       ALU.subtract).then_inc(u_low.sem, 1)
            chunks(pool, up, nothing)

        @block.vector
        def _(dve):
            for x in (wu_low, wd_low, squared, added):
                x.open(dve)
            dve.memset(eps[:, :], RMS_EPS).then_inc(zeroed, 1)

            def up_low(c, f):
                wu_high.wait(dve, c, f)
                dve.tensor_tensor(wul[f][:, :, :], raw_u[f][:, :, :], wuh[f][:, :, :].bitcast(F32), ALU.subtract).then_inc(wu_low.sem, 1)

            def up(c, s, more):
                for f in range(FC):
                    wd_high.wait(dve, c, f)
                    dve.tensor_tensor(wdl[s][:, f, :], raw_d[f][:, :], wdh[s][:, f, :].bitcast(F32), ALU.subtract).then_inc(wd_low.sem, 1)
                for j in range(HALVES):
                    relu_done.wait(dve, c, j)
                    dve.tensor_tensor(relu[j % 2][:, :], relu[j % 2][:, :], relu[j % 2][:, :], ALU.mult).then_inc(squared.sem, 1)
                    if more and j % 2 == 1:
                        up_low(c + 1, j // 2)

            def add(c, o):
                t, g = divmod(o, 2)
                part = acc[:, t, g * 512:g * 512 + 512]
                down_done.wait(dve, c, o)
                added.wait(dve, c, o - OUTS)
                dve.tensor_tensor(part, part, downs[o % 4][:, :], ALU.add).then_inc(added.sem, 1)

            def finish(t):
                dve.wait_ge(rooted, t + 1)
                dve.scalar_tensor_tensor(acc[:, t, :], acc[:, t, :], ss[:, t:t + 1], gain[:, :], ALU.mult, ALU.mult).then_inc(normed, 1)
                dve.wait_ge(normed, t + 1)
                dve.wait_ge(h_loaded[t % 2], 16 * (t // 2 + 1))
                dve.tensor_tensor(acc[:, t, :], acc[:, t, :], h[t % 2], ALU.add).then_inc(finished, 1)

            def down(c, s):
                if isinstance(c, int) and c == LAST:
                    dve.wait_ge(gain_loaded, 16)
                for o in range(OUTS):
                    add(c, o)
                    if isinstance(c, int) and c == LAST and o % 2 == 1 and o > 1:
                        finish(o // 2 - 1)
            for f in range(FC):
                up_low(0, f)
            dve.wait_ge(zeroed, 2)
            chunks(dve, up, down)
            finish(TOK_TILES - 1)

        @block.tensor
        def _(pe):
            for x in (up_done, down_done):
                x.open(pe)

            def up(c, s, more):
                for j in range(HALVES):
                    f, half = divmod(j, 2)
                    wu_low.wait(pe, c, f)
                    relu_done.wait(pe, c, j - HALVES)
                    cols = slice(half * 512, half * 512 + 512)
                    for k in range(KD):
                        for jj, (w, xx) in enumerate([(wuh, mh), (wuh, ml), (wul, mh)]):
                            last = pe.matmul(ups[j][:, :], w[f][:, k, :], xx[:, k, cols],
                                             start=(k == 0 and jj == 0), stop=(k == KD - 1 and jj == 2))
                    last.then_inc(up_done.sem, 1)

            def down(c, s):
                wd_low.wait(pe, c, FC - 1)
                u_low.wait(pe, c, HALVES - 1)
                for o in range(OUTS):
                    t, g = divmod(o, 2)
                    added.wait(pe, c, o - 4)
                    for f in range(FC):
                        for jj, (u, w) in enumerate([(uh, wdh), (uh, wdl), (ul, wdh)]):
                            last = pe.matmul(downs[o % 4][:, :], u[s][:, f, t * P:(t + 1) * P],
                                             w[s][:, f, g * 512:g * 512 + 512],
                                             start=(f == 0 and jj == 0), stop=(f == FC - 1 and jj == 2))
                    last.then_inc(down_done.sem, 1)
            chunks(pe, up, down)


def build(nc, x, meta, w_in, w_out, w_up, w_down, g_pre_mix, g_pre_ffn, g_post_mix, g_post_ffn,
          rwkv_vecs, mu_low, head_vecs, w_decay_up, w_a_up, w_g_up, out):
    p_dram = nc.dram_tensor("p_scratch", [P_PLACES, P, TPAD], F32, kind="Internal").ap()
    chunk_dram = nc.dram_tensor("chunk_scratch", [PAIRS, CHUNKS, P, 5 * CH], F32, kind="Internal").ap()
    gate_dram = nc.dram_tensor("gate_scratch", [PAIRS, P, SEQ], F32, kind="Internal").ap()
    bonus_dram = nc.dram_tensor("bonus_scratch", [PAIRS, P, SEQ], F32, kind="Internal").ap()
    h_dram = nc.dram_tensor("h_scratch", [SEQ, D], F32, kind="Internal").ap()
    with ExitStack() as whole:
        g = Mem(nc, whole, "all")
        ident = g.sb("ident", [P, P])
        ones_bd = g.sb("ones_bd", [P, P])
        pc = g.sb("pc", [P, PAIRS, CHUNKS])
        stage_constants(nc, ident, ones_bd)
        with ExitStack() as mixing:
            right = Mem(nc, mixing, "mixed")
            with ExitStack() as early:
                left = Mem(nc, early, "early")
                masks = left.sb("masks", [P, N_MASKS, P])
                with ExitStack() as c:
                    m = Mem(nc, c, "xn")
                    raw = [m.sb(f"raw{s}", [P, KD, P]) for s in range(2)]
                    xh, xl = m.sb("xh", [P, KD, T], F32R), m.sb("xl", [P, KD, T], F32R)
                    stage_norm_transpose(nc, x, meta, g_pre_mix, ident, xh, xl, w_in, raw)
                    stage_in_proj(nc, w_in, raw, masks, p_dram, xh, xl, rwkv_vecs, mu_low, w_decay_up, w_a_up, w_g_up,
                                  chunk_dram, gate_dram, bonus_dram, pc, ones_bd)
                y_sb, o_sb = right.sb("y", [P, PAIRS, TPAD], side="right"), right.sb("o", [P, PAIRS, SEQ], side="right")
                w_raw = left.sb("w_raw", [P, KD // 2, D])
                stage_mix(nc, chunk_dram, p_dram, masks, ident, pc, y_sb, o_sb, w_out, w_raw)
                wh, wl = (right.sb(name, [P, KD, D], F32R, side="right") for name in ("wh", "wl"))
                stage_post_heads(nc, y_sb, o_sb, head_vecs, gate_dram, bonus_dram, ones_bd, w_out, w_raw, wh, wl)
            mh, ml = g.sb("mh", [P, KD, SEQ], F32R), g.sb("ml", [P, KD, SEQ], F32R)
            stage_out_proj(nc, y_sb, o_sb, wh, wl, x, g_post_mix, g_pre_ffn, ident, h_dram, mh, ml)
        acc = g.sb("acc", [P, TOK_TILES, D])
        stage_ffn(nc, mh, ml, w_up, w_down, acc, h_dram, g_post_ffn, out)


def kernel(**inputs):
    import numpy as np
    import concourse.bacc as bacc
    from concourse.bass_utils import run_bass_kernel_spmd

    get = lambda name: np.asarray(inputs[name])
    by_tile = lambda a: np.ascontiguousarray(a.reshape(-1, P).T)
    by_pair = lambda *vs: np.ascontiguousarray(np.stack([v.reshape(PAIRS, P) for v in vs], axis=-1))
    mu = get("tshift_mu")[0]
    arrays = {
        "x": get("x")[0], "meta": get("meta_tokens"),
        "w_in": get("w_in")[0].reshape(KD, P, IN_TILES, P).transpose(2, 1, 0, 3)[w_in_order()],
        "w_out": get("w_out")[0].reshape(KD, P, D),
        "w_up": get("w_ffn_up")[0].reshape(KD, P, FF_TILES, P).transpose(2, 1, 0, 3),
        "w_down": get("w_ffn_down")[0].reshape(FF_TILES, P, D),
        "g_pre_mix": by_tile(get("g_pre_mix")[0]), "g_pre_ffn": by_tile(get("g_pre_ffn")[0]),
        "g_post_mix": get("g_post_mix"), "g_post_ffn": get("g_post_ffn"),
        "rwkv_vecs": by_pair(mu[0:RW], mu[RW:2 * RW], mu[2 * RW:3 * RW], get("decay_bias")[0], get("a_bias")[0],
                             get("k_k")[0], get("k_a")[0], get("r_k")[0].reshape(-1)),
        "mu_low": by_tile(mu[3 * RW:]),
        "head_vecs": by_pair(get("lnx_gain")[0], get("lnx_bias")[0], get("sb_out_gain")[0]).transpose(1, 0, 2),
        "w_decay_up": get("w_decay_up")[0], "w_a_up": get("w_a_up")[0], "w_g_up": get("w_g_up")[0],
    }
    arrays = {name: np.ascontiguousarray(a) for name, a in arrays.items()}
    nc = bacc.Bacc("TRN2", target_bir_lowering=False, num_devices=1)
    args = {name: nc.dram_tensor(f"in_{name}", a.shape, mybir.dt.from_np(a.dtype), kind="ExternalInput").ap()
            for name, a in arrays.items()}
    args["out"] = nc.dram_tensor("out", (SEQ, D), F32, kind="ExternalOutput").ap()
    build(nc, **args)
    r = run_bass_kernel_spmd(nc, [{f"in_{name}": a for name, a in arrays.items()}], core_ids=[0])
    return r.results[0]["out"].reshape(1, SEQ, D)
```
